# Optimizing a Trainium2 kernel written in Bass

```python
import jax, jax.numpy as jnp
from jax import lax
import numpy as np

D_MODEL = 2048
BATCH = 1
SEQ = 512
DEPTH = 1

N_META = 16
CHUNK = 64
N_HEADS_A = 8
HEAD_DIM_K = 128
HEAD_DIM_V = 128
QK_DIM = N_HEADS_A * HEAD_DIM_K
V_DIM = N_HEADS_A * HEAD_DIM_V
CONV_K = 4
POOL_WINDOWS = (2, 4, 8, 16)
N_POOL_GROUPS = 4
POOL_GROUP_DIM = 256
POOL_DIM = N_POOL_GROUPS * POOL_GROUP_DIM
FFN_DIM = -(-(8 * D_MODEL) // (3 * 256)) * 256
RMS_EPS = 1e-6
L2_EPS = 1e-6
IN_SIZES = (QK_DIM, QK_DIM, V_DIM, V_DIM, N_HEADS_A, N_HEADS_A, POOL_DIM, D_MODEL, D_MODEL)
IN_DIM = QK_DIM * 2 + V_DIM * 2 + N_HEADS_A * 2 + POOL_DIM + D_MODEL * 2

kernel_name = 'hybrid_gated_deltanet_multiscale_pool_block'

def rms_norm(x, w):
    xf = x.astype(jnp.float32)
    y = xf * lax.rsqrt(jnp.mean(xf * xf, axis=-1, keepdims=True) + RMS_EPS)
    return (y * w.astype(jnp.float32)).astype(x.dtype)

def l2_norm(x):
    return x * lax.rsqrt(jnp.sum(x * x, axis=-1, keepdims=True) + L2_EPS)

def causal_dwconv(x, w):
    return lax.conv_general_dilated(
        x, w.astype(x.dtype)[:, None, :], window_strides=(1,), padding=[(CONV_K - 1, 0)],
        dimension_numbers=('NWC', 'WIO', 'NWC'), feature_group_count=x.shape[-1])

def gated_delta_rule_chunked(q, k, v, beta, g):
    B, T, H, DK = q.shape
    DV = v.shape[-1]
    N = T // CHUNK

    def to_chunks(a):
        return a.reshape(B, N, CHUNK, H, a.shape[-1]).transpose(0, 1, 3, 2, 4)

    qc = to_chunks(q * (DK ** -0.5))
    kc = to_chunks(k)
    vc = to_chunks(v)
    bc = beta.reshape(B, N, CHUNK, H).transpose(0, 1, 3, 2)
    gc = jnp.cumsum(g.reshape(B, N, CHUNK, H).transpose(0, 1, 3, 2), axis=-1)

    incl = jnp.tril(jnp.ones((CHUNK, CHUNK), dtype=bool))
    strict = jnp.tril(jnp.ones((CHUNK, CHUNK), dtype=bool), k=-1)
    diff = gc[..., :, None] - gc[..., None, :]
    decay = jnp.exp(jnp.where(incl, diff, -jnp.inf))

    kb = kc * bc[..., None]
    a_mat = jnp.where(strict, jnp.einsum('bnhid,bnhjd->bnhij', kb, kc) * decay, 0.0)
    eye = jnp.broadcast_to(jnp.eye(CHUNK, dtype=jnp.float32), a_mat.shape)
    t_mat = lax.linalg.triangular_solve(a_mat, eye, left_side=True, lower=True, unit_diagonal=True)
    u = jnp.einsum('bnhij,bnhjd->bnhid', t_mat, vc * bc[..., None])
    w = jnp.einsum('bnhij,bnhjd->bnhid', t_mat, kb * jnp.exp(gc)[..., None])
    qk = jnp.einsum('bnhid,bnhjd->bnhij', qc, kc) * decay
    q_dec = qc * jnp.exp(gc)[..., None]
    k_dec = kc * jnp.exp(gc[..., -1:] - gc)[..., None]
    g_last = jnp.exp(gc[..., -1])

    def step(state, inp):
        u_n, w_n, qk_n, qd_n, kd_n, gl_n = inp
        v_new = u_n - jnp.einsum('bhcd,bhde->bhce', w_n, state)
        o_n = jnp.einsum('bhcd,bhde->bhce', qd_n, state) + jnp.einsum('bhij,bhje->bhie', qk_n, v_new)
        state = state * gl_n[..., None, None] + jnp.einsum('bhcd,bhce->bhde', kd_n, v_new)
        return state, o_n

    xs = tuple(jnp.moveaxis(a, 1, 0) for a in (u, w, qk, q_dec, k_dec, g_last))
    s0 = jnp.zeros((B, H, DK, DV), jnp.float32)
    _, o = lax.scan(step, s0, xs)
    return o.transpose(1, 0, 3, 2, 4).reshape(B, T, H, DV)

def causal_multiscale_pool(p):
    B, L, _ = p.shape
    pg = p.reshape(B, L, N_POOL_GROUPS, POOL_GROUP_DIM)
    csum = jnp.cumsum(pg, axis=1)
    t = jnp.arange(L)
    outs = []
    for gi, win in enumerate(POOL_WINDOWS):
        cg = csum[:, :, gi]
        shifted = jnp.pad(cg[:, :L - win], ((0, 0), (win, 0), (0, 0)))
        count = jnp.minimum(t + 1, win).astype(jnp.float32)[None, :, None]
        outs.append((cg - shifted) / count - pg[:, :, gi])
    return jnp.stack(outs, axis=2)

def hybrid_mixer(hn, w_in, conv_w, a_log, dt_bias, o_norm_w, w_proj_a, pool_w, pool_scale, w_proj_b, w_out):
    B, L, _ = hn.shape
    dt = hn.dtype
    split_idx = np.cumsum(IN_SIZES)[:-1].tolist()
    proj = hn @ w_in
    q, k, v, z, b_logit, a_logit, p, gate_a, gate_b = jnp.split(proj, split_idx, axis=-1)

    qkv = jax.nn.silu(causal_dwconv(jnp.concatenate([q, k, v], axis=-1), conv_w)).astype(jnp.float32)
    q, k, v = jnp.split(qkv, [QK_DIM, 2 * QK_DIM], axis=-1)
    q = l2_norm(q.reshape(B, L, N_HEADS_A, HEAD_DIM_K))
    k = l2_norm(k.reshape(B, L, N_HEADS_A, HEAD_DIM_K))
    v = v.reshape(B, L, N_HEADS_A, HEAD_DIM_V)
    beta = jax.nn.sigmoid(b_logit.astype(jnp.float32))
    g = -jnp.exp(a_log.astype(jnp.float32)) * jax.nn.softplus(
        a_logit.astype(jnp.float32) + dt_bias.astype(jnp.float32))
    pad = (-N_META) % CHUNK
    padt = lambda a: jnp.pad(a, ((0, 0), (pad, 0)) + ((0, 0),) * (a.ndim - 2))
    o = gated_delta_rule_chunked(padt(q), padt(k), padt(v), padt(beta), padt(g))[:, pad:]
    zf = z.astype(jnp.float32).reshape(B, L, N_HEADS_A, HEAD_DIM_V)
    o = o * lax.rsqrt(jnp.mean(o * o, axis=-1, keepdims=True) + RMS_EPS) * o_norm_w.astype(jnp.float32) * jax.nn.silu(zf)
    y_a = o.reshape(B, L, V_DIM).astype(dt) @ w_proj_a

    pooled = causal_multiscale_pool(p.astype(jnp.float32))
    zb = jnp.einsum('blgc,gcd->blgd', pooled, pool_w.astype(jnp.float32)).reshape(B, L, POOL_DIM)
    zb = zb * pool_scale.astype(jnp.float32)
    y_b = zb.astype(dt) @ w_proj_b

    merged = jax.nn.sigmoid(gate_a) * y_a + jax.nn.sigmoid(gate_b) * y_b
    return merged @ w_out

def swiglu_ffn(hn, w_gate, w_up, w_down):
    return (jax.nn.silu(hn @ w_gate) * (hn @ w_up)) @ w_down

def setup_inputs(seed: int = 0) -> dict:
    key = jax.random.key(seed)
    ks = jax.random.split(key, 20)
    f32 = jnp.float32
    nrm = lambda k, shape, scale: jax.random.normal(k, shape, f32) * scale
    gain = lambda k, shape: 1.0 + 0.02 * jax.random.normal(k, shape, f32)
    dt_init = jnp.exp(jax.random.uniform(ks[5], (DEPTH, N_HEADS_A), f32, np.log(1e-3), np.log(1e-1)))
    return {
        'x': nrm(ks[0], (BATCH, SEQ, D_MODEL), 1.0),
        'meta_tokens': nrm(ks[1], (N_META, D_MODEL), 1.0),
        'norm_mix_w': gain(ks[2], (DEPTH, D_MODEL)),
        'w_in': nrm(ks[3], (DEPTH, D_MODEL, IN_DIM), D_MODEL ** -0.5),
        'conv_w': nrm(ks[4], (DEPTH, CONV_K, 2 * QK_DIM + V_DIM), CONV_K ** -0.5),
        'a_log': jnp.log(jax.random.uniform(ks[6], (DEPTH, N_HEADS_A), f32, 1.0, 16.0)),
        'dt_bias': dt_init + jnp.log(-jnp.expm1(-dt_init)),
        'o_norm_w': gain(ks[7], (DEPTH, HEAD_DIM_V)),
        'w_proj_a': nrm(ks[8], (DEPTH, V_DIM, D_MODEL), V_DIM ** -0.5),
        'pool_w': nrm(ks[9], (DEPTH, N_POOL_GROUPS, POOL_GROUP_DIM, POOL_GROUP_DIM), POOL_GROUP_DIM ** -0.5),
        'pool_scale': gain(ks[10], (DEPTH, POOL_DIM)),
        'w_proj_b': nrm(ks[11], (DEPTH, POOL_DIM, D_MODEL), POOL_DIM ** -0.5),
        'w_out': nrm(ks[12], (DEPTH, D_MODEL, D_MODEL), D_MODEL ** -0.5),
        'norm_ffn_w': gain(ks[13], (DEPTH, D_MODEL)),
        'w_ffn_gate': nrm(ks[14], (DEPTH, D_MODEL, FFN_DIM), D_MODEL ** -0.5),
        'w_ffn_up': nrm(ks[15], (DEPTH, D_MODEL, FFN_DIM), D_MODEL ** -0.5),
        'w_ffn_down': nrm(ks[16], (DEPTH, FFN_DIM, D_MODEL), FFN_DIM ** -0.5),
        'norm_final_w': gain(ks[17], (D_MODEL,)),
    }

def reference(x, meta_tokens, norm_mix_w, w_in, conv_w, a_log, dt_bias, o_norm_w, w_proj_a, pool_w,
              pool_scale, w_proj_b, w_out, norm_ffn_w, w_ffn_gate, w_ffn_up, w_ffn_down, norm_final_w):
    B = x.shape[0]
    meta = jnp.broadcast_to(meta_tokens.astype(x.dtype)[None], (B, N_META, D_MODEL))
    h = jnp.concatenate([meta, x], axis=1)
    for l in range(DEPTH):
        h = h + hybrid_mixer(rms_norm(h, norm_mix_w[l]), w_in[l], conv_w[l], a_log[l], dt_bias[l], o_norm_w[l],
                             w_proj_a[l], pool_w[l], pool_scale[l], w_proj_b[l], w_out[l])
        h = h + swiglu_ffn(rms_norm(h, norm_ffn_w[l]), w_ffn_gate[l], w_ffn_up[l], w_ffn_down[l])
    h = rms_norm(h, norm_final_w)
    return h[:, N_META:]


_drawn_inputs = setup_inputs


def setup_inputs(seed=0):
    import zlib

    import numpy as np

    out = dict(_drawn_inputs(seed))
    spreads = {}
    factors = {'norm_mix_w': 3.821,
     'o_norm_w': 27.66,
     'pool_scale': 22.708,
     'norm_ffn_w': 14.935,
     'norm_final_w': 7.997}
    for name, (base, spread) in spreads.items():
        noise = np.random.default_rng([zlib.crc32(name.encode()), seed]).standard_normal(out[name].shape)
        drawn = base * np.exp(spread * noise) if base else spread * noise
        out[name] = __import__('jax').numpy.asarray(drawn.astype(out[name].dtype))
    for name, factor in factors.items():
        out[name] = (out[name] * factor).astype(out[name].dtype)
    return out
```

```python
from contextlib import ExitStack

import numpy as np

import concourse.bass as bass
from concourse import mybir
from concourse.alu_op_type import AluOpType as ALU

F32 = mybir.dt.float32
F32R = mybir.dt.float32r
ACT = mybir.ActivationFunctionType
AX = mybir.AxisListType

P = 128
META = 16
SEQ = 512
TOK = META + SEQ
HALF = TOK // 2
D = 2048
KT = D // P
HEADS = 8
QT, K_T, VT = 0, HEADS, 2 * HEADS
CONV = 4
POOL_GROUPS = 4
FFN = 5632
RMS_EPS = 1e-6
L2_EPS = 1e-6
NEG = -1e30

COL_Z = 3 * HEADS * P
COL_AB = COL_Z + HEADS * P
COL_P = COL_AB + 2 * HEADS
COL_GATES = COL_P + POOL_GROUPS * 2 * P

SLOTS = 4
CHUNK = 1024
UNIT = 256
BLOCK = 512

N_A = 3 * HEADS * P // UNIT
N_POOL = HEADS * P // UNIT
N_Z = HEADS * P // UNIT
N_GATES = 2 * D // UNIT
N_MERGE = D // UNIT
N_OUT = D // BLOCK
N_FFN = FFN // BLOCK
TT = SEQ // P

CH = SEQ // P
GH = 4
LEVELS = 7
META_LEVELS = 4
N_CONSTS = 17 + 3 * LEVELS
STEPS = 24
BODY_CHUNKS = N_GATES * 4 // CH
PIECE = 24 * BODY_CHUNKS // (2 * STEPS)

FREE = dict(a_copied=2, conv_done=2, qkv_ready=2, gate_freed=2, gates_stored=16, o_stored=1, p_copied=2,
            z_silu=2, z_y=2, z_lo=2, ya_gated=2, yb_gated=2, merged_sum=2, h1_ready=TT, h2_ready=TT,
            silu_ready=2, act_y=2, act_lo=2)

G_A = 0
G_GATES = G_A + N_A * 4
G_P = G_GATES + N_GATES * 4
G_Z = G_P + N_POOL * 4
G_MERGE = G_Z + N_Z * 4
G_OUT = G_MERGE + N_MERGE * 4
G_FFN = G_OUT + N_OUT * 8
G_END = G_FFN + N_FFN * 24

SEMAPHORES = """
rows_landed ab_landed small_landed poolw_landed scalew_landed
consts_built rows_turned vectors_ready vectors_more
x_squared x_rms_a x_rms x_scaled x_turned x_weighted x_hi x_lo
hi_ready lo_ready chunk_used
a_done a_copied conv_step conv_done qkv_ready
ab_hi ab_lo ab_meta ab_meta_copied ab_done logits_copied ab_vec ab_act
meta_staged meta_pe meta_vec meta_act meta_pool
staged qkv_turned gates_summed q_squared k_squared norms_a norms_summed norms_ready
sums_copied g_differenced g_masked decay_ready last_differenced decays_small nbeg_ready
q_scaled k_scaled vb_ready kd_ready qk_turned qn_ready kn_ready
kk_done kq_done nt_ready pt_ready level_masked s_products rhs_ready qs_ready
level_product level_x x_cleared t_product t_ready tt_product tt_ready
vn_product vn_ready o_product ds_product o_ready state_ready o_squared o_sum o_mean o_rms o_scaled
o_turned o_stored
gate_done gate_freed gates_stored
p_done p_copied window_step pooled_ready
z_done z_silu z_freed z_y z_hi z_lo
zb_done zb_y zb_hi zb_lo
ya_done yb_done ya_gated yb_gated merged_sum merged_hi merged_lo gate_a_landed gate_b_landed
out_done h1_ready xr_landed
fg_done fu_done silu_ready act_y act_hi act_lo down_done h2_ready
f_squared f_rms_a f_rms f_scaled out_stored0 out_stored1
""".split()


def hybrid_block(nc, x, meta_tokens, norm_mix_w, w_in, conv_w, a_log, dt_bias, o_norm_w, w_proj_a, pool_w,
                 pool_scale, w_proj_b, w_out, norm_ffn_w, w_ffn_gate, w_ffn_up, w_ffn_down, norm_final_w, out):
    ctx = ExitStack()
    with ctx:
        S = {n: ctx.enter_context(nc.semaphore(n)) for n in SEMAPHORES}
        landed = [ctx.enter_context(nc.semaphore(f"weights_landed{i}")) for i in range(SLOTS)]
        x_landed = [ctx.enter_context(nc.semaphore(f"x_landed{i}")) for i in range(2)]
        gates_dram = nc.dram_tensor("gates_dram", [2 * D, SEQ], F32).ap()

        top = [(nc.sbuf_base + 63) // 64 * 64]

        def place(name, shape, dtype=F32, at=None):
            size = int(np.prod(shape[1:])) * 4
            offset = top[0] if at is None else at
            if at is None:
                top[0] += (size + 63) // 64 * 64
            return nc.alloc_sbuf_tensor_at(name, shape, dtype, offset=offset)

        raw = [place(f"w_raw{i}", [P, CHUNK]) for i in range(SLOTS)]
        whi = [place(f"w_hi{i}", [P, CHUNK], F32R) for i in range(SLOTS)]
        wlo = [place(f"w_lo{i}", [P, CHUNK], F32R) for i in range(SLOTS)]
        ident = place("ident", [P, P])
        upper = place("upper", [P, P])
        ones = place("ones", [P, P])
        cap = place("cap", [P, P])
        levels_at = top[0]
        levels = place("levels", [P, LEVELS, P])
        minus_half = place("minus_half", [P, 16])
        zero = minus_half[:, 12:16]
        vec_a = place("vec_a", [P, CONV * 3 * HEADS])
        vec_b = place("vec_b", [P, 2 * KT + HEADS + 1])
        nmix, nffn = vec_b[:, 0:KT], vec_b[:, KT:2 * KT]
        pscale, onorm = vec_b[:, 2 * KT:2 * KT + HEADS], vec_b[:, 2 * KT + HEADS:2 * KT + HEADS + 1]
        g_all = place("g_all", [P, CH + 1, HEADS])
        b_all = place("b_all", [P, CH + 1, HEADS])
        ssq = place("ssq", [P, 16])
        rms_a = place("rms_a", [P, 16])
        rms = place("rms", [P, 16])
        small = place("small", [P, 160])
        state_at = top[0]
        state = place("state", [P, HEADS, P])
        hn_at = top[0]
        hn_hi = place("hn_hi", [P, KT, TOK], F32R)
        hn_lo = place("hn_lo", [P, KT, TOK], F32R)
        qkv_at = top[0]
        qkv = place("qkv", [P, 3 * HEADS, TOK])
        kv_at = qkv_at + HEADS * TOK * 4
        v_at = kv_at + HEADS * TOK * 4
        tmp_at = top[0]
        B = [place(f"gdn{i}", [P, GH, P]) for i in range(14)]
        top[0] = tmp_at + 16 * SEQ * 4
        ext_at = top[0]
        gate_out = place("gate_out", [P, 2, SEQ])
        spare = place("spare", [P, 2, SEQ])

        XB = (B[3], B[13])
        xt = [place(f"xt{i}", [P, D], at=qkv_at + i * D * 4) for i in range(2)]
        xs = [place(f"xs{i}", [P, D], at=qkv_at + (2 + i) * D * 4) for i in range(2)]
        rows_a = place("rows_a", [CONV * 3 * HEADS, P], at=qkv_at + 4 * D * 4)
        rows_b = place("rows_b", [2 * KT + HEADS + 1, P], at=qkv_at + 4 * D * 4 + 512)
        xy = [place(f"xy{i}", [P, 4, P], at=tmp_at + i * 2048) for i in range(4)]
        conv_in = [place(f"conv_in{i}", [P, TOK + CONV - 1], at=tmp_at + 8192 + i * 2176) for i in range(2)]
        conv_acc = [place(f"conv_acc{i}", [P, TOK], at=tmp_at + 8192 + (2 + i) * 2176) for i in range(2)]
        ab_raw = place("ab_raw", [P, KT, 2 * HEADS], at=tmp_at + 17408)
        ab_h = place("ab_h", [P, KT, 2 * HEADS], F32R, at=tmp_at + 18432)
        ab_l = place("ab_l", [P, KT, 2 * HEADS], F32R, at=tmp_at + 19456)
        lg = place("lg", [P, CH + 1, 2 * HEADS], at=tmp_at + 20480)
        ab_t = [place(f"ab_t{i}", [P, CH + 1, HEADS], at=tmp_at + 20864 + 192 * i) for i in range(4)]
        alog_b = place("alog_b", [P, HEADS], at=tmp_at + 21760)
        dtb_b = place("dtb_b", [P, HEADS], at=tmp_at + 21824)
        meta_upper = place("meta_upper", [P, P], at=ext_at)
        meta_block = place("meta_block", [P, P], at=ext_at + 512)
        meta_neg = place("meta_neg", [P, P], at=ext_at + 1024)
        meta_sel = place("meta_sel", [P, HEADS], at=ext_at + 1536)
        meta_rep = place("meta_rep", [META, P], at=ext_at + 2048)
        meta_lg = place("meta_lg", [META, 2 * HEADS], at=ext_at + 2560)
        meta_u = place("meta_u", [P, HEADS, P], at=ext_at + 4096)
        o_hi = place("o_hi", [P, HEADS, SEQ], F32R, at=tmp_at)
        o_lo = place("o_lo", [P, HEADS, SEQ], F32R, at=tmp_at + HEADS * SEQ * 4)
        p_in = place("p_in", [P, HEADS, TOK], at=kv_at)
        pooled = place("pooled", [P, HEADS, SEQ], at=v_at)
        zt = place("zt", [P, 2, SEQ], at=ext_at)
        zy = place("zy", [P, 2, SEQ], at=ext_at + 4096)
        zb_hi = place("zb_hi", [P, HEADS, SEQ], F32R, at=kv_at)
        zb_lo = place("zb_lo", [P, HEADS, SEQ], F32R, at=v_at)
        poolw = place("poolw", [P, POOL_GROUPS, 2, UNIT])
        win = [place(f"win{i}", [P, TOK], at=at_) for i, at_ in enumerate((levels_at, state_at))]
        zb_y = [win[i][:, 0:SEQ] for i in range(2)]
        gate_a = place("gate_a", [P, 2, SEQ], at=qkv_at)
        gate_b = place("gate_b", [P, 2, SEQ], at=qkv_at + 4096)
        mg = place("mg", [P, 2, SEQ], at=qkv_at + 8192)
        mg_hi = place("mg_hi", [P, KT, SEQ], F32R, at=hn_at)
        mg_lo = place("mg_lo", [P, KT, SEQ], F32R, at=hn_at + KT * SEQ * 4)
        h = place("h", [P, TT, D], at=tmp_at)
        xr = place("xr", [P, TT, BLOCK], at=v_at)
        hs = [place(f"hs{i}", [P, D], at=qkv_at + 8192 * i) for i in range(2)]
        hy = [place(f"hy{i}", [P, 4, P], at=kv_at + i * 2048) for i in range(4)]
        a_hi = place("a_hi", [P, 2, 4, SEQ], F32R, at=qkv_at)
        a_lo = place("a_lo", [P, 2, 4, SEQ], F32R, at=qkv_at + 16384)
        sg = place("sg", [P, 2, SEQ], at=qkv_at + 32768)
        ay = place("ay", [P, 2, SEQ], at=qkv_at + 32768 + 4096)
        scalew = place("scalew", [P, D], at=qkv_at + 32768 + 8192)
        ot = [place(f"ot{i}", [P, D], at=hn_at + i * 8192) for i in range(2)]
        assert top[0] <= nc.sbuf_usable_end, (top[0], nc.sbuf_usable_end)

        PS = ctx.enter_context(nc.psum_tensor("psum", [P, 8, 512], F32))

        def bank(i, heads=GH):
            return PS[:, i, :].rearrange("p (h c) -> p h c", h=4)[:, 0:heads, :]

        def zb_bank(i):
            return PS[:, 2 + i % 6, :]

        def tile_of(b, i):
            return b[:, i, :] if isinstance(i, int) else b[:, bass.ds(i, 1), :].rearrange("p o t -> p (o t)")

        def slot(g_static):
            return g_static % SLOTS

        gcur, bcur = (small[:, 0:8], small[:, 130:138]), (small[:, 8:16], small[:, 138:146])
        norm_s, norm_e, norm_r = small[:, 16:24], small[:, 24:32], small[:, 32:40]
        sums = small[:, 40:56]
        egc, egl, ged, nbeg = small[:, 56:60], small[:, 60:64], small[:, 64:68], small[:, 68:72]
        gld = small[:, 72:76]
        osum, omean, orms = small[:, 76:80], small[:, 80:84], small[:, 84:88]
        m_g, m_b, m_gs, m_ss, m_se, m_r = (small[:, 96 + i:97 + i] for i in range(6))
        m_sums, m_eg, m_nd, m_ed, m_sel8 = (small[:, 104:106], small[:, 106:107], small[:, 107:108],
                                            small[:, 108:109], small[:, 112:120])
        m_sel8b = small[:, 120:128]
        m_egl = small[:, 128:129]

        def heads_of(v, width=P):
            return v.unsqueeze(2).broadcast_to([P, GH, width])

        def blocks_of(b, l, odd):
            return b.rearrange("p h (n two s) -> p h n two s", two=2, s=1 << l)[:, :, :, odd, :]

        def over_heads(m):
            return m.unsqueeze(1).broadcast_to([P, GH, P])

        w_in_v = w_in[0].rearrange("(k p) n -> p k n", p=P)
        pa_v = w_proj_a[0].rearrange("(k p) n -> p k n", p=P)
        pb_v = w_proj_b[0].rearrange("(k p) n -> p k n", p=P)
        wo_v = w_out[0].rearrange("(k p) n -> p k n", p=P)
        fg_v = w_ffn_gate[0].rearrange("(k p) n -> p k n", p=P)
        fu_v = w_ffn_up[0].rearrange("(k p) n -> p k n", p=P)
        fd_v = w_ffn_down[0].rearrange("(k p) n -> p k n", p=P)
        gates_v = gates_dram.rearrange("(k p) n -> p k n", p=P)
        x_v = x[0].rearrange("(t p) d -> p t d", p=P)
        out_v = out[0].rearrange("(t p) d -> p t d", p=P)

        def unit_tile(m, name, unit, last_chunk):
            return (S[name], unit + 1) if m == 0 else (S["chunk_used"], last_chunk + 1)

        def block_tile(t, name, unit, last_chunk):
            return (S[name], (TT - 1) * unit + t + 1) if t < TT - 1 else (S["chunk_used"], last_chunk + 1)

        block = ctx.enter_context(nc.Block())

        @block.sync
        def _(sp):
            def load_x(u, src, rows):
                if u >= 2:
                    sp.wait_ge(S["x_scaled"], u - 1)
                sp.dma_start(xt[u % 2][0:rows, :], src).then_inc(x_landed[u % 2], 16)

            def load(g, g_static, src, k):
                if not (isinstance(g, int) and g < SLOTS):
                    sp.wait_ge(S["lo_ready"], g - (SLOTS - 1))
                s = slot(g_static)
                sp.dma_start(raw[s][:].rearrange("p (k n) -> p k n", k=k), src).then_inc(landed[s], 16)

            for name, count in FREE.items():
                sp.sem_inc(S[name], count)
            load_x(0, meta_tokens, META)
            load_x(1, x_v[:, 0, :], P)
            sp.dma_start(rows_a[:, :], conv_w[0].rearrange("j (m p) -> (j m) p", p=P)).then_inc(S["rows_landed"], 16)
            at = 0
            for v, n in ((norm_mix_w[0], KT), (norm_ffn_w[0], KT), (pool_scale[0], HEADS), (o_norm_w[0], 1)):
                sp.dma_start(rows_b[at:at + n, :], v.rearrange("(m p) -> m p", p=P)).then_inc(S["rows_landed"], 16)
                at += n
            for c in range(4):
                load(c, c, w_in_v[:, 4 * c:4 * c + 4, 0:UNIT], 4)
            for t in range(1, TT):
                load_x(t + 1, x_v[:, t, :], P)
            sp.dma_start(ab_raw[:, :, :], w_in_v[:, :, COL_AB:COL_AB + 2 * HEADS]).then_inc(S["ab_landed"], 16)
            sp.dma_start(alog_b[:, :], a_log[0].partition_broadcast(P)).then_inc(S["small_landed"], 16)
            sp.dma_start(dtb_b[:, :], dt_bias[0].partition_broadcast(P)).then_inc(S["small_landed"], 16)
            sp.dma_start(poolw[:, :, :, :], pool_w[0].rearrange("g (k p) d -> p g k d", p=P)).then_inc(S["poolw_landed"], 16)
            with sp.Fori(1, N_A) as u:
                for c in range(4):
                    load(G_A + 4 * u + c, c, w_in_v[:, 4 * c:4 * c + 4, bass.ds(UNIT * u, UNIT)], 4)
            with sp.Fori(0, N_GATES) as u:
                for c in range(4):
                    load(G_GATES + 4 * u + c, c, w_in_v[:, 4 * c:4 * c + 4, bass.ds(COL_GATES + UNIT * u, UNIT)], 4)
            with sp.Fori(0, N_POOL) as u:
                for c in range(4):
                    load(G_P + 4 * u + c, c, w_in_v[:, 4 * c:4 * c + 4, bass.ds(COL_P + UNIT * u, UNIT)], 4)
            with sp.Fori(0, N_Z) as u:
                for c in range(4):
                    load(G_Z + 4 * u + c, c, w_in_v[:, 4 * c:4 * c + 4, bass.ds(COL_Z + UNIT * u, UNIT)], 4)
            sp.wait_ge(S["gates_stored"], FREE["gates_stored"] + 16 * N_GATES)

            def merge_unit(u, first):
                for c in range(2):
                    load(G_MERGE + 4 * u + c, c, pa_v[:, 4 * c:4 * c + 4, bass.ds(UNIT * u, UNIT)], 4)
                for c in range(2):
                    load(G_MERGE + 4 * u + 2 + c, 2 + c, pb_v[:, 4 * c:4 * c + 4, bass.ds(UNIT * u, UNIT)], 4)
                if first:
                    sp.wait_ge(S["z_y"], FREE["z_y"] + 2 * N_Z)
                else:
                    sp.wait_ge(S["merged_sum"], FREE["merged_sum"] + 2 * u)
                sp.dma_start(gate_a[:, :, :], gates_v[:, bass.ds(2 * u, 2), :]).then_inc(S["gate_a_landed"], 16)
                sp.dma_start(gate_b[:, :, :], gates_v[:, bass.ds(KT + 2 * u, 2), :]).then_inc(S["gate_b_landed"], 16)

            merge_unit(0, True)
            with sp.Fori(1, N_MERGE) as u:
                merge_unit(u, False)

            def out_unit(u, first):
                for c in range(8):
                    load(G_OUT + 8 * u + c, c, wo_v[:, 2 * c:2 * c + 2, bass.ds(BLOCK * u, BLOCK)], 2)
                if first:
                    sp.wait_ge(S["chunk_used"], G_OUT)
                else:
                    sp.wait_ge(S["h1_ready"], FREE["h1_ready"] + TT * u)
                sp.dma_start(xr[:, :, :], x_v[:, :, bass.ds(BLOCK * u, BLOCK)]).then_inc(S["xr_landed"], 16)

            out_unit(0, True)
            with sp.Fori(1, N_OUT) as u:
                out_unit(u, False)

            def gate_up(g, u):
                for sub in range(2):
                    for i, v in enumerate((fg_v, fu_v)):
                        for c in range(4):
                            n = 8 * sub + 4 * i + c
                            load(g + n, n, v[:, 4 * c:4 * c + 4, bass.ds(BLOCK * u + UNIT * sub, UNIT)], 4)

            def down(g, u):
                for blk in range(N_OUT):
                    for c in range(2):
                        n = 2 * blk + c
                        load(g + n, n, fd_v[:, bass.ds(4 * u + 2 * c, 2), BLOCK * blk:BLOCK * (blk + 1)], 2)

            gate_up(G_FFN, 0)
            with sp.Fori(0, N_FFN // 2) as i:
                g = G_FFN + 16 + 48 * i
                gate_up(g, 2 * i + 1)
                down(g + 16, 2 * i)
                gate_up(g + 24, 2 * i + 2)
                down(g + 40, 2 * i + 1)
            down(G_END - 8, N_FFN - 1)
            sp.dma_start(scalew[:, :], norm_final_w.partition_broadcast(P)).then_inc(S["scalew_landed"], 16)
            for t in range(TT):
                sp.wait_ge(S["f_scaled"], t + 1)
                sp.dma_start(out_v[:, t, :], ot[t % 2][:, :]).then_inc(S[f"out_stored{t % 2}"], 16)
            for i in range(2):
                sp.wait_ge(S[f"out_stored{i}"], 16 * TT // 2)

        @block.gpsimd
        def _(pool):
            built = [0]

            def const(ins):
                built[0] += 1
                ins.then_inc(S["consts_built"], 1)
                pool.wait_ge(S["consts_built"], built[0])

            const(pool.memset(ident[:], 0.0))
            const(pool.affine_select(out=ident[:], in_=ident[:], compare_op=ALU.not_equal, fill=1.0, base=0,
                                     pattern=[[-1, P]], channel_multiplier=1))
            const(pool.memset(minus_half[:], -0.5))
            const(pool.memset(zero, 0.0))

            def rms_of(col, mean, eps, ordinal, rows=P):
                pool.wait_ge(S["x_squared"], ordinal + 1)
                pool.tensor_scalar(rms_a[0:rows, col:col + 1], ssq[0:rows, col:col + 1], mean, eps, ALU.mult, ALU.add) \
                    .then_inc(S["x_rms_a"], 1)
                pool.wait_ge(S["x_rms_a"], ordinal + 1)
                pool.tensor_tensor(rms[0:rows, col:col + 1], rms_a[0:rows, col:col + 1], minus_half[0:rows, 0:1], ALU.pow) \
                    .then_inc(S["x_rms"], 1)

            def lo_quads(u, ybuf, dst_hi, dst_lo, cols, n):
                for q in range(4):
                    pool.wait_ge(S["x_hi"], 4 * u + q + 1)
                    pool.tensor_tensor(dst_lo[:, 4 * q:4 * q + 4, cols], ybuf[q][:, :, 0:n],
                                       dst_hi[:, 4 * q:4 * q + 4, cols].bitcast(F32), ALU.subtract) \
                        .then_inc(S["x_lo"], 1)

            rms_of(0, 1.0 / D, RMS_EPS, 0, META)
            rms_of(1, 1.0 / D, RMS_EPS, 1)
            lo_quads(0, xy, hn_hi, hn_lo, slice(0, META), META)
            for t in range(TT):
                if t + 1 < TT:
                    rms_of(t + 2, 1.0 / D, RMS_EPS, t + 2)
                lo_quads(t + 1, xy, hn_hi, hn_lo, slice(META + P * t, META + P * (t + 1)), P)

            const(pool.memset(ones[:], 1.0))
            const(pool.affine_select(out=upper[:], in_=ones[:], compare_op=ALU.is_ge, fill=0.0, base=0,
                                     pattern=[[1, P]], channel_multiplier=-1))
            const(pool.memset(cap[:], 0.0))
            const(pool.affine_select(out=cap[:], in_=cap[:], compare_op=ALU.is_ge, fill=NEG, base=0,
                                     pattern=[[1, P]], channel_multiplier=-1))
            const(pool.memset(levels[:], 0.0))
            for l in range(LEVELS):
                s = 1 << l
                n = P // (2 * s)
                m = levels[:, l, :].rearrange("p (n w) -> p n w", w=2 * s)
                const(pool.memset(m[:, :, s:2 * s], 1.0))
                const(pool.affine_select(out=m, in_=m, compare_op=ALU.is_ge, fill=0.0, base=0,
                                         pattern=[[-2 * s, n], [0, 2 * s]], channel_multiplier=1))
                const(pool.affine_select(out=m, in_=m, compare_op=ALU.is_ge, fill=0.0, base=s - 1,
                                         pattern=[[2 * s, n], [0, 2 * s]], channel_multiplier=-1))
            for dst, src, w in ((meta_upper[:], upper[:], META), (meta_block[:], ones[:], META),
                                (meta_sel[:], ones[:, 0:HEADS], 1)):
                dv, sv = (a.rearrange("p (n w) -> p n w", w=w) for a in (dst, src))
                const(pool.affine_select(out=dv, in_=sv, compare_op=ALU.is_ge, fill=0.0, base=0,
                                         pattern=[[-META, HEADS], [0, w]], channel_multiplier=1))
                const(pool.affine_select(out=dv, in_=dv, compare_op=ALU.is_ge, fill=0.0, base=META - 1,
                                         pattern=[[META, HEADS], [0, w]], channel_multiplier=-1))
            const(pool.tensor_copy(meta_rep[:].rearrange("p (h c) -> p h c", h=HEADS),
                                   ident[0:META, 0:META].unsqueeze(1).broadcast_to([META, HEADS, META])))
            const(pool.tensor_scalar(meta_neg[:], meta_upper[:], -1.0, -NEG, ALU.add, ALU.mult))

            pool.wait_ge(S["qkv_ready"], FREE["qkv_ready"] + 2 * N_A)
            pool.tensor_copy(B[1][:, 0, :].rearrange("p (h c) -> p h c", h=HEADS), qkv[:, K_T:K_T + HEADS, 0:META]) \
                .then_inc(S["meta_staged"], 1)
            pool.tensor_copy(B[2][:, 0, :].rearrange("p (h c) -> p h c", h=HEADS), qkv[:, VT:VT + HEADS, 0:META]) \
                .then_inc(S["meta_staged"], 1)
            pool.wait_ge(S["meta_vec"], 4)
            pool.tensor_tensor(m_r, m_se, minus_half[:, 0:1], ALU.pow).then_inc(S["meta_pool"], 1)
            pool.wait_ge(S["meta_vec"], 12)
            for l in range(META_LEVELS):
                pool.tensor_tensor(B[4][:, l, :], B[11][:, 0, :], levels[:, l, :], ALU.mult) \
                    .then_inc(S["meta_pool"], 1)

            def stage(n, hf):
                h0 = GH * hf
                v = 2 * n + hf
                tok = bass.ds(META + P * n, P) if not isinstance(n, int) else slice(META + P * n, META + P * (n + 1))
                row = bass.ds(n + 1, 1) if not isinstance(n, int) else slice(n + 1, n + 2)
                if not (isinstance(n, int) and v == 0):
                    pool.wait_ge(S["s_products"], 2 * v)
                    pool.wait_ge(S["rhs_ready"], GH * v)
                for b, t0 in ((7, QT), (8, K_T), (6, VT)):
                    pool.tensor_copy(B[b][:], qkv[:, t0 + h0:t0 + h0 + GH, tok]).then_inc(S["staged"], 1)
                pool.tensor_copy(gcur[hf], g_all[:, row, :].rearrange("p o h -> p (o h)")).then_inc(S["staged"], 1)
                pool.tensor_copy(bcur[hf], b_all[:, row, :].rearrange("p o h -> p (o h)")).then_inc(S["staged"], 1)

            def gdn_pool(n, hf, following):
                v = 2 * n + hf
                pool.wait_ge(S["norms_summed"], 2 * v + 2)
                pool.tensor_tensor(norm_r, norm_e, minus_half[:, 0:8], ALU.pow).then_inc(S["norms_ready"], 1)
                pool.wait_ge(S["g_differenced"], v + 1)
                pool.tensor_tensor(B[9][:], B[9][:], over_heads(cap[:]), ALU.add).then_inc(S["g_masked"], 1)
                pool.wait_ge(S["decays_small"], 3 * v + 3)
                pool.wait_ge(S["k_scaled"], v + 1)
                pool.tensor_tensor(B[5][:], B[4][:], heads_of(ged), ALU.mult).then_inc(S["kd_ready"], 1)
                pool.wait_ge(S["nt_ready"], v + 1)
                for l in range(LEVELS):
                    if l >= 2:
                        pool.wait_ge(S["level_product"], LEVELS * v + l - 1)
                    pool.tensor_tensor(B[1 + l % 2][:], B[10][:], over_heads(levels[:, l, :]), ALU.mult) \
                        .then_inc(S["level_masked"], 1)
                    if l >= 1:
                        if l >= 2:
                            pool.wait_ge(S["tt_product"], LEVELS * v + l - 1)
                        dead = blocks_of(XB[l % 2][:], l, 1)
                        if l == 2:
                            pool.wait_ge(S["t_ready"], (LEVELS - 1) * v + 1)
                        nothing = zero.unsqueeze(2).unsqueeze(3).broadcast_to(dead.shape)
                        pool.tensor_tensor(dead, nothing, nothing, ALU.mult).then_inc(S["x_cleared"], 1)
                    if l == 3 and following is not None:
                        stage(*following)
                pool.wait_ge(S["o_mean"], v + 1)
                pool.tensor_tensor(orms, omean, minus_half[:, 0:GH], ALU.pow).then_inc(S["o_rms"], 1)

            pool.wait_ge(S["state_ready"], 1)
            stage(0, 0)
            with pool.Fori(0, CH - 1) as n:
                gdn_pool(n, 0, (n, 1))
                gdn_pool(n, 1, (n + 1, 0))
            gdn_pool(CH - 1, 0, (CH - 1, 1))
            gdn_pool(CH - 1, 1, None)
            pool.wait_ge(S["state_ready"], 2 * CH + 1)

            step = [0]

            def chained(ins):
                step[0] += 1
                ins.then_inc(S["window_step"], 1)
                pool.wait_ge(S["window_step"], step[0])

            for i in range(HEADS):
                pool.wait_ge(S["p_copied"], FREE["p_copied"] + i + 1)
                g = i // 2
                src = p_in[:, i, :]
                for l in range(g + 1):
                    s = 1 << l
                    dst = win[l % 2]
                    chained(pool.tensor_tensor(dst[:, 2 * s - 1:TOK], src[:, 2 * s - 1:TOK], src[:, s - 1:TOK - s],
                                               ALU.add))
                    src = dst
                mean = win[(g + 1) % 2]
                chained(pool.tensor_scalar(mean[:, META:TOK], src[:, META:TOK], 1.0 / (2 << g), None, ALU.mult))
                chained(pool.tensor_tensor(pooled[:, i, :], mean[:, META:TOK], p_in[:, i, META:TOK], ALU.subtract))
            pool.memset(minus_half[:, 8:9], -0.5).then_inc(S["pooled_ready"], 1)

            with pool.Fori(0, N_MERGE) as u:
                for m in range(2):
                    pool.wait_ge(S["yb_gated"], FREE["yb_gated"] + 2 * u + m + 1)
                    pool.tensor_tensor(mg[:, m, :], gate_a[:, m, :], gate_b[:, m, :], ALU.add).then_inc(S["merged_sum"], 1)

            rms_of(5, 1.0 / D, RMS_EPS, 5)
            for t in range(TT):
                if t + 1 < TT:
                    rms_of(t + 6, 1.0 / D, RMS_EPS, t + 6)
                lo_quads(t + 5, hy, hn_hi, hn_lo, slice(P * t, P * (t + 1)), P)

            for t in range(TT):
                pool.wait_ge(S["f_squared"], t + 1)
                pool.tensor_scalar(rms_a[:, 9 + t:10 + t], ssq[:, 9 + t:10 + t], 1.0 / D, RMS_EPS, ALU.mult, ALU.add) \
                    .then_inc(S["f_rms_a"], 1)
                pool.wait_ge(S["f_rms_a"], t + 1)
                pool.tensor_tensor(rms[:, 9 + t:10 + t], rms_a[:, 9 + t:10 + t], minus_half[:, 0:1], ALU.pow) \
                    .then_inc(S["f_rms"], 1)

        @block.scalar
        def _(act):
            def split(g, g_static):
                s = slot(g_static)
                if isinstance(g, int):
                    act.wait_ge(landed[s], 16 * (g // SLOTS + 1))
                    if g >= SLOTS:
                        act.wait_ge(S["chunk_used"], g - (SLOTS - 1))
                else:
                    act.wait_ge(landed[s], 4 * (g - g_static % SLOTS) + 16)
                    act.wait_ge(S["chunk_used"], g - (SLOTS - 1))
                act.activation(whi[s][:], raw[s][:], ACT.Copy).then_inc(S["hi_ready"], 1)

            def square_tile(u, src, junk, rows, col):
                act.activation(junk[0:rows, :], src, ACT.Square, accum_out=ssq[0:rows, col:col + 1]) \
                    .then_inc(S["x_squared"], 1)

            def hi_quads(u, ybuf, dst, cols, n):
                for q in range(4):
                    act.wait_ge(S["x_weighted"], 4 * u + q + 1)
                    act.activation(dst[:, 4 * q:4 * q + 4, cols], ybuf[q][:, :, 0:n], ACT.Copy).then_inc(S["x_hi"], 1)

            for u in range(2):
                rows = META if u == 0 else P
                act.wait_ge(x_landed[u], 16)
                square_tile(u, xt[u][0:rows, :], xs[u], rows, u)
            act.wait_ge(S["rows_turned"], 1)
            act.activation(vec_a[:], PS[:, 4, 0:CONV * 3 * HEADS], ACT.Copy).then_inc(S["vectors_ready"], 1)
            act.activation(vec_b[:], PS[:, 5, 0:2 * KT + HEADS + 1], ACT.Copy).then_inc(S["vectors_ready"], 1)
            hi_quads(0, xy, hn_hi, slice(0, META), META)
            for t in range(TT):
                u = t + 1
                if t + 1 < TT:
                    act.wait_ge(x_landed[(u + 1) % 2], 16 * ((u + 1) // 2 + 1))
                    act.wait_ge(S["x_turned"], 4 * u)
                    square_tile(u + 1, xt[(u + 1) % 2][:, :], xs[(u + 1) % 2], P, u + 1)
                if t < SLOTS:
                    split(t, t)
                hi_quads(u, xy, hn_hi, slice(META + P * t, META + P * (t + 1)), P)

            with act.Fori(0, N_A) as u:
                for c in range(4):
                    if c == 3:
                        for m in range(2):
                            act.wait_ge(*unit_tile(m, "a_done", u, G_A + 4 * u + 3))
                            act.wait_ge(S["conv_done"], FREE["conv_done"] + 2 * u + m - 1)
                            act.activation(conv_in[m][:, CONV - 1:CONV - 1 + TOK].rearrange("p (a b) -> p a b", a=2),
                                           PS[:, 2 * m:2 * m + 2, 0:HALF], ACT.Copy).then_inc(S["a_copied"], 1)
                    split(G_A + 4 * u + c + 4, c)
                for m in range(2):
                    act.wait_ge(S["conv_done"], FREE["conv_done"] + 2 * u + m + 1)
                    act.activation(qkv[:, bass.ds(2 * u + m, 1), :].rearrange("p o t -> p (o t)"), conv_acc[m][:],
                                   ACT.Silu).then_inc(S["qkv_ready"], 1)

            act.wait_ge(S["ab_landed"], 16)
            act.activation(ab_h[:], ab_raw[:], ACT.Copy).then_inc(S["ab_hi"], 1)
            act.wait_ge(S["logits_copied"], 1)
            act.activation(b_all[:], lg[:, :, 0:HEADS], ACT.Sigmoid).then_inc(S["ab_act"], 1)
            act.wait_ge(S["small_landed"], 32)
            act.activation(alog_b[:], alog_b[:], ACT.Exp).then_inc(S["ab_act"], 1)
            act.wait_ge(S["ab_vec"], 2)
            act.activation(ab_t[1][:], ab_t[1][:], ACT.Exp).then_inc(S["ab_act"], 1)
            act.wait_ge(S["ab_act"], 3)
            act.activation(ab_t[2][:], ab_t[1][:], ACT.Ln, bias=1.0).then_inc(S["ab_act"], 1)

            act.wait_ge(S["meta_pe"], 1)
            act.activation(B[12][:, 0, :], PS[:, 1, 0:P], ACT.Square).then_inc(S["meta_act"], 1)
            act.wait_ge(S["meta_vec"], 8)
            act.activation(m_eg, m_sums[:, 0:1], ACT.Exp).then_inc(S["meta_act"], 1)
            act.activation(m_ed, m_nd, ACT.Exp).then_inc(S["meta_act"], 1)
            act.activation(B[9][:, 0, :], B[9][:, 0, :], ACT.Exp).then_inc(S["meta_act"], 1)
            act.wait_ge(S["meta_pe"], 3)
            act.activation(B[8][:, 0, :], PS[:, 1, 0:P], ACT.Copy).then_inc(S["meta_act"], 1)
            act.wait_ge(S["meta_pe"], META_LEVELS * 3 + 5)
            for i in range(2):
                act.activation(state[:, 4 * i:4 * i + 4, :], bank(2 + i), ACT.Copy).then_inc(S["meta_act"], 1)

            def gdn_act(n, hf):
                v = 2 * n + hf
                h0 = GH * hf
                act.wait_ge(S["qkv_turned"], 3 * v + 1)
                act.activation(B[12][:], bank(0), ACT.Square).then_inc(S["q_squared"], 1)
                act.wait_ge(S["qkv_turned"], 3 * v + 2)
                act.activation(B[13][:], bank(1), ACT.Square).then_inc(S["k_squared"], 1)
                yield
                act.wait_ge(S["sums_copied"], v + 1)
                act.activation(egc, sums[:, h0:h0 + GH], ACT.Exp).then_inc(S["decays_small"], 1)
                act.activation(egl, sums[:, 8 + h0:8 + h0 + GH], ACT.Exp).then_inc(S["decays_small"], 1)
                act.wait_ge(S["last_differenced"], v + 1)
                act.activation(ged, gld, ACT.Exp).then_inc(S["decays_small"], 1)
                act.wait_ge(S["g_masked"], v + 1)
                act.activation(B[9][:], B[9][:], ACT.Exp).then_inc(S["decay_ready"], 1)
                yield
                act.wait_ge(S["qk_turned"], 2 * v + 1)
                act.activation(B[7][:], bank(0), ACT.Copy).then_inc(S["qn_ready"], 1)
                act.wait_ge(S["qk_turned"], 2 * v + 2)
                act.activation(B[8][:], bank(1), ACT.Copy).then_inc(S["kn_ready"], 1)
                yield
                yield
                act.wait_ge(S["s_products"], 2 * v + 2)
                act.wait_ge(S["decays_small"], 3 * v + 3)
                for b in range(GH):
                    act.activation(B[12][:, b, :], PS[:, 5, P * b:P * (b + 1)], ACT.Copy, scale=egc[:, b:b + 1]) \
                        .then_inc(S["qs_ready"], 1)
                for _ in range(15):
                    yield
                act.wait_ge(S["vn_product"], v + 1)
                act.activation(B[10][:], bank(3), ACT.Copy).then_inc(S["vn_ready"], 1)
                yield
                act.wait_ge(S["o_ready"], v + 1)
                act.activation(B[13][:], B[12][:], ACT.Square).then_inc(S["o_squared"], 1)
                yield
                yield
                yield
                act.wait_ge(S["o_turned"], v + 1)
                act.activation(qkv[:, h0:h0 + GH, bass.ds(META + P * n, P)], bank(2), ACT.Copy).then_inc(S["o_stored"], 1)
                yield

            def gate_unit(n, u):
                r = 4 * n + u
                act.wait_ge(S["gates_stored"], FREE["gates_stored"] + 16 * r)
                for m in range(2):
                    act.wait_ge(*unit_tile(m, "gate_done", r, G_GATES + 4 * r + 3))
                    act.activation(gate_out[:, m, :], PS[:, 6 + m, :], ACT.Tanh, scale=0.5).then_inc(S["gate_freed"], 1)
                act.wait_ge(S["gate_freed"], FREE["gate_freed"] + 2 * r + 2)
                act.dma_start(gates_v[:, bass.ds(2 * r, 2), :], gate_out[:, :, :]).then_inc(S["gates_stored"], 16)

            with act.Fori(0, CH) as n:
                k = 0
                for hf in range(2):
                    steps_of_half = gdn_act(n, hf)
                    for _ in range(STEPS):
                        if k % 12 == 11:
                            gate_unit(n, k // 12)
                        next(steps_of_half)
                        if k % 3 == 2:
                            c = (k + 10) // 3
                            split(G_GATES + BODY_CHUNKS * n + c, c)
                        k += 1

            with act.Fori(0, N_POOL) as u:
                for c in range(4):
                    if c == 3:
                        for m in range(2):
                            act.wait_ge(*unit_tile(m, "p_done", u, G_P + 4 * u + 3))
                            act.activation(p_in[:, bass.ds(2 * u + m, 1), :].rearrange("p o (a b) -> p (o a) b", a=2),
                                           PS[:, 4 + 2 * m:6 + 2 * m, 0:HALF], ACT.Copy).then_inc(S["p_copied"], 1)
                    split(G_P + 4 * u + c + 4, c)

            act.wait_ge(S["gates_stored"], FREE["gates_stored"] + 16 * N_GATES)
            def z_unit(u, beside):
                for c in range(4):
                    beside(c)
                    if c == 3:
                        for m in range(2):
                            act.wait_ge(*unit_tile(m, "z_done", u, G_Z + 4 * u + 3))
                            act.wait_ge(S["z_y"], FREE["z_y"] + 2 * u + m - 1)
                            act.activation(zt[:, m, :], PS[:, m, :], ACT.Silu).then_inc(S["z_silu"], 1)
                        for m in range(2):
                            act.wait_ge(S["z_y"], FREE["z_y"] + 2 * u + m + 1)
                            act.activation(tile_of(o_hi, 2 * u + m), zy[:, m, :], ACT.Copy).then_inc(S["z_hi"], 1)
                    split(G_Z + 4 * u + c + 4, c)

            def zb_tiles(c):
                for i in range(2 * c, 2 * c + 2):
                    act.wait_ge(S["zb_y"], i + 1)
                    act.activation(zb_hi[:, i, :], zb_y[i % 2], ACT.Copy).then_inc(S["zb_hi"], 1)

            with act.Fori(0, N_Z - 1) as u:
                z_unit(u, lambda c: None)
            z_unit(N_Z - 1, zb_tiles)

            with act.Fori(0, N_MERGE) as u:
                for c in range(4):
                    if c == 3:
                        for m in range(2):
                            act.wait_ge(S["merged_sum"], FREE["merged_sum"] + 2 * u + m + 1)
                            act.activation(mg_hi[:, bass.ds(2 * u + m, 1), :].rearrange("p o t -> p (o t)"),
                                           mg[:, m, :], ACT.Copy, scale=0.5).then_inc(S["merged_hi"], 1)
                    split(G_MERGE + 4 * u + c + 4, c)

            with act.Fori(0, N_OUT) as u:
                for c in range(8):
                    split(G_OUT + 8 * u + c + 4, c)

            for t in range(TT + 1):
                if t < TT:
                    act.wait_ge(S["h1_ready"], FREE["h1_ready"] + TT * N_OUT)
                    if t >= 2:
                        act.wait_ge(S["x_turned"], 4 * (t + 4))
                    square_tile(t + 5, h[:, t, :], hs[t % 2], P, t + 5)
                if t > 0:
                    hi_quads(t + 4, hy, hn_hi, slice(P * (t - 1), P * t), P)

            def gate_up(g, u, slot_a, splits=16):
                for sub in range(2):
                    for c in range(8):
                        if c == 3:
                            for m in range(2):
                                r = 4 * u + 2 * sub + m
                                act.wait_ge(*unit_tile(m, "fg_done", 2 * u + sub, g + 8 * sub + 3))
                                act.wait_ge(S["act_y"], FREE["act_y"] + r - 1)
                                act.activation(sg[:, m, :], PS[:, m, :], ACT.Silu).then_inc(S["silu_ready"], 1)
                        if c == 7:
                            for m in range(2):
                                r = 4 * u + 2 * sub + m
                                act.wait_ge(S["act_y"], FREE["act_y"] + r + 1)
                                act.activation(a_hi[:, slot_a, 2 * sub + m, :], ay[:, m, :], ACT.Copy) \
                                    .then_inc(S["act_hi"], 1)
                        split(g + 8 * sub + c + 4, c)

            def down(g):
                for c in range(8):
                    split(g + c + 4, c)

            gate_up(G_FFN, 0, 0)
            with act.Fori(0, N_FFN // 2) as i:
                g = G_FFN + 16 + 48 * i
                gate_up(g, 2 * i + 1, 1)
                down(g + 16)
                gate_up(g + 24, 2 * i + 2, 0)
                down(g + 40)
            for c in range(4):
                split(G_END - 4 + c, c)
            for t in range(TT):
                act.wait_ge(S["h2_ready"], FREE["h2_ready"] + N_FFN * N_OUT * TT)
                if t >= 2:
                    act.wait_ge(S[f"out_stored{t % 2}"], 16)
                act.activation(ot[t % 2][:], h[:, t, :], ACT.Square, accum_out=ssq[:, 9 + t:10 + t]) \
                    .then_inc(S["f_squared"], 1)

        @block.vector
        def _(dve):
            def split(g, g_static):
                s = slot(g_static)
                dve.wait_ge(S["hi_ready"], g + 1)
                dve.tensor_tensor(wlo[s][:], raw[s][:], whi[s][:].bitcast(F32), ALU.subtract).then_inc(S["lo_ready"], 1)

            def scale_tile(u, col, dst, src, rows):
                dve.wait_ge(S["x_rms"], u + 1)
                dve.tensor_scalar(dst, src, rms[0:rows, col:col + 1], None, ALU.mult).then_inc(S["x_scaled"], 1)

            def weight_quads(u, ybuf, w, n):
                for q in range(4):
                    dve.wait_ge(S["x_turned"], 4 * u + q + 1)
                    if u not in (0, 5):
                        dve.wait_ge(S["x_lo"], 4 * u + q - 3)
                    dve.tensor_tensor(ybuf[q][:, :, 0:n], bank(q)[:, :, 0:n],
                                      w[:, 4 * q:4 * q + 4].unsqueeze(2).broadcast_to([P, 4, n]), ALU.mult) \
                        .then_inc(S["x_weighted"], 1)

            for m in range(2):
                dve.memset(conv_in[m][:, 0:CONV - 1], 0.0).then_inc(S["vectors_more"], 1)
            scale_tile(0, 0, xs[0][0:META, :], xt[0][0:META, :], META)
            scale_tile(1, 1, xs[1][:], xt[1][:], P)
            dve.wait_ge(S["vectors_ready"], 2)
            weight_quads(0, xy, nmix, META)
            for t in range(TT):
                u = t + 1
                if t + 1 < TT:
                    scale_tile(u + 1, u + 1, xs[(u + 1) % 2][:], xt[(u + 1) % 2][:], P)
                if t < SLOTS:
                    split(t, t)
                weight_quads(u, xy, nmix, P)

            dve.wait_ge(S["vectors_more"], 2)
            with dve.Fori(0, N_A) as u:
                for c in range(4):
                    if c == 3:
                        for m in range(2):
                            dve.wait_ge(S["a_copied"], FREE["a_copied"] + 2 * u + m + 1)
                            dve.wait_ge(S["qkv_ready"], FREE["qkv_ready"] + 2 * u + m - 1)
                            r = 2 * u + m
                            for j in range(CONV):
                                tap = vec_a[:, bass.ds(3 * HEADS * j + r, 1)]
                                src = conv_in[m][:, j:j + TOK]
                                if j == 0:
                                    ins = dve.tensor_scalar(conv_acc[m][:], src, tap, None, ALU.mult)
                                else:
                                    dve.wait_ge(S["conv_step"], 3 * r + j)
                                    ins = dve.scalar_tensor_tensor(conv_acc[m][:], src, tap, conv_acc[m][:],
                                                                   ALU.mult, ALU.add)
                                ins.then_inc(S["conv_done"] if j == CONV - 1 else S["conv_step"], 1)
                    split(G_A + 4 * u + c + 4, c)

            dve.wait_ge(S["ab_hi"], 1)
            dve.tensor_tensor(ab_l[:], ab_raw[:], ab_h[:].bitcast(F32), ALU.subtract).then_inc(S["ab_lo"], 1)
            dve.wait_ge(S["ab_meta"], 1)
            dve.tensor_copy(meta_lg[:], PS[0:META, 5, 0:2 * HEADS]).then_inc(S["ab_meta_copied"], 1)
            dve.wait_ge(S["ab_done"], 1)
            dve.tensor_copy(lg[:], PS[:, 4, 0:(CH + 1) * 2 * HEADS].rearrange("p (t c) -> p t c", c=2 * HEADS)) \
                .then_inc(S["logits_copied"], 1)
            dve.wait_ge(S["logits_copied"], 1)
            dve.wait_ge(S["small_landed"], 32)
            bc5 = [P, CH + 1, HEADS]
            dve.tensor_tensor(ab_t[0][:], lg[:, :, HEADS:], dtb_b[:].unsqueeze(1).broadcast_to(bc5), ALU.add) \
                .then_inc(S["ab_vec"], 1)
            dve.wait_ge(S["ab_vec"], 1)
            dve.scalar_tensor_tensor(ab_t[1][:], ab_t[0][:], -1.0, ab_t[0][:], ALU.mult, ALU.min) \
                .then_inc(S["ab_vec"], 1)
            dve.wait_ge(S["ab_act"], 4)
            dve.scalar_tensor_tensor(ab_t[3][:], ab_t[0][:], 0.0, ab_t[2][:], ALU.max, ALU.add).then_inc(S["ab_vec"], 1)
            dve.wait_ge(S["ab_vec"], 3)
            dve.scalar_tensor_tensor(g_all[:], ab_t[3][:], -1.0, alog_b[:].unsqueeze(1).broadcast_to(bc5),
                                     ALU.mult, ALU.mult).then_inc(S["ab_vec"], 1)

            steps = [0]

            def meta(ins):
                steps[0] += 1
                ins.then_inc(S["meta_vec"], 1)
                dve.wait_ge(S["meta_vec"], steps[0])

            dve.wait_ge(S["consts_built"], N_CONSTS)
            dve.wait_ge(S["ab_vec"], 4)
            meta(dve.tensor_tensor(m_sel8, g_all[:, 0, :], meta_sel[:], ALU.mult))
            meta(dve.tensor_reduce(m_g, m_sel8, AX.X, ALU.add))
            dve.wait_ge(S["meta_act"], 1)
            meta(dve.tensor_reduce(m_ss, B[12][:, 0, :], AX.X, ALU.add))
            meta(dve.tensor_scalar(m_se, m_ss, L2_EPS, None, ALU.add))
            dve.wait_ge(S["meta_pe"], 2)
            meta(dve.tensor_copy(m_sums, PS[:, 4, 0:2]))
            meta(dve.scalar_tensor_tensor(B[9][:, 0, :], PS[:, 3, 0:P], m_sums[:, 0:1], meta_upper[:],
                                          ALU.subtract, ALU.mult))
            meta(dve.tensor_tensor(B[9][:, 0, :], B[9][:, 0, :], meta_neg[:], ALU.add))
            meta(dve.tensor_tensor(m_nd, m_sums[:, 1:2], m_sums[:, 0:1], ALU.subtract))
            meta(dve.tensor_tensor(m_sel8b, b_all[:, 0, :], meta_sel[:], ALU.mult))
            meta(dve.tensor_reduce(m_b, m_sel8b, AX.X, ALU.add))
            dve.wait_ge(S["meta_pool"], 1)
            meta(dve.tensor_scalar(B[3][:, 0, :], PS[:, 1, 0:P], m_r, None, ALU.mult))
            dve.wait_ge(S["meta_pe"], 4)
            dve.wait_ge(S["meta_act"], 4)
            meta(dve.tensor_tensor(B[11][:, 0, :], PS[:, 0, 0:P], B[9][:, 0, :], ALU.mult))
            meta(dve.tensor_scalar(B[5][:, 0, :], B[3][:, 0, :], m_ed, None, ALU.mult))
            meta(dve.tensor_scalar(B[6][:, 0, :], PS[:, 2, 0:P], m_b, None, ALU.mult))
            xb, tb, ttb = B[7][:, 0, :], B[10][:, 0, :], B[0][:, 0, :]
            dve.wait_ge(S["meta_pe"], 5)
            meta(dve.tensor_scalar(xb, PS[:, 0, 0:P], m_b, None, ALU.mult))
            meta(dve.tensor_tensor(tb, ident[:], xb, ALU.subtract))
            dve.wait_ge(S["meta_pe"], 6)
            meta(dve.tensor_tensor(ttb, ident[:], PS[:, 1, 0:P], ALU.subtract))
            for l in range(1, META_LEVELS):
                dve.wait_ge(S["meta_pe"], 3 * l + 4)
                meta(dve.tensor_scalar(xb, PS[:, 0, 0:P], m_b, None, ALU.mult))
                dve.wait_ge(S["meta_pe"], 3 * l + 6)
                meta(dve.tensor_tensor(tb, tb, PS[:, 2, 0:P], ALU.subtract))
                meta(dve.tensor_tensor(ttb, ttb, PS[:, 1, 0:P], ALU.subtract))
            dve.wait_ge(S["meta_pe"], 3 * META_LEVELS + 4)
            meta(dve.tensor_tensor(meta_u[:], PS[:, 0, 0:P].unsqueeze(1).broadcast_to([P, HEADS, P]),
                                   meta_sel[:].unsqueeze(2).broadcast_to([P, HEADS, P]), ALU.mult))
            dve.wait_ge(S["meta_act"], 7)
            dve.memset(m_sel8b, 0.0).then_inc(S["state_ready"], 1)

            def gdn_dve(n, hf):
                v = 2 * n + hf
                h0 = GH * hf
                bh = bcur[hf][:, h0:h0 + GH]
                dve.wait_ge(S["q_squared"], v + 1)
                dve.tensor_reduce(norm_s[:, 0:GH], B[12][:], AX.X, ALU.add).then_inc(S["norms_a"], 1)
                dve.wait_ge(S["k_squared"], v + 1)
                dve.tensor_reduce(norm_s[:, GH:], B[13][:], AX.X, ALU.add).then_inc(S["norms_a"], 1)
                dve.wait_ge(S["norms_a"], 2 * v + 2)
                dve.tensor_scalar(norm_e[:, 0:GH], norm_s[:, 0:GH], L2_EPS, float(P), ALU.add, ALU.mult) \
                    .then_inc(S["norms_summed"], 1)
                dve.tensor_scalar(norm_e[:, GH:], norm_s[:, GH:], L2_EPS, None, ALU.add).then_inc(S["norms_summed"], 1)
                yield
                dve.wait_ge(S["gates_summed"], v + 1)
                dve.tensor_copy(sums, PS[:, 4, 0:16]).then_inc(S["sums_copied"], 1)
                dve.wait_ge(S["sums_copied"], v + 1)
                dve.tensor_tensor(B[9][:], bank(3), heads_of(sums[:, h0:h0 + GH]), ALU.subtract) \
                    .then_inc(S["g_differenced"], 1)
                dve.tensor_tensor(gld, sums[:, 8 + h0:8 + h0 + GH], sums[:, h0:h0 + GH], ALU.subtract) \
                    .then_inc(S["last_differenced"], 1)
                dve.wait_ge(S["norms_ready"], v + 1)
                dve.tensor_tensor(B[3][:], bank(0), heads_of(norm_r[:, 0:GH]), ALU.mult).then_inc(S["q_scaled"], 1)
                dve.tensor_tensor(B[4][:], bank(1), heads_of(norm_r[:, GH:]), ALU.mult).then_inc(S["k_scaled"], 1)
                dve.wait_ge(S["qkv_turned"], 3 * v + 3)
                dve.tensor_tensor(B[6][:], bank(2), heads_of(bh), ALU.mult).then_inc(S["vb_ready"], 1)
                dve.wait_ge(S["decays_small"], 3 * v + 3)
                dve.scalar_tensor_tensor(nbeg, bh, -1.0, egc, ALU.mult, ALU.mult).then_inc(S["nbeg_ready"], 1)
                yield
                yield
                dve.wait_ge(S["kk_done"], v + 1)
                dve.wait_ge(S["decay_ready"], v + 1)
                dve.tensor_tensor(B[10][:], bank(2), B[9][:], ALU.mult).then_inc(S["nt_ready"], 1)
                dve.wait_ge(S["kq_done"], v + 1)
                dve.wait_ge(S["kd_ready"], v + 1)
                dve.tensor_tensor(B[4][:], bank(3), B[9][:], ALU.mult).then_inc(S["pt_ready"], 1)
                yield
                dve.wait_ge(S["s_products"], 2 * v + 1)
                dve.wait_ge(S["nbeg_ready"], v + 1)
                for b in range(GH):
                    dve.scalar_tensor_tensor(B[0][:, b, :], PS[:, 4, P * b:P * (b + 1)], nbeg[:, b:b + 1],
                                             B[6][:, b, :], ALU.mult, ALU.add).then_inc(S["rhs_ready"], 1)
                yield
                dve.wait_ge(S["level_product"], LEVELS * v + 1)
                dve.tensor_tensor(B[3][:], bank(0), heads_of(bh), ALU.mult).then_inc(S["level_x"], 1)
                dve.wait_ge(S["level_x"], LEVELS * v + 1)
                dve.wait_ge(S["pt_ready"], v + 1)
                dve.tensor_tensor(B[9][:], over_heads(ident[:]), B[3][:], ALU.subtract).then_inc(S["t_ready"], 1)
                yield
                dve.wait_ge(S["tt_product"], LEVELS * v + 1)
                dve.tensor_tensor(B[11][:], over_heads(ident[:]), bank(1), ALU.subtract).then_inc(S["tt_ready"], 1)
                yield
                for l in range(1, LEVELS):
                    x = blocks_of(XB[l % 2][:], l, 0)
                    n_blocks, width = x.shape[2], x.shape[3]
                    dve.wait_ge(S["level_product"], LEVELS * v + l + 1)
                    dve.tensor_tensor(x, blocks_of(bank(0), l, 0),
                                      bh.unsqueeze(2).unsqueeze(3).broadcast_to([P, GH, n_blocks, width]), ALU.mult) \
                        .then_inc(S["level_x"], 1)
                    yield
                    if l < LEVELS - 1:
                        dve.wait_ge(S["t_product"], (LEVELS - 2) * v + l)
                        dve.wait_ge(S["t_ready"], (LEVELS - 1) * v + l)
                        t_even = blocks_of(B[9][:], l, 0)
                        dve.tensor_tensor(t_even, t_even, blocks_of(bank(2), l, 0), ALU.subtract).then_inc(S["t_ready"], 1)
                    dve.wait_ge(S["tt_product"], LEVELS * v + l + 1)
                    dve.wait_ge(S["tt_ready"], LEVELS * v + l)
                    tt_odd = blocks_of(B[11][:], l, 1)
                    dve.tensor_tensor(tt_odd, tt_odd, blocks_of(bank(1), l, 1), ALU.subtract).then_inc(S["tt_ready"], 1)
                    yield
                yield
                dve.wait_ge(S["o_product"], v + 1)
                dve.wait_ge(S["qs_ready"], GH * v + GH)
                dve.tensor_tensor(B[12][:], B[12][:], bank(0), ALU.add).then_inc(S["o_ready"], 1)
                yield
                dve.wait_ge(S["o_squared"], v + 1)
                dve.tensor_reduce(osum, B[13][:], AX.X, ALU.add).then_inc(S["o_sum"], 1)
                dve.wait_ge(S["o_sum"], v + 1)
                dve.tensor_scalar(omean, osum, 1.0 / P, RMS_EPS, ALU.mult, ALU.add).then_inc(S["o_mean"], 1)
                dve.wait_ge(S["ds_product"], v + 1)
                for b in range(GH):
                    ins = dve.scalar_tensor_tensor(state[:, h0 + b, :], state[:, h0 + b, :], egl[:, b:b + 1],
                                                   PS[:, 1, P * b:P * (b + 1)], ALU.mult, ALU.add)
                ins.then_inc(S["state_ready"], 1)
                yield
                dve.wait_ge(S["o_rms"], v + 1)
                dve.tensor_tensor(B[13][:], B[12][:], heads_of(orms), ALU.mult).then_inc(S["o_scaled"], 1)
                yield
                yield

            with dve.Fori(0, CH) as n:
                k = 0
                for hf in range(2):
                    for _ in gdn_dve(n, hf):
                        if k % 3 == 2:
                            c = (k + 10) // 3
                            split(G_GATES + BODY_CHUNKS * n + c, c)
                        k += 1

            with dve.Fori(0, N_POOL) as u:
                for c in range(4):
                    split(G_P + 4 * u + c + 4, c)

            def z_unit(u, beside):
                for c in range(4):
                    beside(c)
                    if c == 3:
                        for m in range(2):
                            dve.wait_ge(S["z_silu"], FREE["z_silu"] + 2 * u + m + 1)
                            dve.wait_ge(S["z_lo"], FREE["z_lo"] + 2 * u + m - 1)
                            o_tile = (qkv[:, 2 * u + m, META:] if isinstance(u, int) else
                                      qkv[:, bass.ds(2 * u + m, 1), META:].rearrange("p o t -> p (o t)"))
                            dve.scalar_tensor_tensor(zy[:, m, :], zt[:, m, :], onorm, o_tile, ALU.mult, ALU.mult) \
                                .then_inc(S["z_y"], 1)
                        for m in range(2):
                            dve.wait_ge(S["z_hi"], 2 * u + m + 1)
                            dve.tensor_tensor(tile_of(o_lo, 2 * u + m), zy[:, m, :],
                                              tile_of(o_hi, 2 * u + m).bitcast(F32), ALU.subtract).then_inc(S["z_lo"], 1)
                    split(G_Z + 4 * u + c + 4, c)

            def zb_tiles(c):
                for i in range(2 * c, 2 * c + 2):
                    dve.wait_ge(S["zb_done"], i + 1)
                    if i >= 2:
                        dve.wait_ge(S["zb_lo"], i - 1)
                    dve.tensor_scalar(zb_y[i % 2], zb_bank(i), pscale[:, i:i + 1], None, ALU.mult).then_inc(S["zb_y"], 1)
                    dve.wait_ge(S["zb_hi"], i + 1)
                    dve.wait_ge(S["zb_done"], i // 2 * 2 + 2)
                    dve.tensor_tensor(zb_lo[:, i, :], zb_y[i % 2], zb_hi[:, i, :].bitcast(F32), ALU.subtract) \
                        .then_inc(S["zb_lo"], 1)

            with dve.Fori(0, N_Z - 1) as u:
                z_unit(u, lambda c: None)
            z_unit(N_Z - 1, zb_tiles)

            with dve.Fori(0, N_MERGE) as u:
                for c in range(4):
                    if c == 1:
                        for m in range(2):
                            dve.wait_ge(S["gate_a_landed"], 16 * u + 16)
                            dve.wait_ge(*unit_tile(m, "ya_done", u, G_MERGE + 4 * u + 1))
                            dve.scalar_tensor_tensor(gate_a[:, m, :], gate_a[:, m, :], 1.0, PS[:, 4 + m, :],
                                                     ALU.add, ALU.mult).then_inc(S["ya_gated"], 1)
                    if c == 3:
                        for m in range(2):
                            dve.wait_ge(S["gate_b_landed"], 16 * u + 16)
                            dve.wait_ge(*unit_tile(m, "yb_done", u, G_MERGE + 4 * u + 3))
                            dve.wait_ge(S["ya_gated"], FREE["ya_gated"] + 2 * u + m + 1)
                            dve.scalar_tensor_tensor(gate_b[:, m, :], gate_b[:, m, :], 1.0, PS[:, 6 + m, :],
                                                     ALU.add, ALU.mult).then_inc(S["yb_gated"], 1)
                        for m in range(2):
                            dve.wait_ge(S["merged_hi"], 2 * u + m + 1)
                            one = bass.ds(2 * u + m, 1)
                            dve.scalar_tensor_tensor(mg_lo[:, one, :].rearrange("p o t -> p (o t)"), mg[:, m, :], 0.5,
                                                     mg_hi[:, one, :].rearrange("p o t -> p (o t)").bitcast(F32),
                                                     ALU.mult, ALU.subtract).then_inc(S["merged_lo"], 1)
                    split(G_MERGE + 4 * u + c + 4, c)

            with dve.Fori(0, N_OUT) as u:
                for c in range(8):
                    if c == 7:
                        for t in range(TT):
                            dve.wait_ge(S["xr_landed"], 16 * u + 16)
                            dve.wait_ge(*block_tile(t, "out_done", u, G_OUT + 8 * u + 7))
                            dve.tensor_tensor(h[:, t, bass.ds(BLOCK * u, BLOCK)], xr[:, t, :], PS[:, t, :], ALU.add) \
                                .then_inc(S["h1_ready"], 1)
                    split(G_OUT + 8 * u + c + 4, c)

            for t in range(TT):
                scale_tile(t + 5, t + 5, hs[t % 2][:], h[:, t, :], P)
                if t > 0:
                    weight_quads(t + 4, hy, nffn, P)
            weight_quads(TT + 4, hy, nffn, P)

            def gate_up(g, u, slot_a):
                for sub in range(2):
                    for c in range(8):
                        if c == 7:
                            for m in range(2):
                                r = 4 * u + 2 * sub + m
                                dve.wait_ge(*unit_tile(m, "fu_done", 2 * u + sub, g + 8 * sub + 7))
                                dve.wait_ge(S["silu_ready"], FREE["silu_ready"] + r + 1)
                                dve.wait_ge(S["act_lo"], FREE["act_lo"] + r - 1)
                                dve.tensor_tensor(ay[:, m, :], sg[:, m, :], PS[:, 2 + m, :], ALU.mult) \
                                    .then_inc(S["act_y"], 1)
                            for m in range(2):
                                r = 4 * u + 2 * sub + m
                                dve.wait_ge(S["act_hi"], r + 1)
                                dve.tensor_tensor(a_lo[:, slot_a, 2 * sub + m, :], ay[:, m, :],
                                                  a_hi[:, slot_a, 2 * sub + m, :].bitcast(F32), ALU.subtract) \
                                    .then_inc(S["act_lo"], 1)
                        split(g + 8 * sub + c + 4, c)

            def down(g, u, last=False):
                for blk in range(N_OUT):
                    for c in range(2):
                        if c == 1:
                            for t in range(TT):
                                r = TT * (N_OUT * u + blk) + t
                                dve.wait_ge(*block_tile(t, "down_done", N_OUT * u + blk, g + 2 * blk + 1))
                                dve.wait_ge(S["h2_ready"], FREE["h2_ready"] + r - TT + 1)
                                dst = h[:, t, BLOCK * blk:BLOCK * (blk + 1)]
                                dve.tensor_tensor(dst, dst, PS[:, 4 + t, :], ALU.add).then_inc(S["h2_ready"], 1)
                        if not last or 2 * blk + c < 4:
                            split(g + 2 * blk + c + 4, 2 * blk + c)

            gate_up(G_FFN, 0, 0)
            with dve.Fori(0, N_FFN // 2) as i:
                g = G_FFN + 16 + 48 * i
                gate_up(g, 2 * i + 1, 1)
                down(g + 16, 2 * i)
                gate_up(g + 24, 2 * i + 2, 0)
                down(g + 40, 2 * i + 1)
            down(G_END - 8, N_FFN - 1, last=True)
            dve.wait_ge(S["scalew_landed"], 16)
            for t in range(TT):
                dve.wait_ge(S["f_rms"], t + 1)
                dve.scalar_tensor_tensor(ot[t % 2][:], h[:, t, :], rms[:, 9 + t:10 + t], scalew[:], ALU.mult, ALU.mult) \
                    .then_inc(S["f_scaled"], 1)

        @block.tensor
        def _(pe):
            def turn_quads(u, src, rows):
                pe.wait_ge(S["x_scaled"], u + 1)
                for q in range(4):
                    if u not in (0, 5):
                        pe.wait_ge(S["x_weighted"], 4 * u + q - 3)
                    for i in range(4):
                        k = 4 * q + i
                        ins = pe.transpose(bank(q)[:, i, 0:rows], src[0:rows, P * k:P * (k + 1)],
                                           ident[0:rows, 0:rows])
                    ins.then_inc(S["x_turned"], 1)

            def chunk_products(g, g_static, j, n_chunks, moving, outs, done, freed, used=True):
                s = slot(g_static)
                pe.wait_ge(S["lo_ready"], g + 1)
                for m in range(2):
                    if j == 0:
                        freed(m)
                    for k in range(4):
                        kt = 4 * j + k
                        hi, lo = moving(kt)
                        w = [t[s][:].rearrange("p (k n) -> p k n", k=4)[:, k, P * m:P * (m + 1)] for t in (whi, wlo)]
                        for i, (lhs, mv) in enumerate(((w[0], hi), (w[0], lo), (w[1], hi))):
                            for o, r in zip(outs(m), mv):
                                ins = pe.matmul(o, lhs, r, start=kt == 0 and i == 0,
                                                stop=kt == 4 * n_chunks - 1 and i == 2)
                            end = k == 3 and i == 2
                            if end and m == 0 and j == n_chunks - 1:
                                ins.then_inc(S[done], 1)
                            if end and m == 1:
                                ins.then_inc(S["chunk_used"], 1)
                            yield

            def run(products):
                for _ in products:
                    pass

            def token_chunk(g, g_static, k0, n_k, lhs_of, banks, done, freed):
                s = slot(g_static)
                pe.wait_ge(S["lo_ready"], g + 1)
                for t in range(TT):
                    if k0 == 0:
                        freed(t)
                    for k in range(2):
                        hi, lo = lhs_of(k0 + k, t)
                        w = [b[s][:, BLOCK * k:BLOCK * (k + 1)] for b in (whi, wlo)]
                        first, last = k0 + k == 0, k0 + k == n_k - 1
                        pe.matmul(PS[:, banks + t, :], hi, w[0], start=first, stop=False)
                        pe.matmul(PS[:, banks + t, :], hi, w[1], start=False, stop=False)
                        ins = pe.matmul(PS[:, banks + t, :], lo, w[0], start=False, stop=last)
                    if k0 + 2 == n_k and t < TT - 1:
                        ins.then_inc(S[done], 1)
                ins.then_inc(S["chunk_used"], 1)

            pe.wait_ge(S["consts_built"], 2)
            pe.wait_ge(S["rows_landed"], 80)
            na, nb = CONV * 3 * HEADS, 2 * KT + HEADS + 1
            pe.transpose(PS[:, 4, 0:na], rows_a[:, :], ident[0:na, 0:na])
            pe.transpose(PS[:, 5, 0:nb], rows_b[:, :], ident[0:nb, 0:nb]).then_inc(S["rows_turned"], 1)
            turn_quads(0, xs[0], META)
            for t in range(TT):
                turn_quads(t + 1, xs[(t + 1) % 2], P)

            pe.wait_ge(S["x_lo"], 4 * (TT + 1))

            def hn_halves(kt):
                return tuple([b[:, kt, HALF * i:HALF * (i + 1)] for i in range(2)] for b in (hn_hi, hn_lo))

            def hn_real(kt):
                return [hn_hi[:, kt, META:]], [hn_lo[:, kt, META:]]

            with pe.Fori(0, N_A) as u:
                for c in range(4):
                    run(chunk_products(G_A + 4 * u + c, c, c, 4, hn_halves,
                                       lambda m: [PS[:, 2 * m + i, 0:HALF] for i in range(2)], "a_done",
                                       lambda m: pe.wait_ge(S["a_copied"], FREE["a_copied"] + 2 * u + m - 1)))

            pe.wait_ge(S["ab_lo"], 1)
            for t in range(CH + 1):
                for k in range(KT):
                    own = slice(0, META) if t == 0 else slice(META + P * (t - 1), META + P * t)
                    dst = PS[0:META, 5, 0:2 * HEADS] if t == 0 else PS[:, 4, 2 * HEADS * t:2 * HEADS * (t + 1)]
                    pe.matmul(dst, hn_hi[:, k, own], ab_h[:, k, :], start=k == 0, stop=False)
                    pe.matmul(dst, hn_hi[:, k, own], ab_l[:, k, :], start=False, stop=False)
                    ins = pe.matmul(dst, hn_lo[:, k, own], ab_h[:, k, :], start=False, stop=k == KT - 1)
                if t == 0:
                    ins.then_inc(S["ab_meta"], 1)
            pe.wait_ge(S["ab_meta_copied"], 1)
            pe.wait_ge(S["consts_built"], N_CONSTS)
            pe.matmul(PS[:, 4, 0:2 * HEADS], meta_rep[:], meta_lg[:], start=True, stop=True).then_inc(S["ab_done"], 1)

            pe.wait_ge(S["meta_staged"], 2)
            pe.wait_ge(S["a_copied"], FREE["a_copied"] + 2 * N_A)
            pe.transpose(PS[:, 1, 0:P], B[1][:, 0, :], ident[:]).then_inc(S["meta_pe"], 1)
            pe.transpose(PS[:, 2, 0:P], B[2][:, 0, :], ident[:])
            pe.wait_ge(S["meta_vec"], 2)
            pe.wait_ge(S["consts_built"], N_CONSTS)
            pe.matmul(PS[:, 3, 0:P], m_g.broadcast_to([P, P]), meta_upper[:], start=True, stop=True)
            pe.matmul(PS[:, 4, 0:1], meta_upper[:], m_g, start=True, stop=True)
            pe.matmul(PS[:, 4, 1:2], meta_block[:], m_g, start=True, stop=True).then_inc(S["meta_pe"], 1)
            pe.wait_ge(S["meta_vec"], 11)
            pe.transpose(PS[:, 1, 0:P], B[3][:, 0, :], ident[:]).then_inc(S["meta_pe"], 1)
            pe.wait_ge(S["meta_act"], 5)
            pe.matmul(PS[:, 0, 0:P], B[8][:, 0, :], B[8][:, 0, :], start=True, stop=True).then_inc(S["meta_pe"], 1)
            pe.wait_ge(S["meta_pool"], 2)
            pe.transpose(PS[:, 0, 0:P], B[4][:, 0, :], ident[:]).then_inc(S["meta_pe"], 1)
            pe.wait_ge(S["meta_vec"], 15)
            pe.transpose(PS[:, 1, 0:P], B[7][:, 0, :], ident[:]).then_inc(S["meta_pe"], 1)
            for l in range(1, META_LEVELS):
                pe.wait_ge(S["meta_pool"], l + 2)
                pe.wait_ge(S["meta_vec"], 14 + 3 * l)
                pe.matmul(PS[:, 0, 0:P], B[4][:, l, :], B[10][:, 0, :], start=True, stop=True).then_inc(S["meta_pe"], 1)
                pe.wait_ge(S["meta_vec"], 15 + 3 * l)
                pe.matmul(PS[:, 2, 0:P], B[0][:, 0, :], B[7][:, 0, :], start=True, stop=True).then_inc(S["meta_pe"], 1)
                pe.matmul(PS[:, 1, 0:P], B[7][:, 0, :], B[0][:, 0, :], start=True, stop=True).then_inc(S["meta_pe"], 1)
            pe.wait_ge(S["meta_vec"], 14 + 3 * META_LEVELS)
            pe.matmul(PS[:, 0, 0:P], B[0][:, 0, :], B[6][:, 0, :], start=True, stop=True).then_inc(S["meta_pe"], 1)
            pe.wait_ge(S["meta_vec"], 15 + 3 * META_LEVELS)
            for i in range(2):
                ins = pe.matmul(bank(2 + i), B[5][:, 0, :], meta_u[:, 4 * i:4 * i + 4, :], start=True, stop=True)
            ins.then_inc(S["meta_pe"], 1)

            def gdn_pe(n, hf):
                v = 2 * n + hf
                h0 = GH * hf
                pe.wait_ge(S["staged"], 5 * v + 5)
                pe.wait_ge(S["state_ready"], v + 1)
                for j, b in enumerate((7, 8, 6)):
                    if j == 2:
                        pe.wait_ge(S["o_stored"], FREE["o_stored"] + v)
                    for i in range(GH):
                        ins = pe.transpose(bank(j)[:, i, :], B[b][:, i, :], ident[:])
                    ins.then_inc(S["qkv_turned"], 1)
                yield
                for i in range(GH):
                    pe.matmul(bank(3)[:, i, :], gcur[hf][:, h0 + i:h0 + i + 1].broadcast_to([P, P]), upper[:],
                              start=True, stop=True)
                pe.matmul(PS[:, 4, 0:8], upper[:], gcur[hf], start=True, stop=True)
                pe.matmul(PS[:, 4, 8:16], ones[:], gcur[hf], start=True, stop=True).then_inc(S["gates_summed"], 1)
                yield
                for j, (b, name) in enumerate(((3, "q_scaled"), (4, "k_scaled"))):
                    pe.wait_ge(S[name], v + 1)
                    for i in range(GH):
                        ins = pe.transpose(bank(j)[:, i, :], B[b][:, i, :], ident[:])
                    ins.then_inc(S["qk_turned"], 1)
                yield
                pe.wait_ge(S["kn_ready"], v + 1)
                pe.wait_ge(S["vb_ready"], v + 1)
                for i in range(GH):
                    ins = pe.matmul(bank(2)[:, i, :], B[8][:, i, :], B[8][:, i, :], start=True, stop=True)
                ins.then_inc(S["kk_done"], 1)
                for i in range(GH):
                    ins = pe.matmul(bank(3)[:, i, :], B[8][:, i, :], B[7][:, i, :], start=True, stop=True)
                ins.then_inc(S["kq_done"], 1)
                yield
                pe.wait_ge(S["sums_copied"], v + 1)
                for j in (8, 7):
                    for i in range(GH):
                        ins = pe.matmul(bank(4 if j == 8 else 5)[:, i, :], B[j][:, i, :], state[:, h0 + i, :],
                                        start=True, stop=True)
                    ins.then_inc(S["s_products"], 1)
                yield
                pe.wait_ge(S["level_masked"], LEVELS * v + 1)
                for i in range(GH):
                    ins = pe.transpose(bank(0)[:, i, :], B[1][:, i, :], ident[:])
                ins.then_inc(S["level_product"], 1)
                yield
                pe.wait_ge(S["level_x"], LEVELS * v + 1)
                for i in range(GH):
                    ins = pe.transpose(bank(1)[:, i, :], B[3][:, i, :], ident[:])
                ins.then_inc(S["tt_product"], 1)
                yield
                for l in range(1, LEVELS):
                    x = XB[l % 2]
                    pe.wait_ge(S["level_masked"], LEVELS * v + l + 1)
                    pe.wait_ge(S["t_ready"], (LEVELS - 1) * v + l)
                    for i in range(GH):
                        ins = pe.matmul(blocks_of(bank(0), l, 0)[:, i, :, :], B[1 + l % 2][:, i, :],
                                        blocks_of(B[9][:], l, 0)[:, i, :, :], start=True, stop=True)
                    ins.then_inc(S["level_product"], 1)
                    yield
                    pe.wait_ge(S["level_x"], LEVELS * v + l + 1)
                    pe.wait_ge(S["x_cleared"], (LEVELS - 1) * v + l)
                    pe.wait_ge(S["tt_ready"], LEVELS * v + l)
                    if l < LEVELS - 1:
                        for i in range(GH):
                            ins = pe.matmul(blocks_of(bank(2), l, 0)[:, i, :, :], B[11][:, i, :],
                                            blocks_of(x[:], l, 0)[:, i, :, :], start=True, stop=True)
                        ins.then_inc(S["t_product"], 1)
                    for i in range(GH):
                        ins = pe.matmul(blocks_of(bank(1), l, 1)[:, i, :, :], x[:, i, :],
                                        blocks_of(B[11][:], l, 1)[:, i, :, :], start=True, stop=True)
                    ins.then_inc(S["tt_product"], 1)
                    yield
                pe.wait_ge(S["tt_ready"], LEVELS * v + LEVELS)
                pe.wait_ge(S["rhs_ready"], GH * v + GH)
                pe.wait_ge(S["pt_ready"], v + 1)
                for i in range(GH):
                    ins = pe.matmul(bank(3)[:, i, :], B[11][:, i, :], B[0][:, i, :], start=True, stop=True)
                ins.then_inc(S["vn_product"], 1)
                yield
                pe.wait_ge(S["vn_ready"], v + 1)
                for i in range(GH):
                    ins = pe.matmul(bank(0)[:, i, :], B[4][:, i, :], B[10][:, i, :], start=True, stop=True)
                ins.then_inc(S["o_product"], 1)
                yield
                for i in range(GH):
                    ins = pe.matmul(bank(1)[:, i, :], B[5][:, i, :], B[10][:, i, :], start=True, stop=True)
                ins.then_inc(S["ds_product"], 1)
                yield
                yield
                pe.wait_ge(S["o_scaled"], v + 1)
                for i in range(GH):
                    ins = pe.transpose(bank(2)[:, i, :], B[13][:, i, :], ident[:])
                ins.then_inc(S["o_turned"], 1)
                yield

            def gate_products(n):
                for u in range(BODY_CHUNKS // 4):
                    for c in range(4):
                        yield from chunk_products(G_GATES + BODY_CHUNKS * n + 4 * u + c, c, c, 4, hn_real,
                                                  lambda m: [PS[:, 6 + m, :]], "gate_done",
                                                  lambda m: pe.wait_ge(S["gate_freed"], FREE["gate_freed"] + 8 * n + 2 * u + m - 1))

            with pe.Fori(0, CH) as n:
                gates = gate_products(n)
                for hf in range(2):
                    steps_of_half = gdn_pe(n, hf)
                    for _ in range(STEPS):
                        for _ in range(PIECE):
                            next(gates, None)
                        next(steps_of_half)

            def p_banks_free(u, m):
                if m == 1:
                    pe.wait_ge(S["gate_freed"], FREE["gate_freed"] + 2 * N_GATES)
                pe.wait_ge(S["p_copied"], FREE["p_copied"] + 2 * u + m - 1)

            with pe.Fori(0, N_POOL) as u:
                for c in range(4):
                    run(chunk_products(G_P + 4 * u + c, c, c, 4, hn_halves,
                                       lambda m: [PS[:, 4 + 2 * m + i, 0:HALF] for i in range(2)], "p_done",
                                       lambda m: p_banks_free(u, m)))
            def z_unit(u):
                for c in range(4):
                    run(chunk_products(G_Z + 4 * u + c, c, c, 4, hn_real, lambda m: [PS[:, m, :]],
                                       "z_done", lambda m: pe.wait_ge(S["z_silu"], FREE["z_silu"] + 2 * u + m - 1)))

            pe.wait_ge(S["o_stored"], FREE["o_stored"] + 2 * CH)
            pe.wait_ge(S["state_ready"], 2 * CH + 1)
            with pe.Fori(0, N_Z - 1) as u:
                z_unit(u)
            pe.wait_ge(S["poolw_landed"], 16)
            pe.wait_ge(S["pooled_ready"], 1)
            for i in range(HEADS):
                g, m = i // 2, i % 2
                if i >= 6:
                    pe.wait_ge(S["zb_y"], i - 5)
                for k in range(2):
                    ins = pe.matmul(zb_bank(i), poolw[:, g, k, P * m:P * (m + 1)], pooled[:, 2 * g + k, :],
                                    start=k == 0, stop=k == 1)
                ins.then_inc(S["zb_done"], 1)
            z_unit(N_Z - 1)
            pe.wait_ge(S["zb_y"], HEADS)

            with pe.Fori(0, N_MERGE) as u:
                for c in range(2):
                    pe.wait_ge(S["z_lo"], FREE["z_lo"] + 2 * (N_Z - 1 + c))
                    run(chunk_products(G_MERGE + 4 * u + c, c, c, 2, lambda kt: ([o_hi[:, kt, :]], [o_lo[:, kt, :]]),
                                       lambda m: [PS[:, 4 + m, :]], "ya_done",
                                       lambda m: pe.wait_ge(S["ya_gated"], FREE["ya_gated"] + 2 * u + m - 1)))
                pe.wait_ge(S["zb_lo"], HEADS)
                for c in range(2):
                    run(chunk_products(G_MERGE + 4 * u + 2 + c, 2 + c, c, 2,
                                       lambda kt: ([zb_hi[:, kt, :]], [zb_lo[:, kt, :]]),
                                       lambda m: [PS[:, 6 + m, :]], "yb_done",
                                       lambda m: pe.wait_ge(S["yb_gated"], FREE["yb_gated"] + 2 * u + m - 1)))

            def merged_tile(kt, t):
                return mg_hi[:, kt, P * t:P * (t + 1)], mg_lo[:, kt, P * t:P * (t + 1)]

            with pe.Fori(0, N_OUT) as u:
                for c in range(8):
                    pe.wait_ge(S["merged_lo"], 2 * (N_MERGE - 1 + c // 7))
                    token_chunk(G_OUT + 8 * u + c, c, 2 * c, KT, merged_tile, 0, "out_done",
                                lambda t: pe.wait_ge(S["h1_ready"], FREE["h1_ready"] + TT * (u - 1) + t + 1))
            for t in range(TT):
                turn_quads(t + 5, hs[t % 2], P)
            pe.wait_ge(S["x_lo"], 4 * (2 * TT + 1))

            def hn_ffn(kt):
                return [hn_hi[:, kt, 0:SEQ]], [hn_lo[:, kt, 0:SEQ]]

            def gate_up(g, u, first=False):
                for sub in range(2):
                    r = 4 * u + 2 * sub

                    for c in range(4):
                        run(chunk_products(g + 8 * sub + c, c, c, 4, hn_ffn, lambda m: [PS[:, m, :]], "fg_done",
                                           lambda m: pe.wait_ge(S["silu_ready"], FREE["silu_ready"] + r + m - 1)))
                    for c in range(4):
                        run(chunk_products(g + 8 * sub + 4 + c, c, c, 4, hn_ffn, lambda m: [PS[:, 2 + m, :]],
                                           "fu_done", lambda m: pe.wait_ge(S["act_y"], FREE["act_y"] + r + m - 1)))

            def down(g, u, slot_a):
                pe.wait_ge(S["act_lo"], FREE["act_lo"] + 4 * u + 4)
                for blk in range(N_OUT):
                    for c in range(2):
                        token_chunk(g + 2 * blk + c, 2 * blk + c, 2 * c, 4,
                                    lambda k, t: (a_hi[:, slot_a, k, P * t:P * (t + 1)],
                                                  a_lo[:, slot_a, k, P * t:P * (t + 1)]),
                                    4, "down_done",
                                    lambda t: pe.wait_ge(S["h2_ready"], FREE["h2_ready"] + TT * (N_OUT * u + blk - 1) + t + 1))

            gate_up(G_FFN, 0)
            with pe.Fori(0, N_FFN // 2) as i:
                g = G_FFN + 16 + 48 * i
                gate_up(g, 2 * i + 1)
                down(g + 16, 2 * i, 0)
                gate_up(g + 24, 2 * i + 2)
                down(g + 40, 2 * i + 1, 1)
            down(G_END - 8, N_FFN - 1, 0)


_INS = ["x", "meta_tokens", "norm_mix_w", "w_in", "conv_w", "a_log", "dt_bias", "o_norm_w", "w_proj_a", "pool_w",
        "pool_scale", "w_proj_b", "w_out", "norm_ffn_w", "w_ffn_gate", "w_ffn_up", "w_ffn_down", "norm_final_w"]


def kernel(**inputs):
    import concourse.bacc as bacc
    from concourse.bass_utils import run_bass_kernel_spmd

    nc = bacc.Bacc("TRN2", target_bir_lowering=False, num_devices=1, dynamic_dma_scratch_size=1024)
    arrays, args = {}, []
    for name in _INS:
        a = np.ascontiguousarray(inputs[name])
        arrays[f"in_{name}"] = a
        args.append(nc.dram_tensor(f"in_{name}", a.shape, mybir.dt.from_np(a.dtype), kind="ExternalInput").ap())
    res = nc.dram_tensor("result", (1, SEQ, D), F32, kind="ExternalOutput").ap()
    hybrid_block(nc, *args, res)
    return run_bass_kernel_spmd(nc, [arrays], core_ids=[0]).results[0]["result"]
```

```python
from contextlib import ExitStack

import numpy as np

import concourse.bass as bass
from concourse import mybir
from concourse.alu_op_type import AluOpType as ALU

F32 = mybir.dt.float32
F32R = mybir.dt.float32r
ACT = mybir.ActivationFunctionType
AX = mybir.AxisListType

P = 128
META = 16
SEQ = 512
TOK = META + SEQ
HALF = TOK // 2
D = 2048
KT = D // P
HEADS = 8
QT, K_T, VT = 0, HEADS, 2 * HEADS
CONV = 4
POOL_GROUPS = 4
FFN = 5632
RMS_EPS = 1e-6
L2_EPS = 1e-6
NEG = -1e30

COL_Z = 3 * HEADS * P
COL_AB = COL_Z + HEADS * P
COL_P = COL_AB + 2 * HEADS
COL_GATES = COL_P + POOL_GROUPS * 2 * P

SLOTS = 4
CHUNK = 1024
UNIT = 256
BLOCK = 512

N_A = 3 * HEADS * P // UNIT
N_POOL = HEADS * P // UNIT
N_Z = HEADS * P // UNIT
N_GATES = 2 * D // UNIT
N_MERGE = D // UNIT
N_OUT = D // BLOCK
N_FFN = FFN // BLOCK
TT = SEQ // P

CH = SEQ // P
GH = 4
LEVELS = 7
META_LEVELS = 4
N_CONSTS = 17 + 3 * LEVELS
STEPS = 24
BODY_CHUNKS = N_GATES * 4 // CH
PIECE = 24 * BODY_CHUNKS // (2 * STEPS)

FREE = dict(a_copied=2, conv_done=2, qkv_ready=2, gate_freed=2, gates_stored=16, o_stored=1, p_copied=2,
            z_silu=2, z_y=2, z_lo=2, ya_gated=2, yb_gated=2, merged_sum=2, h1_ready=TT, h2_ready=TT,
            silu_ready=2, act_y=2, act_lo=2)

G_A = 0
G_GATES = G_A + N_A * 4
G_P = G_GATES + N_GATES * 4
G_Z = G_P + N_POOL * 4
G_MERGE = G_Z + N_Z * 4
G_OUT = G_MERGE + N_MERGE * 4
G_FFN = G_OUT + N_OUT * 8
G_END = G_FFN + N_FFN * 24

SEMAPHORES = """
rows_landed ab_landed small_landed poolw_landed scalew_landed
consts_built rows_turned vectors_ready vectors_more
x_squared x_rms_a x_rms x_diag x_turned x_weighted x_hi x_lo x_lo_v
h_squared h_summed
hi_ready lo_ready chunk_used
a_done a_copied conv_step conv_done qkv_ready
ab_hi ab_lo ab_meta ab_meta_copied ab_done logits_copied ab_vec ab_act
meta_staged meta_pe meta_vec meta_act meta_pool
staged qkv_turned gates_summed q_squared k_squared norms_a norms_summed norms_ready
sums_copied g_differenced g_masked decay_ready last_differenced decays_small nbeg_ready
q_scaled k_scaled vb_ready kd_ready qk_turned qn_ready kn_ready
kk_done kq_done nt_ready pt_ready level_masked s_products rhs_ready qs_ready
level_product level_x x_cleared t_product t_ready tt_product tt_ready
vn_product vn_ready o_product ds_product o_ready state_ready o_squared o_sum o_mean o_rms o_scaled
o_turned o_stored
gate_done gate_freed gates_stored
p_done p_copied window_step pooled_ready
z_done z_silu z_freed z_y z_hi z_lo
zb_done zb_y zb_hi zb_lo
ya_done yb_done ya_gated yb_gated merged_sum merged_hi merged_lo gate_a_landed gate_b_landed
out_done h1_ready xr_landed
fg_done fu_done silu_ready act_y act_hi act_lo down_done h2_ready
f_squared f_summed f_mean f_rms f_scaled out_stored
""".split()


def hybrid_block(nc, x, meta_tokens, norm_mix_w, w_in, conv_w, a_log, dt_bias, o_norm_w, w_proj_a, pool_w,
                 pool_scale, w_proj_b, w_out, norm_ffn_w, w_ffn_gate, w_ffn_up, w_ffn_down, norm_final_w, out):
    ctx = ExitStack()
    with ctx:
        S = {n: ctx.enter_context(nc.semaphore(n)) for n in SEMAPHORES}
        landed = [ctx.enter_context(nc.semaphore(f"weights_landed{i}")) for i in range(SLOTS)]
        x_landed = [ctx.enter_context(nc.semaphore(f"x_landed{i}")) for i in range(TT + 1)]
        gates_dram = nc.dram_tensor("gates_dram", [2 * D, SEQ], F32).ap()

        top = [(nc.sbuf_base + 63) // 64 * 64]

        def place(name, shape, dtype=F32, at=None):
            size = int(np.prod(shape[1:])) * 4
            offset = top[0] if at is None else at
            if at is None:
                top[0] += (size + 63) // 64 * 64
            return nc.alloc_sbuf_tensor_at(name, shape, dtype, offset=offset)

        raw = [place(f"w_raw{i}", [P, CHUNK]) for i in range(SLOTS)]
        whi = [place(f"w_hi{i}", [P, CHUNK], F32R) for i in range(SLOTS)]
        wlo = [place(f"w_lo{i}", [P, CHUNK], F32R) for i in range(SLOTS)]
        ident = place("ident", [P, P])
        upper = place("upper", [P, P])
        ones = place("ones", [P, P])
        cap = place("cap", [P, P])
        levels_at = top[0]
        levels = place("levels", [P, LEVELS, P])
        minus_half = place("minus_half", [P, 16])
        zero = minus_half[:, 12:16]
        vec_a = place("vec_a", [P, CONV * 3 * HEADS])
        vec_b = place("vec_b", [P, 2 * KT + HEADS + 1])
        nmix, nffn = vec_b[:, 0:KT], vec_b[:, KT:2 * KT]
        pscale, onorm = vec_b[:, 2 * KT:2 * KT + HEADS], vec_b[:, 2 * KT + HEADS:2 * KT + HEADS + 1]
        g_all = place("g_all", [P, CH + 1, HEADS])
        b_all = place("b_all", [P, CH + 1, HEADS])
        ssq = place("ssq", [P, 16])
        rms_a = place("rms_a", [P, 16])
        rms = place("rms", [P, 16])
        small = place("small", [P, 160])
        state_at = top[0]
        state = place("state", [P, HEADS, P])
        hn_at = top[0]
        hn_hi = place("hn_hi", [P, KT, TOK], F32R)
        hn_lo = place("hn_lo", [P, KT, TOK], F32R)
        qkv_at = top[0]
        qkv = place("qkv", [P, 3 * HEADS, TOK])
        kv_at = qkv_at + HEADS * TOK * 4
        v_at = kv_at + HEADS * TOK * 4
        tmp_at = top[0]
        B = [place(f"gdn{i}", [P, GH, P]) for i in range(14)]
        top[0] = tmp_at + 16 * SEQ * 4
        ext_at = top[0]
        gate_out = place("gate_out", [P, 2, SEQ])
        spare = place("spare", [P, 2, SEQ])

        XB = (B[3], B[13])
        xt = [place(f"xt{i}", [P, D], at=qkv_at + i * D * 4) for i in range(TT + 1)]
        x_junk = place("x_junk", [P, D], at=qkv_at + (TT + 1) * D * 4)
        rows_a = place("rows_a", [CONV * 3 * HEADS, P], at=qkv_at + (TT + 2) * D * 4)
        rows_b = place("rows_b", [2 * KT + HEADS + 1, P], at=qkv_at + (TT + 2) * D * 4 + 512)
        xy = [place(f"xy{i}", [P, 4, P], at=tmp_at + i * 2048) for i in range(4)]
        diag = [place(f"diag{i}", [P, P], at=ext_at + 4608 + 512 * i) for i in range(TT + 1)]
        conv_in = [place(f"conv_in{i}", [P, TOK + CONV - 1], at=tmp_at + 8192 + i * 2176) for i in range(2)]
        conv_acc = [place(f"conv_acc{i}", [P, TOK], at=tmp_at + 8192 + (2 + i) * 2176) for i in range(2)]
        ab_raw = place("ab_raw", [P, KT, 2 * HEADS], at=tmp_at + 17408)
        ab_h = place("ab_h", [P, KT, 2 * HEADS], F32R, at=tmp_at + 18432)
        ab_l = place("ab_l", [P, KT, 2 * HEADS], F32R, at=tmp_at + 19456)
        lg = place("lg", [P, CH + 1, 2 * HEADS], at=tmp_at + 20480)
        ab_t = [place(f"ab_t{i}", [P, CH + 1, HEADS], at=tmp_at + 20864 + 192 * i) for i in range(4)]
        alog_b = place("alog_b", [P, HEADS], at=tmp_at + 21760)
        dtb_b = place("dtb_b", [P, HEADS], at=tmp_at + 21824)
        meta_upper = place("meta_upper", [P, P], at=ext_at)
        meta_block = place("meta_block", [P, P], at=ext_at + 512)
        meta_neg = place("meta_neg", [P, P], at=ext_at + 1024)
        meta_sel = place("meta_sel", [P, HEADS], at=ext_at + 1536)
        meta_rep = place("meta_rep", [META, P], at=ext_at + 2048)
        meta_lg = place("meta_lg", [META, 2 * HEADS], at=ext_at + 2560)
        meta_u = place("meta_u", [P, HEADS, P], at=ext_at + 4096)
        o_hi = place("o_hi", [P, HEADS, SEQ], F32R, at=tmp_at)
        o_lo = place("o_lo", [P, HEADS, SEQ], F32R, at=tmp_at + HEADS * SEQ * 4)
        p_in = place("p_in", [P, HEADS, TOK], at=kv_at)
        pooled = place("pooled", [P, HEADS, SEQ], at=v_at)
        zt = place("zt", [P, 2, SEQ], at=ext_at)
        zy = place("zy", [P, 2, SEQ], at=ext_at + 4096)
        zb_hi = place("zb_hi", [P, HEADS, SEQ], F32R, at=kv_at)
        zb_lo = place("zb_lo", [P, HEADS, SEQ], F32R, at=v_at)
        poolw = place("poolw", [P, POOL_GROUPS, 2, UNIT])
        win = [place(f"win{i}", [P, TOK], at=at_) for i, at_ in enumerate((levels_at, state_at))]
        zb_y = [win[i][:, 0:SEQ] for i in range(2)]
        gate_a = place("gate_a", [P, 2, SEQ], at=qkv_at)
        gate_b = place("gate_b", [P, 2, SEQ], at=qkv_at + 4096)
        mg = place("mg", [P, 2, SEQ], at=qkv_at + 8192)
        mg_hi = place("mg_hi", [P, KT, SEQ], F32R, at=hn_at)
        mg_lo = place("mg_lo", [P, KT, SEQ], F32R, at=hn_at + KT * SEQ * 4)
        h = place("h", [P, TT, D], at=tmp_at)
        xr = place("xr", [P, TT, BLOCK], at=v_at)
        h_junk = place("h_junk", [P, D - BLOCK], at=qkv_at)
        hy = [place(f"hy{i}", [P, 4, P], at=kv_at + i * 2048) for i in range(4)]
        a_hi = place("a_hi", [P, 2, 4, SEQ], F32R, at=qkv_at)
        a_lo = place("a_lo", [P, 2, 4, SEQ], F32R, at=qkv_at + 16384)
        sg = place("sg", [P, 2, SEQ], at=qkv_at + 32768)
        ay = place("ay", [P, 2, SEQ], at=qkv_at + 32768 + 4096)
        ot = [place(f"ot{i}", [P, D], at=hn_at + i * 8192) for i in range(TT)]
        scalew = place("scalew", [P, D], at=hn_at + TT * 8192)
        f_junk = place("f_junk", [P, D // 2], at=hn_at + (TT + 1) * 8192)
        assert top[0] <= nc.sbuf_usable_end, (top[0], nc.sbuf_usable_end)

        PS = ctx.enter_context(nc.psum_tensor("psum", [P, 8, 512], F32))

        def bank(i, heads=GH):
            return PS[:, i, :].rearrange("p (h c) -> p h c", h=4)[:, 0:heads, :]

        def last_bank(t, b):
            return PS[:, (4 if b == 0 else 0) + t, :]

        def zb_bank(i):
            return PS[:, 2 + i % 6, :]

        def tile_of(b, i):
            return b[:, i, :] if isinstance(i, int) else b[:, bass.ds(i, 1), :].rearrange("p o t -> p (o t)")

        def x_tokens(u):
            return slice(0, META) if u == 0 else slice(META + P * (u - 1), META + P * u)

        def slot(g_static):
            return g_static % SLOTS

        gcur, bcur = (small[:, 0:8], small[:, 130:138]), (small[:, 8:16], small[:, 138:146])
        norm_s, norm_e, norm_r = small[:, 16:24], small[:, 24:32], small[:, 32:40]
        sums = small[:, 40:56]
        egc, egl, ged, nbeg = small[:, 56:60], small[:, 60:64], small[:, 64:68], small[:, 68:72]
        gld = small[:, 72:76]
        osum, omean, orms = small[:, 76:80], small[:, 80:84], small[:, 84:88]
        m_g, m_b, m_gs, m_ss, m_se, m_r = (small[:, 96 + i:97 + i] for i in range(6))
        m_sums, m_eg, m_nd, m_ed, m_sel8 = (small[:, 104:106], small[:, 106:107], small[:, 107:108],
                                            small[:, 108:109], small[:, 112:120])
        m_sel8b = small[:, 120:128]
        rms_s = small[:, 108:108 + TT]
        m_egl = small[:, 128:129]
        ssf = small[:, 96:96 + 3 * TT]

        def heads_of(v, width=P):
            return v.unsqueeze(2).broadcast_to([P, GH, width])

        def blocks_of(b, l, odd):
            return b.rearrange("p h (n two s) -> p h n two s", two=2, s=1 << l)[:, :, :, odd, :]

        def over_heads(m):
            return m.unsqueeze(1).broadcast_to([P, GH, P])

        w_in_v = w_in[0].rearrange("(k p) n -> p k n", p=P)
        pa_v = w_proj_a[0].rearrange("(k p) n -> p k n", p=P)
        pb_v = w_proj_b[0].rearrange("(k p) n -> p k n", p=P)
        wo_v = w_out[0].rearrange("(k p) n -> p k n", p=P)
        fg_v = w_ffn_gate[0].rearrange("(k p) n -> p k n", p=P)
        fu_v = w_ffn_up[0].rearrange("(k p) n -> p k n", p=P)
        fd_v = w_ffn_down[0].rearrange("(k p) n -> p k n", p=P)
        gates_v = gates_dram.rearrange("(k p) n -> p k n", p=P)
        x_v = x[0].rearrange("(t p) d -> p t d", p=P)
        out_v = out[0].rearrange("(t p) d -> p t d", p=P)

        def unit_tile(m, name, unit, last_chunk):
            return (S[name], unit + 1) if m == 0 else (S["chunk_used"], last_chunk + 1)

        def block_tile(t, name, unit, last_chunk):
            return (S[name], (TT - 1) * unit + t + 1) if t < TT - 1 else (S["chunk_used"], last_chunk + 1)

        block = ctx.enter_context(nc.Block())

        @block.sync
        def _(sp):
            def load_x(u, src, rows):
                sp.dma_start(xt[u][0:rows, :], src).then_inc(x_landed[u], 16)

            def load(g, g_static, src, k):
                if not (isinstance(g, int) and g < SLOTS):
                    sp.wait_ge(S["lo_ready"], g - (SLOTS - 1))
                s = slot(g_static)
                sp.dma_start(raw[s][:].rearrange("p (k n) -> p k n", k=k), src).then_inc(landed[s], 16)

            for name, count in FREE.items():
                sp.sem_inc(S[name], count)
            load_x(0, meta_tokens, META)
            load_x(1, x_v[:, 0, :], P)
            sp.dma_start(rows_a[:, :], conv_w[0].rearrange("j (m p) -> (j m) p", p=P)).then_inc(S["rows_landed"], 16)
            at = 0
            for v, n in ((norm_mix_w[0], KT), (norm_ffn_w[0], KT), (pool_scale[0], HEADS), (o_norm_w[0], 1)):
                sp.dma_start(rows_b[at:at + n, :], v.rearrange("(m p) -> m p", p=P)).then_inc(S["rows_landed"], 16)
                at += n
            for t in range(1, TT):
                load_x(t + 1, x_v[:, t, :], P)
            for c in range(4):
                load(c, c, w_in_v[:, 4 * c:4 * c + 4, 0:UNIT], 4)
            sp.dma_start(ab_raw[:, :, :], w_in_v[:, :, COL_AB:COL_AB + 2 * HEADS]).then_inc(S["ab_landed"], 16)
            sp.dma_start(alog_b[:, :], a_log[0].partition_broadcast(P)).then_inc(S["small_landed"], 16)
            sp.dma_start(dtb_b[:, :], dt_bias[0].partition_broadcast(P)).then_inc(S["small_landed"], 16)
            sp.dma_start(poolw[:, :, :, :], pool_w[0].rearrange("g (k p) d -> p g k d", p=P)).then_inc(S["poolw_landed"], 16)
            with sp.Fori(1, N_A) as u:
                for c in range(4):
                    load(G_A + 4 * u + c, c, w_in_v[:, 4 * c:4 * c + 4, bass.ds(UNIT * u, UNIT)], 4)
            with sp.Fori(0, N_GATES) as u:
                for c in range(4):
                    load(G_GATES + 4 * u + c, c, w_in_v[:, 4 * c:4 * c + 4, bass.ds(COL_GATES + UNIT * u, UNIT)], 4)
            with sp.Fori(0, N_POOL) as u:
                for c in range(4):
                    load(G_P + 4 * u + c, c, w_in_v[:, 4 * c:4 * c + 4, bass.ds(COL_P + UNIT * u, UNIT)], 4)
            with sp.Fori(0, N_Z) as u:
                for c in range(4):
                    load(G_Z + 4 * u + c, c, w_in_v[:, 4 * c:4 * c + 4, bass.ds(COL_Z + UNIT * u, UNIT)], 4)
            sp.wait_ge(S["gates_stored"], FREE["gates_stored"] + 16 * N_GATES)

            def merge_unit(u, first):
                for c in range(2):
                    load(G_MERGE + 4 * u + c, c, pa_v[:, 4 * c:4 * c + 4, bass.ds(UNIT * u, UNIT)], 4)
                for c in range(2):
                    load(G_MERGE + 4 * u + 2 + c, 2 + c, pb_v[:, 4 * c:4 * c + 4, bass.ds(UNIT * u, UNIT)], 4)
                if first:
                    sp.wait_ge(S["z_y"], FREE["z_y"] + 2 * N_Z)
                else:
                    sp.wait_ge(S["merged_sum"], FREE["merged_sum"] + 2 * u)
                sp.dma_start(gate_a[:, :, :], gates_v[:, bass.ds(2 * u, 2), :]).then_inc(S["gate_a_landed"], 16)
                sp.dma_start(gate_b[:, :, :], gates_v[:, bass.ds(KT + 2 * u, 2), :]).then_inc(S["gate_b_landed"], 16)

            merge_unit(0, True)
            with sp.Fori(1, N_MERGE) as u:
                merge_unit(u, False)

            def out_unit(u, first):
                for c in range(8):
                    load(G_OUT + 8 * u + c, c, wo_v[:, 2 * c:2 * c + 2, bass.ds(BLOCK * u, BLOCK)], 2)
                if first:
                    sp.wait_ge(S["chunk_used"], G_OUT)
                else:
                    sp.wait_ge(S["h1_ready"], FREE["h1_ready"] + TT * u)
                sp.dma_start(xr[:, :, :], x_v[:, :, bass.ds(BLOCK * u, BLOCK)]).then_inc(S["xr_landed"], 16)

            out_unit(0, True)
            with sp.Fori(1, N_OUT) as u:
                out_unit(u, False)

            def gate_up(g, u):
                for sub in range(2):
                    for i, v in enumerate((fg_v, fu_v)):
                        for c in range(4):
                            n = 8 * sub + 4 * i + c
                            load(g + n, n, v[:, 4 * c:4 * c + 4, bass.ds(BLOCK * u + UNIT * sub, UNIT)], 4)

            def down(g, u):
                for blk in range(N_OUT):
                    for c in range(2):
                        n = 2 * blk + c
                        load(g + n, n, fd_v[:, bass.ds(4 * u + 2 * c, 2), BLOCK * blk:BLOCK * (blk + 1)], 2)

            gate_up(G_FFN, 0)
            with sp.Fori(0, N_FFN // 2) as i:
                g = G_FFN + 16 + 48 * i
                gate_up(g, 2 * i + 1)
                down(g + 16, 2 * i)
                gate_up(g + 24, 2 * i + 2)
                down(g + 40, 2 * i + 1)
            down(G_END - 8, N_FFN - 1)
            sp.wait_ge(S["chunk_used"], G_END - 16)
            sp.dma_start(scalew[:, :], norm_final_w.partition_broadcast(P)).then_inc(S["scalew_landed"], 16)
            for t in range(TT):
                for i in range(2):
                    cols = slice(D // 2 * i, D // 2 * (i + 1))
                    sp.wait_ge(S["f_scaled"], 2 * t + i + 1)
                    sp.dma_start(out_v[:, t, cols], ot[t][:, cols]).then_inc(S["out_stored"], 16)
            sp.wait_ge(S["out_stored"], 16 * 2 * TT)

        @block.gpsimd
        def _(pool):
            built = [0]

            def const(ins):
                built[0] += 1
                ins.then_inc(S["consts_built"], 1)
                pool.wait_ge(S["consts_built"], built[0])

            const(pool.memset(ident[:], 0.0))
            const(pool.affine_select(out=ident[:], in_=ident[:], compare_op=ALU.not_equal, fill=1.0, base=0,
                                     pattern=[[-1, P]], channel_multiplier=1))
            const(pool.memset(minus_half[:], -0.5))
            const(pool.memset(zero, 0.0))

            def rms_of(u, rows, total, ready, count):
                pool.wait_ge(S[ready], count)
                pool.tensor_scalar(rms_a[0:rows, u:u + 1], total, 1.0 / D, RMS_EPS, ALU.mult, ALU.add) \
                    .then_inc(S["x_rms_a"], 1)
                pool.wait_ge(S["x_rms_a"], u + 1)
                pool.tensor_tensor(rms[0:rows, u:u + 1], rms_a[0:rows, u:u + 1], minus_half[0:rows, 0:1], ALU.pow) \
                    .then_inc(S["x_rms"], 1)

            def lo_quads(u, ybuf, cols, n):
                for q in range(2):
                    pool.wait_ge(S["x_hi"], 4 * u + q + 1)
                    pool.tensor_tensor(hn_lo[:, 4 * q:4 * q + 4, cols], ybuf[q][:, :, 0:n],
                                       hn_hi[:, 4 * q:4 * q + 4, cols].bitcast(F32), ALU.subtract) \
                        .then_inc(S["x_lo"], 1)

            def rms_of_x(u):
                rows = META if u == 0 else P
                rms_of(u, rows, ssq[0:rows, u:u + 1], "x_squared", u + 1)

            rms_of_x(0)
            rms_of_x(1)
            for u in range(TT + 1):
                if 2 <= u + 1 <= TT:
                    rms_of_x(u + 1)
                lo_quads(u, xy, x_tokens(u), META if u == 0 else P)

            const(pool.memset(ones[:], 1.0))
            const(pool.affine_select(out=upper[:], in_=ones[:], compare_op=ALU.is_ge, fill=0.0, base=0,
                                     pattern=[[1, P]], channel_multiplier=-1))
            const(pool.memset(cap[:], 0.0))
            const(pool.affine_select(out=cap[:], in_=cap[:], compare_op=ALU.is_ge, fill=NEG, base=0,
                                     pattern=[[1, P]], channel_multiplier=-1))
            const(pool.memset(levels[:], 0.0))
            for l in range(LEVELS):
                s = 1 << l
                n = P // (2 * s)
                m = levels[:, l, :].rearrange("p (n w) -> p n w", w=2 * s)
                const(pool.memset(m[:, :, s:2 * s], 1.0))
                const(pool.affine_select(out=m, in_=m, compare_op=ALU.is_ge, fill=0.0, base=0,
                                         pattern=[[-2 * s, n], [0, 2 * s]], channel_multiplier=1))
                const(pool.affine_select(out=m, in_=m, compare_op=ALU.is_ge, fill=0.0, base=s - 1,
                                         pattern=[[2 * s, n], [0, 2 * s]], channel_multiplier=-1))
            for dst, src, w in ((meta_upper[:], upper[:], META), (meta_block[:], ones[:], META),
                                (meta_sel[:], ones[:, 0:HEADS], 1)):
                dv, sv = (a.rearrange("p (n w) -> p n w", w=w) for a in (dst, src))
                const(pool.affine_select(out=dv, in_=sv, compare_op=ALU.is_ge, fill=0.0, base=0,
                                         pattern=[[-META, HEADS], [0, w]], channel_multiplier=1))
                const(pool.affine_select(out=dv, in_=dv, compare_op=ALU.is_ge, fill=0.0, base=META - 1,
                                         pattern=[[META, HEADS], [0, w]], channel_multiplier=-1))
            const(pool.tensor_copy(meta_rep[:].rearrange("p (h c) -> p h c", h=HEADS),
                                   ident[0:META, 0:META].unsqueeze(1).broadcast_to([META, HEADS, META])))
            const(pool.tensor_scalar(meta_neg[:], meta_upper[:], -1.0, -NEG, ALU.add, ALU.mult))

            pool.wait_ge(S["qkv_ready"], FREE["qkv_ready"] + 2 * N_A)
            pool.tensor_copy(B[1][:, 0, :].rearrange("p (h c) -> p h c", h=HEADS), qkv[:, K_T:K_T + HEADS, 0:META]) \
                .then_inc(S["meta_staged"], 1)
            pool.tensor_copy(B[2][:, 0, :].rearrange("p (h c) -> p h c", h=HEADS), qkv[:, VT:VT + HEADS, 0:META]) \
                .then_inc(S["meta_staged"], 1)
            pool.wait_ge(S["meta_vec"], 4)
            pool.tensor_tensor(m_r, m_se, minus_half[:, 0:1], ALU.pow).then_inc(S["meta_pool"], 1)
            pool.wait_ge(S["meta_vec"], 12)
            for l in range(META_LEVELS):
                pool.tensor_tensor(B[4][:, l, :], B[11][:, 0, :], levels[:, l, :], ALU.mult) \
                    .then_inc(S["meta_pool"], 1)

            def stage(n, hf):
                h0 = GH * hf
                v = 2 * n + hf
                tok = bass.ds(META + P * n, P) if not isinstance(n, int) else slice(META + P * n, META + P * (n + 1))
                row = bass.ds(n + 1, 1) if not isinstance(n, int) else slice(n + 1, n + 2)
                if not (isinstance(n, int) and v == 0):
                    pool.wait_ge(S["s_products"], 2 * v)
                    pool.wait_ge(S["rhs_ready"], GH * v)
                for b, t0 in ((7, QT), (8, K_T), (6, VT)):
                    pool.tensor_copy(B[b][:], qkv[:, t0 + h0:t0 + h0 + GH, tok]).then_inc(S["staged"], 1)
                pool.tensor_copy(gcur[hf], g_all[:, row, :].rearrange("p o h -> p (o h)")).then_inc(S["staged"], 1)
                pool.tensor_copy(bcur[hf], b_all[:, row, :].rearrange("p o h -> p (o h)")).then_inc(S["staged"], 1)

            def gdn_pool(n, hf, following):
                v = 2 * n + hf
                pool.wait_ge(S["norms_summed"], 2 * v + 2)
                pool.tensor_tensor(norm_r, norm_e, minus_half[:, 0:8], ALU.pow).then_inc(S["norms_ready"], 1)
                pool.wait_ge(S["g_differenced"], v + 1)
                pool.tensor_tensor(B[9][:], B[9][:], over_heads(cap[:]), ALU.add).then_inc(S["g_masked"], 1)
                pool.wait_ge(S["decays_small"], 3 * v + 3)
                pool.wait_ge(S["k_scaled"], v + 1)
                pool.tensor_tensor(B[5][:], B[4][:], heads_of(ged), ALU.mult).then_inc(S["kd_ready"], 1)
                pool.wait_ge(S["nt_ready"], v + 1)
                for l in range(LEVELS):
                    if l >= 2:
                        pool.wait_ge(S["level_product"], LEVELS * v + l - 1)
                    pool.tensor_tensor(B[1 + l % 2][:], B[10][:], over_heads(levels[:, l, :]), ALU.mult) \
                        .then_inc(S["level_masked"], 1)
                    if l >= 1:
                        if l >= 2:
                            pool.wait_ge(S["tt_product"], LEVELS * v + l - 1)
                        dead = blocks_of(XB[l % 2][:], l, 1)
                        if l == 2:
                            pool.wait_ge(S["t_ready"], (LEVELS - 1) * v + 1)
                        nothing = zero.unsqueeze(2).unsqueeze(3).broadcast_to(dead.shape)
                        pool.tensor_tensor(dead, nothing, nothing, ALU.mult).then_inc(S["x_cleared"], 1)
                    if l == 3 and following is not None:
                        stage(*following)
                pool.wait_ge(S["o_mean"], v + 1)
                pool.tensor_tensor(orms, omean, minus_half[:, 0:GH], ALU.pow).then_inc(S["o_rms"], 1)

            pool.wait_ge(S["state_ready"], 1)
            stage(0, 0)
            with pool.Fori(0, CH - 1) as n:
                gdn_pool(n, 0, (n, 1))
                gdn_pool(n, 1, (n + 1, 0))
            gdn_pool(CH - 1, 0, (CH - 1, 1))
            gdn_pool(CH - 1, 1, None)
            pool.wait_ge(S["state_ready"], 2 * CH + 1)

            step = [0]

            def chained(ins):
                step[0] += 1
                ins.then_inc(S["window_step"], 1)
                pool.wait_ge(S["window_step"], step[0])

            for i in range(HEADS):
                pool.wait_ge(S["p_copied"], FREE["p_copied"] + i + 1)
                g = i // 2
                src = p_in[:, i, :]
                for l in range(g + 1):
                    s = 1 << l
                    dst = win[l % 2]
                    chained(pool.tensor_tensor(dst[:, 2 * s - 1:TOK], src[:, 2 * s - 1:TOK], src[:, s - 1:TOK - s],
                                               ALU.add))
                    src = dst
                mean = win[(g + 1) % 2]
                chained(pool.tensor_scalar(mean[:, META:TOK], src[:, META:TOK], 1.0 / (2 << g), None, ALU.mult))
                chained(pool.tensor_tensor(pooled[:, i, :], mean[:, META:TOK], p_in[:, i, META:TOK], ALU.subtract))
            pool.memset(minus_half[:, 8:9], -0.5).then_inc(S["pooled_ready"], 1)

            with pool.Fori(0, N_MERGE) as u:
                for m in range(2):
                    pool.wait_ge(S["yb_gated"], FREE["yb_gated"] + 2 * u + m + 1)
                    pool.tensor_tensor(mg[:, m, :], gate_a[:, m, :], gate_b[:, m, :], ALU.add).then_inc(S["merged_sum"], 1)

            for t in range(TT):
                if t == 0:
                    rms_of(TT + 1, P, rms_a[:, TT + 1:TT + 2], "h_summed", 1)
                if t + 1 < TT:
                    rms_of(TT + 2 + t, P, rms_a[:, TT + 2 + t:TT + 3 + t], "h_summed", t + 2)
                lo_quads(TT + 1 + t, hy, slice(P * t, P * (t + 1)), P)

            for t in range(TT):
                pool.wait_ge(S["f_mean"], t + 1)
                pool.tensor_tensor(rms[:, 9 + t:10 + t], rms_a[:, 9 + t:10 + t], minus_half[:, 0:1], ALU.pow) \
                    .then_inc(S["f_rms"], 1)

        @block.scalar
        def _(act):
            def split(g, g_static):
                s = slot(g_static)
                if isinstance(g, int):
                    act.wait_ge(landed[s], 16 * (g // SLOTS + 1))
                    if g >= SLOTS:
                        act.wait_ge(S["chunk_used"], g - (SLOTS - 1))
                else:
                    act.wait_ge(landed[s], 4 * (g - g_static % SLOTS) + 16)
                    act.wait_ge(S["chunk_used"], g - (SLOTS - 1))
                act.activation(whi[s][:], raw[s][:], ACT.Copy).then_inc(S["hi_ready"], 1)

            def square_tile(u):
                rows = META if u == 0 else P
                act.wait_ge(x_landed[u], 16)
                if u > 0:
                    act.wait_ge(S["x_squared"], u)
                act.activation(x_junk[0:rows, :], xt[u][0:rows, :], ACT.Square, accum_out=ssq[0:rows, u:u + 1]) \
                    .then_inc(S["x_squared"], 1)

            def hi_quads(u, ybuf, cols, n):
                for q in range(4):
                    act.wait_ge(S["x_weighted"], 4 * u + q + 1)
                    act.activation(hn_hi[:, 4 * q:4 * q + 4, cols], ybuf[q][:, :, 0:n], ACT.Copy).then_inc(S["x_hi"], 1)

            square_tile(0)
            square_tile(1)
            act.wait_ge(S["rows_turned"], 1)
            act.activation(vec_a[:], PS[:, 0, 0:CONV * 3 * HEADS], ACT.Copy).then_inc(S["vectors_ready"], 1)
            act.activation(vec_b[:], PS[:, 1, 0:2 * KT + HEADS + 1], ACT.Copy).then_inc(S["vectors_ready"], 1)
            for u in range(TT + 1):
                if 2 <= u + 1 <= TT:
                    square_tile(u + 1)
                hi_quads(u, xy, x_tokens(u), META if u == 0 else P)
                if u >= 2:
                    split(u - 2, u - 2)
            split(SLOTS - 1, SLOTS - 1)

            with act.Fori(0, N_A) as u:
                for c in range(4):
                    if c == 3:
                        for m in range(2):
                            act.wait_ge(*unit_tile(m, "a_done", u, G_A + 4 * u + 3))
                            act.wait_ge(S["conv_done"], FREE["conv_done"] + 2 * u + m - 1)
                            act.activation(conv_in[m][:, CONV - 1:CONV - 1 + TOK].rearrange("p (a b) -> p a b", a=2),
                                           PS[:, 2 * m:2 * m + 2, 0:HALF], ACT.Copy).then_inc(S["a_copied"], 1)
                    split(G_A + 4 * u + c + 4, c)
                for m in range(2):
                    act.wait_ge(S["conv_done"], FREE["conv_done"] + 2 * u + m + 1)
                    act.activation(qkv[:, bass.ds(2 * u + m, 1), :].rearrange("p o t -> p (o t)"), conv_acc[m][:],
                                   ACT.Silu).then_inc(S["qkv_ready"], 1)

            act.wait_ge(S["ab_landed"], 16)
            act.activation(ab_h[:], ab_raw[:], ACT.Copy).then_inc(S["ab_hi"], 1)
            act.wait_ge(S["logits_copied"], 1)
            act.activation(b_all[:], lg[:, :, 0:HEADS], ACT.Sigmoid).then_inc(S["ab_act"], 1)
            act.wait_ge(S["small_landed"], 32)
            act.activation(alog_b[:], alog_b[:], ACT.Exp).then_inc(S["ab_act"], 1)
            act.wait_ge(S["ab_vec"], 2)
            act.activation(ab_t[1][:], ab_t[1][:], ACT.Exp).then_inc(S["ab_act"], 1)
            act.wait_ge(S["ab_act"], 3)
            act.activation(ab_t[2][:], ab_t[1][:], ACT.Ln, bias=1.0).then_inc(S["ab_act"], 1)

            act.wait_ge(S["meta_pe"], 1)
            act.activation(B[12][:, 0, :], PS[:, 1, 0:P], ACT.Square).then_inc(S["meta_act"], 1)
            act.wait_ge(S["meta_vec"], 8)
            act.activation(m_eg, m_sums[:, 0:1], ACT.Exp).then_inc(S["meta_act"], 1)
            act.activation(m_ed, m_nd, ACT.Exp).then_inc(S["meta_act"], 1)
            act.activation(B[9][:, 0, :], B[9][:, 0, :], ACT.Exp).then_inc(S["meta_act"], 1)
            act.wait_ge(S["meta_pe"], 3)
            act.activation(B[8][:, 0, :], PS[:, 1, 0:P], ACT.Copy).then_inc(S["meta_act"], 1)
            act.wait_ge(S["meta_pe"], META_LEVELS * 3 + 5)
            for i in range(2):
                act.activation(state[:, 4 * i:4 * i + 4, :], bank(2 + i), ACT.Copy).then_inc(S["meta_act"], 1)

            def gdn_act(n, hf):
                v = 2 * n + hf
                h0 = GH * hf
                act.wait_ge(S["qkv_turned"], 3 * v + 1)
                act.activation(B[12][:], bank(0), ACT.Square).then_inc(S["q_squared"], 1)
                act.wait_ge(S["qkv_turned"], 3 * v + 2)
                act.activation(B[13][:], bank(1), ACT.Square).then_inc(S["k_squared"], 1)
                yield
                act.wait_ge(S["sums_copied"], v + 1)
                act.activation(egc, sums[:, h0:h0 + GH], ACT.Exp).then_inc(S["decays_small"], 1)
                act.activation(egl, sums[:, 8 + h0:8 + h0 + GH], ACT.Exp).then_inc(S["decays_small"], 1)
                act.wait_ge(S["last_differenced"], v + 1)
                act.activation(ged, gld, ACT.Exp).then_inc(S["decays_small"], 1)
                act.wait_ge(S["g_masked"], v + 1)
                act.activation(B[9][:], B[9][:], ACT.Exp).then_inc(S["decay_ready"], 1)
                yield
                act.wait_ge(S["qk_turned"], 2 * v + 1)
                act.activation(B[7][:], bank(0), ACT.Copy).then_inc(S["qn_ready"], 1)
                act.wait_ge(S["qk_turned"], 2 * v + 2)
                act.activation(B[8][:], bank(1), ACT.Copy).then_inc(S["kn_ready"], 1)
                yield
                yield
                act.wait_ge(S["s_products"], 2 * v + 2)
                act.wait_ge(S["decays_small"], 3 * v + 3)
                for b in range(GH):
                    act.activation(B[12][:, b, :], PS[:, 5, P * b:P * (b + 1)], ACT.Copy, scale=egc[:, b:b + 1]) \
                        .then_inc(S["qs_ready"], 1)
                for _ in range(15):
                    yield
                act.wait_ge(S["vn_product"], v + 1)
                act.activation(B[10][:], bank(3), ACT.Copy).then_inc(S["vn_ready"], 1)
                yield
                act.wait_ge(S["o_ready"], v + 1)
                act.activation(B[13][:], B[12][:], ACT.Square).then_inc(S["o_squared"], 1)
                yield
                yield
                yield
                act.wait_ge(S["o_turned"], v + 1)
                act.activation(qkv[:, h0:h0 + GH, bass.ds(META + P * n, P)], bank(2), ACT.Copy).then_inc(S["o_stored"], 1)
                yield

            def gate_unit(n, u):
                r = 4 * n + u
                act.wait_ge(S["gates_stored"], FREE["gates_stored"] + 16 * r)
                for m in range(2):
                    act.wait_ge(*unit_tile(m, "gate_done", r, G_GATES + 4 * r + 3))
                    act.activation(gate_out[:, m, :], PS[:, 6 + m, :], ACT.Tanh, scale=0.5).then_inc(S["gate_freed"], 1)
                act.wait_ge(S["gate_freed"], FREE["gate_freed"] + 2 * r + 2)
                act.dma_start(gates_v[:, bass.ds(2 * r, 2), :], gate_out[:, :, :]).then_inc(S["gates_stored"], 16)

            with act.Fori(0, CH) as n:
                k = 0
                for hf in range(2):
                    steps_of_half = gdn_act(n, hf)
                    for _ in range(STEPS):
                        if k % 12 == 11:
                            gate_unit(n, k // 12)
                        next(steps_of_half)
                        if k % 3 == 2:
                            c = (k + 10) // 3
                            split(G_GATES + BODY_CHUNKS * n + c, c)
                        k += 1

            with act.Fori(0, N_POOL) as u:
                for c in range(4):
                    if c == 3:
                        for m in range(2):
                            act.wait_ge(*unit_tile(m, "p_done", u, G_P + 4 * u + 3))
                            act.activation(p_in[:, bass.ds(2 * u + m, 1), :].rearrange("p o (a b) -> p (o a) b", a=2),
                                           PS[:, 4 + 2 * m:6 + 2 * m, 0:HALF], ACT.Copy).then_inc(S["p_copied"], 1)
                    split(G_P + 4 * u + c + 4, c)

            act.wait_ge(S["gates_stored"], FREE["gates_stored"] + 16 * N_GATES)
            def z_unit(u, beside):
                for c in range(4):
                    beside(c)
                    if c == 3:
                        for m in range(2):
                            act.wait_ge(*unit_tile(m, "z_done", u, G_Z + 4 * u + 3))
                            act.wait_ge(S["z_y"], FREE["z_y"] + 2 * u + m - 1)
                            act.activation(zt[:, m, :], PS[:, m, :], ACT.Silu).then_inc(S["z_silu"], 1)
                        for m in range(2):
                            act.wait_ge(S["z_y"], FREE["z_y"] + 2 * u + m + 1)
                            act.activation(tile_of(o_hi, 2 * u + m), zy[:, m, :], ACT.Copy).then_inc(S["z_hi"], 1)
                    split(G_Z + 4 * u + c + 4, c)

            def zb_tiles(c):
                for i in range(2 * c, 2 * c + 2):
                    act.wait_ge(S["zb_y"], i + 1)
                    act.activation(zb_hi[:, i, :], zb_y[i % 2], ACT.Copy).then_inc(S["zb_hi"], 1)

            with act.Fori(0, N_Z - 1) as u:
                z_unit(u, lambda c: None)
            z_unit(N_Z - 1, zb_tiles)

            with act.Fori(0, N_MERGE) as u:
                for c in range(4):
                    if c == 3:
                        for m in range(2):
                            act.wait_ge(S["merged_sum"], FREE["merged_sum"] + 2 * u + m + 1)
                            act.activation(mg_hi[:, bass.ds(2 * u + m, 1), :].rearrange("p o t -> p (o t)"),
                                           mg[:, m, :], ACT.Copy, scale=0.5).then_inc(S["merged_hi"], 1)
                    split(G_MERGE + 4 * u + c + 4, c)

            with act.Fori(0, N_OUT - 1) as u:
                for c in range(8):
                    split(G_OUT + 8 * u + c + 4, c)

            def square_h(n, t, cols):
                act.wait_ge(S["h1_ready"], FREE["h1_ready"] + TT * (cols.stop // BLOCK - 1) + t + 1)
                if n > 0:
                    act.wait_ge(S["h_squared"], n)
                i = 5 + 2 * t + (n >= TT)
                act.activation(h_junk[:, 0:cols.stop - cols.start], h[:, t, cols], ACT.Square,
                               accum_out=ssq[:, i:i + 1]).then_inc(S["h_squared"], 1)

            for c in range(8):
                if c < TT:
                    square_h(c, c, slice(0, D - BLOCK))
                if c == 7:
                    for t in range(TT):
                        square_h(TT + t, t, slice(D - BLOCK, D))
                split(G_OUT + 8 * (N_OUT - 1) + c + 4, c)

            for t in range(TT):
                hi_quads(TT + 1 + t, hy, slice(P * t, P * (t + 1)), P)

            def gate_up(g, u, slot_a, splits=16):
                for sub in range(2):
                    for c in range(8):
                        if c == 3:
                            for m in range(2):
                                r = 4 * u + 2 * sub + m
                                act.wait_ge(*unit_tile(m, "fg_done", 2 * u + sub, g + 8 * sub + 3))
                                act.wait_ge(S["act_y"], FREE["act_y"] + r - 1)
                                act.activation(sg[:, m, :], PS[:, m, :], ACT.Silu).then_inc(S["silu_ready"], 1)
                        if c == 7:
                            for m in range(2):
                                r = 4 * u + 2 * sub + m
                                act.wait_ge(S["act_y"], FREE["act_y"] + r + 1)
                                act.activation(a_hi[:, slot_a, 2 * sub + m, :], ay[:, m, :], ACT.Copy) \
                                    .then_inc(S["act_hi"], 1)
                        split(g + 8 * sub + c + 4, c)

            def down(g):
                for c in range(8):
                    split(g + c + 4, c)

            gate_up(G_FFN, 0, 0)
            with act.Fori(0, N_FFN // 2) as i:
                g = G_FFN + 16 + 48 * i
                gate_up(g, 2 * i + 1, 1)
                down(g + 16)
                gate_up(g + 24, 2 * i + 2, 0)
                down(g + 40)
            for c in range(4):
                split(G_END - 4 + c, c)
            done = TT * (N_OUT * N_FFN - 2)
            pieces = [(done - TT + t + 1, t, 0, D // 2) for t in range(TT)]
            for t in range(TT):
                pieces += [(done + 2 * t + b + 1, t, 1 + b, BLOCK) for b in range(2)]
            for n, (count, t, part, width) in enumerate(pieces):
                act.wait_ge(S["h2_ready"], FREE["h2_ready"] + count)
                if n > 0:
                    act.wait_ge(S["f_squared"], n)
                first = 0 if part == 0 else D // 2 + BLOCK * (part - 1)
                act.activation(f_junk[:, 0:width], h[:, t, first:first + width], ACT.Square,
                               accum_out=ssf[:, 3 * t + part:3 * t + part + 1]).then_inc(S["f_squared"], 1)

        @block.vector
        def _(dve):
            def split(g, g_static):
                s = slot(g_static)
                dve.wait_ge(S["hi_ready"], g + 1)
                dve.tensor_tensor(wlo[s][:], raw[s][:], whi[s][:].bitcast(F32), ALU.subtract).then_inc(S["lo_ready"], 1)

            def diagonal(u, rows=P):
                dve.wait_ge(S["x_rms"], u + 1)
                dve.tensor_scalar(diag[u % (TT + 1)][0:rows, 0:rows], ident[0:rows, 0:rows], rms[0:rows, u:u + 1], None,
                                  ALU.mult).then_inc(S["x_diag"], 1)

            def weight_quads(u, ybuf, w, cols, n):
                for q in range(4):
                    dve.wait_ge(S["x_turned"], 4 * u + q + 1)
                    if u not in (0, TT + 1):
                        dve.wait_ge(S["x_lo" if q < 2 else "x_lo_v"], 2 * (u - 1) + q % 2 + 1)
                    dve.tensor_tensor(ybuf[q][:, :, 0:n], bank(4 + q)[:, :, 0:n],
                                      w[:, 4 * q:4 * q + 4].unsqueeze(2).broadcast_to([P, 4, n]), ALU.mult) \
                        .then_inc(S["x_weighted"], 1)
                for q in range(2, 4):
                    dve.wait_ge(S["x_hi"], 4 * u + q + 1)
                    dve.tensor_tensor(hn_lo[:, 4 * q:4 * q + 4, cols], ybuf[q][:, :, 0:n],
                                      hn_hi[:, 4 * q:4 * q + 4, cols].bitcast(F32), ALU.subtract) \
                        .then_inc(S["x_lo_v"], 1)

            for m in range(2):
                dve.memset(conv_in[m][:, 0:CONV - 1], 0.0).then_inc(S["vectors_more"], 1)
            diagonal(0, META)
            diagonal(1)
            dve.wait_ge(S["vectors_ready"], 2)
            for u in range(TT + 1):
                if 2 <= u + 1 <= TT:
                    diagonal(u + 1)
                weight_quads(u, xy, nmix, x_tokens(u), META if u == 0 else P)
                if u >= 2:
                    split(u - 2, u - 2)
            split(SLOTS - 1, SLOTS - 1)

            dve.wait_ge(S["vectors_more"], 2)
            with dve.Fori(0, N_A) as u:
                for c in range(4):
                    if c == 3:
                        for m in range(2):
                            dve.wait_ge(S["a_copied"], FREE["a_copied"] + 2 * u + m + 1)
                            dve.wait_ge(S["qkv_ready"], FREE["qkv_ready"] + 2 * u + m - 1)
                            r = 2 * u + m
                            for j in range(CONV):
                                tap = vec_a[:, bass.ds(3 * HEADS * j + r, 1)]
                                src = conv_in[m][:, j:j + TOK]
                                if j == 0:
                                    ins = dve.tensor_scalar(conv_acc[m][:], src, tap, None, ALU.mult)
                                else:
                                    dve.wait_ge(S["conv_step"], 3 * r + j)
                                    ins = dve.scalar_tensor_tensor(conv_acc[m][:], src, tap, conv_acc[m][:],
                                                                   ALU.mult, ALU.add)
                                ins.then_inc(S["conv_done"] if j == CONV - 1 else S["conv_step"], 1)
                    split(G_A + 4 * u + c + 4, c)

            dve.wait_ge(S["ab_hi"], 1)
            dve.tensor_tensor(ab_l[:], ab_raw[:], ab_h[:].bitcast(F32), ALU.subtract).then_inc(S["ab_lo"], 1)
            dve.wait_ge(S["ab_meta"], 1)
            dve.tensor_copy(meta_lg[:], PS[0:META, 5, 0:2 * HEADS]).then_inc(S["ab_meta_copied"], 1)
            dve.wait_ge(S["ab_done"], 1)
            dve.tensor_copy(lg[:], PS[:, 4, 0:(CH + 1) * 2 * HEADS].rearrange("p (t c) -> p t c", c=2 * HEADS)) \
                .then_inc(S["logits_copied"], 1)
            dve.wait_ge(S["logits_copied"], 1)
            dve.wait_ge(S["small_landed"], 32)
            bc5 = [P, CH + 1, HEADS]
            dve.tensor_tensor(ab_t[0][:], lg[:, :, HEADS:], dtb_b[:].unsqueeze(1).broadcast_to(bc5), ALU.add) \
                .then_inc(S["ab_vec"], 1)
            dve.wait_ge(S["ab_vec"], 1)
            dve.scalar_tensor_tensor(ab_t[1][:], ab_t[0][:], -1.0, ab_t[0][:], ALU.mult, ALU.min) \
                .then_inc(S["ab_vec"], 1)
            dve.wait_ge(S["ab_act"], 4)
            dve.scalar_tensor_tensor(ab_t[3][:], ab_t[0][:], 0.0, ab_t[2][:], ALU.max, ALU.add).then_inc(S["ab_vec"], 1)
            dve.wait_ge(S["ab_vec"], 3)
            dve.scalar_tensor_tensor(g_all[:], ab_t[3][:], -1.0, alog_b[:].unsqueeze(1).broadcast_to(bc5),
                                     ALU.mult, ALU.mult).then_inc(S["ab_vec"], 1)

            steps = [0]

            def meta(ins):
                steps[0] += 1
                ins.then_inc(S["meta_vec"], 1)
                dve.wait_ge(S["meta_vec"], steps[0])

            dve.wait_ge(S["consts_built"], N_CONSTS)
            dve.wait_ge(S["ab_vec"], 4)
            meta(dve.tensor_tensor(m_sel8, g_all[:, 0, :], meta_sel[:], ALU.mult))
            meta(dve.tensor_reduce(m_g, m_sel8, AX.X, ALU.add))
            dve.wait_ge(S["meta_act"], 1)
            meta(dve.tensor_reduce(m_ss, B[12][:, 0, :], AX.X, ALU.add))
            meta(dve.tensor_scalar(m_se, m_ss, L2_EPS, None, ALU.add))
            dve.wait_ge(S["meta_pe"], 2)
            meta(dve.tensor_copy(m_sums, PS[:, 4, 0:2]))
            meta(dve.scalar_tensor_tensor(B[9][:, 0, :], PS[:, 3, 0:P], m_sums[:, 0:1], meta_upper[:],
                                          ALU.subtract, ALU.mult))
            meta(dve.tensor_tensor(B[9][:, 0, :], B[9][:, 0, :], meta_neg[:], ALU.add))
            meta(dve.tensor_tensor(m_nd, m_sums[:, 1:2], m_sums[:, 0:1], ALU.subtract))
            meta(dve.tensor_tensor(m_sel8b, b_all[:, 0, :], meta_sel[:], ALU.mult))
            meta(dve.tensor_reduce(m_b, m_sel8b, AX.X, ALU.add))
            dve.wait_ge(S["meta_pool"], 1)
            meta(dve.tensor_scalar(B[3][:, 0, :], PS[:, 1, 0:P], m_r, None, ALU.mult))
            dve.wait_ge(S["meta_pe"], 4)
            dve.wait_ge(S["meta_act"], 4)
            meta(dve.tensor_tensor(B[11][:, 0, :], PS[:, 0, 0:P], B[9][:, 0, :], ALU.mult))
            meta(dve.tensor_scalar(B[5][:, 0, :], B[3][:, 0, :], m_ed, None, ALU.mult))
            meta(dve.tensor_scalar(B[6][:, 0, :], PS[:, 2, 0:P], m_b, None, ALU.mult))
            xb, tb, ttb = B[7][:, 0, :], B[10][:, 0, :], B[0][:, 0, :]
            dve.wait_ge(S["meta_pe"], 5)
            meta(dve.tensor_scalar(xb, PS[:, 0, 0:P], m_b, None, ALU.mult))
            meta(dve.tensor_tensor(tb, ident[:], xb, ALU.subtract))
            dve.wait_ge(S["meta_pe"], 6)
            meta(dve.tensor_tensor(ttb, ident[:], PS[:, 1, 0:P], ALU.subtract))
            for l in range(1, META_LEVELS):
                dve.wait_ge(S["meta_pe"], 3 * l + 4)
                meta(dve.tensor_scalar(xb, PS[:, 0, 0:P], m_b, None, ALU.mult))
                dve.wait_ge(S["meta_pe"], 3 * l + 6)
                meta(dve.tensor_tensor(tb, tb, PS[:, 2, 0:P], ALU.subtract))
                meta(dve.tensor_tensor(ttb, ttb, PS[:, 1, 0:P], ALU.subtract))
            dve.wait_ge(S["meta_pe"], 3 * META_LEVELS + 4)
            meta(dve.tensor_tensor(meta_u[:], PS[:, 0, 0:P].unsqueeze(1).broadcast_to([P, HEADS, P]),
                                   meta_sel[:].unsqueeze(2).broadcast_to([P, HEADS, P]), ALU.mult))
            dve.wait_ge(S["meta_act"], 7)
            dve.memset(m_sel8b, 0.0).then_inc(S["state_ready"], 1)

            def gdn_dve(n, hf):
                v = 2 * n + hf
                h0 = GH * hf
                bh = bcur[hf][:, h0:h0 + GH]
                dve.wait_ge(S["q_squared"], v + 1)
                dve.tensor_reduce(norm_s[:, 0:GH], B[12][:], AX.X, ALU.add).then_inc(S["norms_a"], 1)
                dve.wait_ge(S["k_squared"], v + 1)
                dve.tensor_reduce(norm_s[:, GH:], B[13][:], AX.X, ALU.add).then_inc(S["norms_a"], 1)
                dve.wait_ge(S["norms_a"], 2 * v + 2)
                dve.tensor_scalar(norm_e[:, 0:GH], norm_s[:, 0:GH], L2_EPS, float(P), ALU.add, ALU.mult) \
                    .then_inc(S["norms_summed"], 1)
                dve.tensor_scalar(norm_e[:, GH:], norm_s[:, GH:], L2_EPS, None, ALU.add).then_inc(S["norms_summed"], 1)
                yield
                dve.wait_ge(S["gates_summed"], v + 1)
                dve.tensor_copy(sums, PS[:, 4, 0:16]).then_inc(S["sums_copied"], 1)
                dve.wait_ge(S["sums_copied"], v + 1)
                dve.tensor_tensor(B[9][:], bank(3), heads_of(sums[:, h0:h0 + GH]), ALU.subtract) \
                    .then_inc(S["g_differenced"], 1)
                dve.tensor_tensor(gld, sums[:, 8 + h0:8 + h0 + GH], sums[:, h0:h0 + GH], ALU.subtract) \
                    .then_inc(S["last_differenced"], 1)
                dve.wait_ge(S["norms_ready"], v + 1)
                dve.tensor_tensor(B[3][:], bank(0), heads_of(norm_r[:, 0:GH]), ALU.mult).then_inc(S["q_scaled"], 1)
                dve.tensor_tensor(B[4][:], bank(1), heads_of(norm_r[:, GH:]), ALU.mult).then_inc(S["k_scaled"], 1)
                dve.wait_ge(S["qkv_turned"], 3 * v + 3)
                dve.tensor_tensor(B[6][:], bank(2), heads_of(bh), ALU.mult).then_inc(S["vb_ready"], 1)
                dve.wait_ge(S["decays_small"], 3 * v + 3)
                dve.scalar_tensor_tensor(nbeg, bh, -1.0, egc, ALU.mult, ALU.mult).then_inc(S["nbeg_ready"], 1)
                yield
                yield
                dve.wait_ge(S["kk_done"], v + 1)
                dve.wait_ge(S["decay_ready"], v + 1)
                dve.tensor_tensor(B[10][:], bank(2), B[9][:], ALU.mult).then_inc(S["nt_ready"], 1)
                dve.wait_ge(S["kq_done"], v + 1)
                dve.wait_ge(S["kd_ready"], v + 1)
                dve.tensor_tensor(B[4][:], bank(3), B[9][:], ALU.mult).then_inc(S["pt_ready"], 1)
                yield
                dve.wait_ge(S["s_products"], 2 * v + 1)
                dve.wait_ge(S["nbeg_ready"], v + 1)
                for b in range(GH):
                    dve.scalar_tensor_tensor(B[0][:, b, :], PS[:, 4, P * b:P * (b + 1)], nbeg[:, b:b + 1],
                                             B[6][:, b, :], ALU.mult, ALU.add).then_inc(S["rhs_ready"], 1)
                yield
                dve.wait_ge(S["level_product"], LEVELS * v + 1)
                dve.tensor_tensor(B[3][:], bank(0), heads_of(bh), ALU.mult).then_inc(S["level_x"], 1)
                dve.wait_ge(S["level_x"], LEVELS * v + 1)
                dve.wait_ge(S["pt_ready"], v + 1)
                dve.tensor_tensor(B[9][:], over_heads(ident[:]), B[3][:], ALU.subtract).then_inc(S["t_ready"], 1)
                yield
                dve.wait_ge(S["tt_product"], LEVELS * v + 1)
                dve.tensor_tensor(B[11][:], over_heads(ident[:]), bank(1), ALU.subtract).then_inc(S["tt_ready"], 1)
                yield
                for l in range(1, LEVELS):
                    x = blocks_of(XB[l % 2][:], l, 0)
                    n_blocks, width = x.shape[2], x.shape[3]
                    dve.wait_ge(S["level_product"], LEVELS * v + l + 1)
                    dve.tensor_tensor(x, blocks_of(bank(0), l, 0),
                                      bh.unsqueeze(2).unsqueeze(3).broadcast_to([P, GH, n_blocks, width]), ALU.mult) \
                        .then_inc(S["level_x"], 1)
                    yield
                    if l < LEVELS - 1:
                        dve.wait_ge(S["t_product"], (LEVELS - 2) * v + l)
                        dve.wait_ge(S["t_ready"], (LEVELS - 1) * v + l)
                        t_even = blocks_of(B[9][:], l, 0)
                        dve.tensor_tensor(t_even, t_even, blocks_of(bank(2), l, 0), ALU.subtract).then_inc(S["t_ready"], 1)
                    dve.wait_ge(S["tt_product"], LEVELS * v + l + 1)
                    dve.wait_ge(S["tt_ready"], LEVELS * v + l)
                    tt_odd = blocks_of(B[11][:], l, 1)
                    dve.tensor_tensor(tt_odd, tt_odd, blocks_of(bank(1), l, 1), ALU.subtract).then_inc(S["tt_ready"], 1)
                    yield
                yield
                dve.wait_ge(S["o_product"], v + 1)
                dve.wait_ge(S["qs_ready"], GH * v + GH)
                dve.tensor_tensor(B[12][:], B[12][:], bank(0), ALU.add).then_inc(S["o_ready"], 1)
                yield
                dve.wait_ge(S["o_squared"], v + 1)
                dve.tensor_reduce(osum, B[13][:], AX.X, ALU.add).then_inc(S["o_sum"], 1)
                dve.wait_ge(S["o_sum"], v + 1)
                dve.tensor_scalar(omean, osum, 1.0 / P, RMS_EPS, ALU.mult, ALU.add).then_inc(S["o_mean"], 1)
                dve.wait_ge(S["ds_product"], v + 1)
                for b in range(GH):
                    ins = dve.scalar_tensor_tensor(state[:, h0 + b, :], state[:, h0 + b, :], egl[:, b:b + 1],
                                                   PS[:, 1, P * b:P * (b + 1)], ALU.mult, ALU.add)
                ins.then_inc(S["state_ready"], 1)
                yield
                dve.wait_ge(S["o_rms"], v + 1)
                dve.tensor_tensor(B[13][:], B[12][:], heads_of(orms), ALU.mult).then_inc(S["o_scaled"], 1)
                yield
                yield

            with dve.Fori(0, CH) as n:
                k = 0
                for hf in range(2):
                    for _ in gdn_dve(n, hf):
                        if k % 3 == 2:
                            c = (k + 10) // 3
                            split(G_GATES + BODY_CHUNKS * n + c, c)
                        k += 1

            with dve.Fori(0, N_POOL) as u:
                for c in range(4):
                    split(G_P + 4 * u + c + 4, c)

            def z_unit(u, beside):
                for c in range(4):
                    beside(c)
                    if c == 3:
                        for m in range(2):
                            dve.wait_ge(S["z_silu"], FREE["z_silu"] + 2 * u + m + 1)
                            dve.wait_ge(S["z_lo"], FREE["z_lo"] + 2 * u + m - 1)
                            o_tile = (qkv[:, 2 * u + m, META:] if isinstance(u, int) else
                                      qkv[:, bass.ds(2 * u + m, 1), META:].rearrange("p o t -> p (o t)"))
                            dve.scalar_tensor_tensor(zy[:, m, :], zt[:, m, :], onorm, o_tile, ALU.mult, ALU.mult) \
                                .then_inc(S["z_y"], 1)
                        for m in range(2):
                            dve.wait_ge(S["z_hi"], 2 * u + m + 1)
                            dve.tensor_tensor(tile_of(o_lo, 2 * u + m), zy[:, m, :],
                                              tile_of(o_hi, 2 * u + m).bitcast(F32), ALU.subtract).then_inc(S["z_lo"], 1)
                    split(G_Z + 4 * u + c + 4, c)

            def zb_tiles(c):
                for i in range(2 * c, 2 * c + 2):
                    dve.wait_ge(S["zb_done"], i + 1)
                    if i >= 2:
                        dve.wait_ge(S["zb_lo"], i - 1)
                    dve.tensor_scalar(zb_y[i % 2], zb_bank(i), pscale[:, i:i + 1], None, ALU.mult).then_inc(S["zb_y"], 1)
                    dve.wait_ge(S["zb_hi"], i + 1)
                    dve.wait_ge(S["zb_done"], i // 2 * 2 + 2)
                    dve.tensor_tensor(zb_lo[:, i, :], zb_y[i % 2], zb_hi[:, i, :].bitcast(F32), ALU.subtract) \
                        .then_inc(S["zb_lo"], 1)

            with dve.Fori(0, N_Z - 1) as u:
                z_unit(u, lambda c: None)
            z_unit(N_Z - 1, zb_tiles)

            with dve.Fori(0, N_MERGE) as u:
                for c in range(4):
                    if c == 1:
                        for m in range(2):
                            dve.wait_ge(S["gate_a_landed"], 16 * u + 16)
                            dve.wait_ge(*unit_tile(m, "ya_done", u, G_MERGE + 4 * u + 1))
                            dve.scalar_tensor_tensor(gate_a[:, m, :], gate_a[:, m, :], 1.0, PS[:, 4 + m, :],
                                                     ALU.add, ALU.mult).then_inc(S["ya_gated"], 1)
                    if c == 3:
                        for m in range(2):
                            dve.wait_ge(S["gate_b_landed"], 16 * u + 16)
                            dve.wait_ge(*unit_tile(m, "yb_done", u, G_MERGE + 4 * u + 3))
                            dve.wait_ge(S["ya_gated"], FREE["ya_gated"] + 2 * u + m + 1)
                            dve.scalar_tensor_tensor(gate_b[:, m, :], gate_b[:, m, :], 1.0, PS[:, 6 + m, :],
                                                     ALU.add, ALU.mult).then_inc(S["yb_gated"], 1)
                        for m in range(2):
                            dve.wait_ge(S["merged_hi"], 2 * u + m + 1)
                            one = bass.ds(2 * u + m, 1)
                            dve.scalar_tensor_tensor(mg_lo[:, one, :].rearrange("p o t -> p (o t)"), mg[:, m, :], 0.5,
                                                     mg_hi[:, one, :].rearrange("p o t -> p (o t)").bitcast(F32),
                                                     ALU.mult, ALU.subtract).then_inc(S["merged_lo"], 1)
                    split(G_MERGE + 4 * u + c + 4, c)

            with dve.Fori(0, N_OUT) as u:
                for c in range(8):
                    if c == 7:
                        for t in range(TT):
                            dve.wait_ge(S["xr_landed"], 16 * u + 16)
                            dve.wait_ge(*block_tile(t, "out_done", u, G_OUT + 8 * u + 7))
                            dve.tensor_tensor(h[:, t, bass.ds(BLOCK * u, BLOCK)], xr[:, t, :], PS[:, t, :], ALU.add) \
                                .then_inc(S["h1_ready"], 1)
                    split(G_OUT + 8 * u + c + 4, c)

            def sum_of_h(t):
                dve.wait_ge(S["h_squared"], TT + t + 1)
                dve.tensor_reduce(rms_a[:, TT + 1 + t:TT + 2 + t], ssq[:, 5 + 2 * t:7 + 2 * t], AX.X, ALU.add) \
                    .then_inc(S["h_summed"], 1)

            sum_of_h(0)
            sum_of_h(1)
            diagonal(TT + 1)
            for t in range(TT):
                if t + 2 < TT:
                    sum_of_h(t + 2)
                if t + 1 < TT:
                    diagonal(TT + 2 + t)
                weight_quads(TT + 1 + t, hy, nffn, slice(P * t, P * (t + 1)), P)

            def gate_up(g, u, slot_a):
                for sub in range(2):
                    for c in range(8):
                        if c == 7:
                            for m in range(2):
                                r = 4 * u + 2 * sub + m
                                dve.wait_ge(*unit_tile(m, "fu_done", 2 * u + sub, g + 8 * sub + 7))
                                dve.wait_ge(S["silu_ready"], FREE["silu_ready"] + r + 1)
                                dve.wait_ge(S["act_lo"], FREE["act_lo"] + r - 1)
                                dve.tensor_tensor(ay[:, m, :], sg[:, m, :], PS[:, 2 + m, :], ALU.mult) \
                                    .then_inc(S["act_y"], 1)
                            for m in range(2):
                                r = 4 * u + 2 * sub + m
                                dve.wait_ge(S["act_hi"], r + 1)
                                dve.tensor_tensor(a_lo[:, slot_a, 2 * sub + m, :], ay[:, m, :],
                                                  a_hi[:, slot_a, 2 * sub + m, :].bitcast(F32), ALU.subtract) \
                                    .then_inc(S["act_lo"], 1)
                        split(g + 8 * sub + c + 4, c)

            def down(g, u, blocks=N_OUT):
                for blk in range(blocks):
                    for c in range(2):
                        if c == 1:
                            for t in range(TT):
                                r = TT * (N_OUT * u + blk) + t
                                dve.wait_ge(*block_tile(t, "down_done", N_OUT * u + blk, g + 2 * blk + 1))
                                dve.wait_ge(S["h2_ready"], FREE["h2_ready"] + r - TT + 1)
                                dst = h[:, t, BLOCK * blk:BLOCK * (blk + 1)]
                                dve.tensor_tensor(dst, dst, PS[:, 4 + t, :], ALU.add).then_inc(S["h2_ready"], 1)
                        split(g + 2 * blk + c + 4, 2 * blk + c)

            gate_up(G_FFN, 0, 0)
            with dve.Fori(0, N_FFN // 2) as i:
                g = G_FFN + 16 + 48 * i
                gate_up(g, 2 * i + 1, 1)
                down(g + 16, 2 * i)
                gate_up(g + 24, 2 * i + 2, 0)
                down(g + 40, 2 * i + 1)
            down(G_END - 8, N_FFN - 1, 2)
            dve.wait_ge(S["scalew_landed"], 16)
            for t in range(TT):
                for b in range(2):
                    dve.wait_ge(S["down_done"], (TT - 1) * (N_OUT * N_FFN - 2) + 2 * t + b + 1)
                    dve.wait_ge(S["h2_ready"], FREE["h2_ready"] + TT * (N_OUT * N_FFN - 2))
                    dst = h[:, t, BLOCK * (2 + b):BLOCK * (3 + b)]
                    dve.tensor_tensor(dst, dst, last_bank(t, b), ALU.add).then_inc(S["h2_ready"], 1)
                dve.wait_ge(S["f_squared"], TT + 2 * t + 2)
                dve.tensor_reduce(rms_s[:, t:t + 1], ssf[:, 3 * t:3 * t + 3], AX.X, ALU.add).then_inc(S["f_summed"], 1)
                dve.wait_ge(S["f_summed"], t + 1)
                dve.tensor_scalar(rms_a[:, 9 + t:10 + t], rms_s[:, t:t + 1], 1.0 / D, RMS_EPS, ALU.mult, ALU.add) \
                    .then_inc(S["f_mean"], 1)
                dve.wait_ge(S["f_rms"], t + 1)
                dve.wait_ge(S["h2_ready"], FREE["h2_ready"] + TT * (N_OUT * N_FFN - 2) + 2 * t + 2)
                for i in range(2):
                    cols = slice(D // 2 * i, D // 2 * (i + 1))
                    dve.scalar_tensor_tensor(ot[t][:, cols], h[:, t, cols], rms[:, 9 + t:10 + t], scalew[:, cols],
                                             ALU.mult, ALU.mult).then_inc(S["f_scaled"], 1)

        @block.tensor
        def _(pe):
            def turn_quads(u, src, rows):
                pe.wait_ge(S["x_diag"], u + 1)
                for q in range(4):
                    if u not in (0, TT + 1):
                        pe.wait_ge(S["x_weighted"], 4 * u + q - 3)
                    for i in range(4):
                        k = 4 * q + i
                        ins = pe.matmul(bank(4 + q)[:, i, 0:rows], src[0:rows, P * k:P * (k + 1)],
                                        diag[u % (TT + 1)][0:rows, 0:rows], start=True, stop=True)
                    ins.then_inc(S["x_turned"], 1)

            def tiles_split(u):
                pe.wait_ge(S["x_lo"], 2 * (u + 1))
                pe.wait_ge(S["x_lo_v"], 2 * (u + 1))

            def first_unit(g, halves, outs, done, last_tiles):
                for i in range(2):
                    tiles_split(last_tiles[i])
                    for c in range(4):
                        if i == 0:
                            pe.wait_ge(S["lo_ready"], g + c + 1)
                        for m in range(2):
                            for k in range(4):
                                kt = 4 * c + k
                                hi, lo = halves(kt)
                                w = [t[c][:].rearrange("p (k n) -> p k n", k=4)[:, k, P * m:P * (m + 1)]
                                     for t in (whi, wlo)]
                                for j, (lhs, mv) in enumerate(((w[0], hi[i]), (w[0], lo[i]), (w[1], hi[i]))):
                                    ins = pe.matmul(outs(m)[i], lhs, mv, start=kt == 0 and j == 0,
                                                    stop=kt == KT - 1 and j == 2)
                            if i == 1 and m == 0 and c == 3:
                                ins.then_inc(S[done], 1)
                        if i == 1:
                            ins.then_inc(S["chunk_used"], 1)

            def chunk_products(g, g_static, j, n_chunks, moving, outs, done, freed, used=True):
                s = slot(g_static)
                pe.wait_ge(S["lo_ready"], g + 1)
                for m in range(2):
                    if j == 0:
                        freed(m)
                    for k in range(4):
                        kt = 4 * j + k
                        hi, lo = moving(kt)
                        w = [t[s][:].rearrange("p (k n) -> p k n", k=4)[:, k, P * m:P * (m + 1)] for t in (whi, wlo)]
                        for i, (lhs, mv) in enumerate(((w[0], hi), (w[0], lo), (w[1], hi))):
                            for o, r in zip(outs(m), mv):
                                ins = pe.matmul(o, lhs, r, start=kt == 0 and i == 0,
                                                stop=kt == 4 * n_chunks - 1 and i == 2)
                            end = k == 3 and i == 2
                            if end and m == 0 and j == n_chunks - 1:
                                ins.then_inc(S[done], 1)
                            if end and m == 1:
                                ins.then_inc(S["chunk_used"], 1)
                            yield

            def run(products):
                for _ in products:
                    pass

            def token_chunk(g, g_static, k0, n_k, lhs_of, banks, done, freed):
                s = slot(g_static)
                pe.wait_ge(S["lo_ready"], g + 1)
                for t in range(TT):
                    if k0 == 0:
                        freed(t)
                    for k in range(2):
                        hi, lo = lhs_of(k0 + k, t)
                        w = [b[s][:, BLOCK * k:BLOCK * (k + 1)] for b in (whi, wlo)]
                        first, last = k0 + k == 0, k0 + k == n_k - 1
                        pe.matmul(PS[:, banks + t, :], hi, w[0], start=first, stop=False)
                        pe.matmul(PS[:, banks + t, :], hi, w[1], start=False, stop=False)
                        ins = pe.matmul(PS[:, banks + t, :], lo, w[0], start=False, stop=last)
                    if k0 + 2 == n_k and t < TT - 1:
                        ins.then_inc(S[done], 1)
                ins.then_inc(S["chunk_used"], 1)

            pe.wait_ge(S["consts_built"], 2)
            pe.wait_ge(S["rows_landed"], 80)
            na, nb = CONV * 3 * HEADS, 2 * KT + HEADS + 1
            pe.transpose(PS[:, 0, 0:na], rows_a[:, :], ident[0:na, 0:na])
            pe.transpose(PS[:, 1, 0:nb], rows_b[:, :], ident[0:nb, 0:nb]).then_inc(S["rows_turned"], 1)
            turn_quads(0, xt[0], META)
            for t in range(TT):
                turn_quads(t + 1, xt[t + 1], P)

            pe.wait_ge(S["vectors_ready"], 2)

            def hn_halves(kt):
                return tuple([b[:, kt, HALF * i:HALF * (i + 1)] for i in range(2)] for b in (hn_hi, hn_lo))

            def hn_real(kt):
                return [hn_hi[:, kt, META:]], [hn_lo[:, kt, META:]]

            def half_banks(m):
                return [PS[:, 2 * m + i, 0:HALF] for i in range(2)]

            first_unit(G_A, hn_halves, half_banks, "a_done", (2, TT))
            with pe.Fori(1, N_A) as u:
                for c in range(4):
                    run(chunk_products(G_A + 4 * u + c, c, c, 4, hn_halves,
                                       half_banks, "a_done",
                                       lambda m: pe.wait_ge(S["a_copied"], FREE["a_copied"] + 2 * u + m - 1)))

            pe.wait_ge(S["ab_lo"], 1)
            for t in range(CH + 1):
                for k in range(KT):
                    own = slice(0, META) if t == 0 else slice(META + P * (t - 1), META + P * t)
                    dst = PS[0:META, 5, 0:2 * HEADS] if t == 0 else PS[:, 4, 2 * HEADS * t:2 * HEADS * (t + 1)]
                    pe.matmul(dst, hn_hi[:, k, own], ab_h[:, k, :], start=k == 0, stop=False)
                    pe.matmul(dst, hn_hi[:, k, own], ab_l[:, k, :], start=False, stop=False)
                    ins = pe.matmul(dst, hn_lo[:, k, own], ab_h[:, k, :], start=False, stop=k == KT - 1)
                if t == 0:
                    ins.then_inc(S["ab_meta"], 1)
            pe.wait_ge(S["ab_meta_copied"], 1)
            pe.wait_ge(S["consts_built"], N_CONSTS)
            pe.matmul(PS[:, 4, 0:2 * HEADS], meta_rep[:], meta_lg[:], start=True, stop=True).then_inc(S["ab_done"], 1)

            pe.wait_ge(S["meta_staged"], 2)
            pe.wait_ge(S["a_copied"], FREE["a_copied"] + 2 * N_A)
            pe.transpose(PS[:, 1, 0:P], B[1][:, 0, :], ident[:]).then_inc(S["meta_pe"], 1)
            pe.transpose(PS[:, 2, 0:P], B[2][:, 0, :], ident[:])
            pe.wait_ge(S["meta_vec"], 2)
            pe.wait_ge(S["consts_built"], N_CONSTS)
            pe.matmul(PS[:, 3, 0:P], m_g.broadcast_to([P, P]), meta_upper[:], start=True, stop=True)
            pe.matmul(PS[:, 4, 0:1], meta_upper[:], m_g, start=True, stop=True)
            pe.matmul(PS[:, 4, 1:2], meta_block[:], m_g, start=True, stop=True).then_inc(S["meta_pe"], 1)
            pe.wait_ge(S["meta_vec"], 11)
            pe.transpose(PS[:, 1, 0:P], B[3][:, 0, :], ident[:]).then_inc(S["meta_pe"], 1)
            pe.wait_ge(S["meta_act"], 5)
            pe.matmul(PS[:, 0, 0:P], B[8][:, 0, :], B[8][:, 0, :], start=True, stop=True).then_inc(S["meta_pe"], 1)
            pe.wait_ge(S["meta_pool"], 2)
            pe.transpose(PS[:, 0, 0:P], B[4][:, 0, :], ident[:]).then_inc(S["meta_pe"], 1)
            pe.wait_ge(S["meta_vec"], 15)
            pe.transpose(PS[:, 1, 0:P], B[7][:, 0, :], ident[:]).then_inc(S["meta_pe"], 1)
            for l in range(1, META_LEVELS):
                pe.wait_ge(S["meta_pool"], l + 2)
                pe.wait_ge(S["meta_vec"], 14 + 3 * l)
                pe.matmul(PS[:, 0, 0:P], B[4][:, l, :], B[10][:, 0, :], start=True, stop=True).then_inc(S["meta_pe"], 1)
                pe.wait_ge(S["meta_vec"], 15 + 3 * l)
                pe.matmul(PS[:, 2, 0:P], B[0][:, 0, :], B[7][:, 0, :], start=True, stop=True).then_inc(S["meta_pe"], 1)
                pe.matmul(PS[:, 1, 0:P], B[7][:, 0, :], B[0][:, 0, :], start=True, stop=True).then_inc(S["meta_pe"], 1)
            pe.wait_ge(S["meta_vec"], 14 + 3 * META_LEVELS)
            pe.matmul(PS[:, 0, 0:P], B[0][:, 0, :], B[6][:, 0, :], start=True, stop=True).then_inc(S["meta_pe"], 1)
            pe.wait_ge(S["meta_vec"], 15 + 3 * META_LEVELS)
            for i in range(2):
                ins = pe.matmul(bank(2 + i), B[5][:, 0, :], meta_u[:, 4 * i:4 * i + 4, :], start=True, stop=True)
            ins.then_inc(S["meta_pe"], 1)

            def gdn_pe(n, hf):
                v = 2 * n + hf
                h0 = GH * hf
                pe.wait_ge(S["staged"], 5 * v + 5)
                pe.wait_ge(S["state_ready"], v + 1)
                for j, b in enumerate((7, 8, 6)):
                    if j == 2:
                        pe.wait_ge(S["o_stored"], FREE["o_stored"] + v)
                    for i in range(GH):
                        ins = pe.transpose(bank(j)[:, i, :], B[b][:, i, :], ident[:])
                    ins.then_inc(S["qkv_turned"], 1)
                yield
                for i in range(GH):
                    pe.matmul(bank(3)[:, i, :], gcur[hf][:, h0 + i:h0 + i + 1].broadcast_to([P, P]), upper[:],
                              start=True, stop=True)
                pe.matmul(PS[:, 4, 0:8], upper[:], gcur[hf], start=True, stop=True)
                pe.matmul(PS[:, 4, 8:16], ones[:], gcur[hf], start=True, stop=True).then_inc(S["gates_summed"], 1)
                yield
                for j, (b, name) in enumerate(((3, "q_scaled"), (4, "k_scaled"))):
                    pe.wait_ge(S[name], v + 1)
                    for i in range(GH):
                        ins = pe.transpose(bank(j)[:, i, :], B[b][:, i, :], ident[:])
                    ins.then_inc(S["qk_turned"], 1)
                yield
                pe.wait_ge(S["kn_ready"], v + 1)
                pe.wait_ge(S["vb_ready"], v + 1)
                for i in range(GH):
                    ins = pe.matmul(bank(2)[:, i, :], B[8][:, i, :], B[8][:, i, :], start=True, stop=True)
                ins.then_inc(S["kk_done"], 1)
                for i in range(GH):
                    ins = pe.matmul(bank(3)[:, i, :], B[8][:, i, :], B[7][:, i, :], start=True, stop=True)
                ins.then_inc(S["kq_done"], 1)
                yield
                pe.wait_ge(S["sums_copied"], v + 1)
                for j in (8, 7):
                    for i in range(GH):
                        ins = pe.matmul(bank(4 if j == 8 else 5)[:, i, :], B[j][:, i, :], state[:, h0 + i, :],
                                        start=True, stop=True)
                    ins.then_inc(S["s_products"], 1)
                yield
                pe.wait_ge(S["level_masked"], LEVELS * v + 1)
                for i in range(GH):
                    ins = pe.transpose(bank(0)[:, i, :], B[1][:, i, :], ident[:])
                ins.then_inc(S["level_product"], 1)
                yield
                pe.wait_ge(S["level_x"], LEVELS * v + 1)
                for i in range(GH):
                    ins = pe.transpose(bank(1)[:, i, :], B[3][:, i, :], ident[:])
                ins.then_inc(S["tt_product"], 1)
                yield
                for l in range(1, LEVELS):
                    x = XB[l % 2]
                    pe.wait_ge(S["level_masked"], LEVELS * v + l + 1)
                    pe.wait_ge(S["t_ready"], (LEVELS - 1) * v + l)
                    for i in range(GH):
                        ins = pe.matmul(blocks_of(bank(0), l, 0)[:, i, :, :], B[1 + l % 2][:, i, :],
                                        blocks_of(B[9][:], l, 0)[:, i, :, :], start=True, stop=True)
                    ins.then_inc(S["level_product"], 1)
                    yield
                    pe.wait_ge(S["level_x"], LEVELS * v + l + 1)
                    pe.wait_ge(S["x_cleared"], (LEVELS - 1) * v + l)
                    pe.wait_ge(S["tt_ready"], LEVELS * v + l)
                    if l < LEVELS - 1:
                        for i in range(GH):
                            ins = pe.matmul(blocks_of(bank(2), l, 0)[:, i, :, :], B[11][:, i, :],
                                            blocks_of(x[:], l, 0)[:, i, :, :], start=True, stop=True)
                        ins.then_inc(S["t_product"], 1)
                    for i in range(GH):
                        ins = pe.matmul(blocks_of(bank(1), l, 1)[:, i, :, :], x[:, i, :],
                                        blocks_of(B[11][:], l, 1)[:, i, :, :], start=True, stop=True)
                    ins.then_inc(S["tt_product"], 1)
                    yield
                pe.wait_ge(S["tt_ready"], LEVELS * v + LEVELS)
                pe.wait_ge(S["rhs_ready"], GH * v + GH)
                pe.wait_ge(S["pt_ready"], v + 1)
                for i in range(GH):
                    ins = pe.matmul(bank(3)[:, i, :], B[11][:, i, :], B[0][:, i, :], start=True, stop=True)
                ins.then_inc(S["vn_product"], 1)
                yield
                pe.wait_ge(S["vn_ready"], v + 1)
                for i in range(GH):
                    ins = pe.matmul(bank(0)[:, i, :], B[4][:, i, :], B[10][:, i, :], start=True, stop=True)
                ins.then_inc(S["o_product"], 1)
                yield
                for i in range(GH):
                    ins = pe.matmul(bank(1)[:, i, :], B[5][:, i, :], B[10][:, i, :], start=True, stop=True)
                ins.then_inc(S["ds_product"], 1)
                yield
                yield
                pe.wait_ge(S["o_scaled"], v + 1)
                for i in range(GH):
                    ins = pe.transpose(bank(2)[:, i, :], B[13][:, i, :], ident[:])
                ins.then_inc(S["o_turned"], 1)
                yield

            def gate_products(n):
                for u in range(BODY_CHUNKS // 4):
                    for c in range(4):
                        yield from chunk_products(G_GATES + BODY_CHUNKS * n + 4 * u + c, c, c, 4, hn_real,
                                                  lambda m: [PS[:, 6 + m, :]], "gate_done",
                                                  lambda m: pe.wait_ge(S["gate_freed"], FREE["gate_freed"] + 8 * n + 2 * u + m - 1))

            with pe.Fori(0, CH) as n:
                gates = gate_products(n)
                for hf in range(2):
                    steps_of_half = gdn_pe(n, hf)
                    for _ in range(STEPS):
                        for _ in range(PIECE):
                            next(gates, None)
                        next(steps_of_half)

            def p_banks_free(u, m):
                if m == 1:
                    pe.wait_ge(S["gate_freed"], FREE["gate_freed"] + 2 * N_GATES)
                pe.wait_ge(S["p_copied"], FREE["p_copied"] + 2 * u + m - 1)

            with pe.Fori(0, N_POOL) as u:
                for c in range(4):
                    run(chunk_products(G_P + 4 * u + c, c, c, 4, hn_halves,
                                       lambda m: [PS[:, 4 + 2 * m + i, 0:HALF] for i in range(2)], "p_done",
                                       lambda m: p_banks_free(u, m)))
            def z_unit(u):
                for c in range(4):
                    run(chunk_products(G_Z + 4 * u + c, c, c, 4, hn_real, lambda m: [PS[:, m, :]],
                                       "z_done", lambda m: pe.wait_ge(S["z_silu"], FREE["z_silu"] + 2 * u + m - 1)))

            pe.wait_ge(S["o_stored"], FREE["o_stored"] + 2 * CH)
            pe.wait_ge(S["state_ready"], 2 * CH + 1)
            with pe.Fori(0, N_Z - 1) as u:
                z_unit(u)
            pe.wait_ge(S["poolw_landed"], 16)
            pe.wait_ge(S["pooled_ready"], 1)
            for i in range(HEADS):
                g, m = i // 2, i % 2
                if i >= 6:
                    pe.wait_ge(S["zb_y"], i - 5)
                for k in range(2):
                    ins = pe.matmul(zb_bank(i), poolw[:, g, k, P * m:P * (m + 1)], pooled[:, 2 * g + k, :],
                                    start=k == 0, stop=k == 1)
                ins.then_inc(S["zb_done"], 1)
            z_unit(N_Z - 1)
            pe.wait_ge(S["zb_y"], HEADS)

            with pe.Fori(0, N_MERGE) as u:
                for c in range(2):
                    pe.wait_ge(S["z_lo"], FREE["z_lo"] + 2 * (N_Z - 1 + c))
                    run(chunk_products(G_MERGE + 4 * u + c, c, c, 2, lambda kt: ([o_hi[:, kt, :]], [o_lo[:, kt, :]]),
                                       lambda m: [PS[:, 4 + m, :]], "ya_done",
                                       lambda m: pe.wait_ge(S["ya_gated"], FREE["ya_gated"] + 2 * u + m - 1)))
                pe.wait_ge(S["zb_lo"], HEADS)
                for c in range(2):
                    run(chunk_products(G_MERGE + 4 * u + 2 + c, 2 + c, c, 2,
                                       lambda kt: ([zb_hi[:, kt, :]], [zb_lo[:, kt, :]]),
                                       lambda m: [PS[:, 6 + m, :]], "yb_done",
                                       lambda m: pe.wait_ge(S["yb_gated"], FREE["yb_gated"] + 2 * u + m - 1)))

            def merged_tile(kt, t):
                return mg_hi[:, kt, P * t:P * (t + 1)], mg_lo[:, kt, P * t:P * (t + 1)]

            with pe.Fori(0, N_OUT) as u:
                for c in range(8):
                    pe.wait_ge(S["merged_lo"], 2 * (N_MERGE - 1 + c // 7))
                    token_chunk(G_OUT + 8 * u + c, c, 2 * c, KT, merged_tile, 0, "out_done",
                                lambda t: pe.wait_ge(S["h1_ready"], FREE["h1_ready"] + TT * (u - 1) + t + 1))
            for t in range(TT):
                turn_quads(TT + 1 + t, h[:, t, :], P)

            def hn_ffn(kt):
                return [hn_hi[:, kt, 0:SEQ]], [hn_lo[:, kt, 0:SEQ]]

            def ffn_halves(kt):
                return tuple([b[:, kt, SEQ // 2 * i:SEQ // 2 * (i + 1)] for i in range(2)] for b in (hn_hi, hn_lo))

            def gate_up(g, u, first=False):
                for sub in range(2):
                    r = 4 * u + 2 * sub

                    if first and sub == 0:
                        first_unit(g, ffn_halves, lambda m: [PS[:, m, SEQ // 2 * i:SEQ // 2 * (i + 1)] for i in range(2)],
                                   "fg_done", (TT + 2, 2 * TT))
                    for c in range(4) if not (first and sub == 0) else ():
                        run(chunk_products(g + 8 * sub + c, c, c, 4, hn_ffn, lambda m: [PS[:, m, :]], "fg_done",
                                           lambda m: pe.wait_ge(S["silu_ready"], FREE["silu_ready"] + r + m - 1)))
                    for c in range(4):
                        run(chunk_products(g + 8 * sub + 4 + c, c, c, 4, hn_ffn, lambda m: [PS[:, 2 + m, :]],
                                           "fu_done", lambda m: pe.wait_ge(S["act_y"], FREE["act_y"] + r + m - 1)))

            def down(g, u, slot_a, blocks=N_OUT):
                pe.wait_ge(S["act_lo"], FREE["act_lo"] + 4 * u + 4)
                for blk in range(blocks):
                    for c in range(2):
                        token_chunk(g + 2 * blk + c, 2 * blk + c, 2 * c, 4,
                                    lambda k, t: (a_hi[:, slot_a, k, P * t:P * (t + 1)],
                                                  a_lo[:, slot_a, k, P * t:P * (t + 1)]),
                                    4, "down_done",
                                    lambda t: pe.wait_ge(S["h2_ready"], FREE["h2_ready"] + TT * (N_OUT * u + blk - 1) + t + 1))

            gate_up(G_FFN, 0, first=True)
            with pe.Fori(0, N_FFN // 2) as i:
                g = G_FFN + 16 + 48 * i
                gate_up(g, 2 * i + 1)
                down(g + 16, 2 * i, 0)
                gate_up(g + 24, 2 * i + 2)
                down(g + 40, 2 * i + 1, 1)
            down(G_END - 8, N_FFN - 1, 0, 2)
            pe.wait_ge(S["lo_ready"], G_END)
            for t in range(TT):
                for b in range(2):
                    if b == 0:
                        pe.wait_ge(S["h2_ready"], FREE["h2_ready"] + TT * (N_OUT * N_FFN - 3) + t + 1)
                    for k in range(4):
                        s = slot(2 * b + k // 2)
                        w_hi, w_lo = (x[s][:, BLOCK * (k % 2):BLOCK * (k % 2 + 1)] for x in (whi, wlo))
                        hi, lo = (x[:, 0, k, P * t:P * (t + 1)] for x in (a_hi, a_lo))
                        pe.matmul(last_bank(t, b), hi, w_hi, start=k == 0, stop=False)
                        pe.matmul(last_bank(t, b), hi, w_lo, start=False, stop=False)
                        ins = pe.matmul(last_bank(t, b), lo, w_hi, start=False, stop=k == 3)
                    ins.then_inc(S["down_done"], 1)


_INS = ["x", "meta_tokens", "norm_mix_w", "w_in", "conv_w", "a_log", "dt_bias", "o_norm_w", "w_proj_a", "pool_w",
        "pool_scale", "w_proj_b", "w_out", "norm_ffn_w", "w_ffn_gate", "w_ffn_up", "w_ffn_down", "norm_final_w"]


def kernel(**inputs):
    import concourse.bacc as bacc
    from concourse.bass_utils import run_bass_kernel_spmd

    nc = bacc.Bacc("TRN2", target_bir_lowering=False, num_devices=1, dynamic_dma_scratch_size=1024)
    arrays, args = {}, []
    for name in _INS:
        a = np.ascontiguousarray(inputs[name])
        arrays[f"in_{name}"] = a
        args.append(nc.dram_tensor(f"in_{name}", a.shape, mybir.dt.from_np(a.dtype), kind="ExternalInput").ap())
    res = nc.dram_tensor("result", (1, SEQ, D), F32, kind="ExternalOutput").ap()
    hybrid_block(nc, *args, res)
    return run_bass_kernel_spmd(nc, [arrays], core_ids=[0]).results[0]["result"]
```

```python
from contextlib import ExitStack

import numpy as np

import concourse.bass as bass
from concourse import mybir
from concourse.alu_op_type import AluOpType as ALU

F32 = mybir.dt.float32
F32R = mybir.dt.float32r
ACT = mybir.ActivationFunctionType
AX = mybir.AxisListType

P = 128
META = 16
SEQ = 512
TOK = META + SEQ
HALF = TOK // 2
D = 2048
KT = D // P
HEADS = 8
QT, K_T, VT = 0, HEADS, 2 * HEADS
CONV = 4
POOL_GROUPS = 4
FFN = 5632
RMS_EPS = 1e-6
L2_EPS = 1e-6
NEG = -1e30

COL_K = HEADS * P
COL_Z = 3 * HEADS * P
COL_AB = COL_Z + HEADS * P
COL_P = COL_AB + 2 * HEADS
COL_GATES = COL_P + POOL_GROUPS * 2 * P

SLOTS = 4
CHUNK = 1024
UNIT = 256
BLOCK = 512

N_A = 3 * HEADS * P // UNIT
N_KV = 2 * HEADS * P // UNIT
N_BESIDE = 2
N_POOL = HEADS * P // UNIT
N_Z = HEADS * P // UNIT
N_GATES = 2 * D // UNIT
N_MERGE = D // UNIT
N_OUT = D // BLOCK
N_FFN = FFN // BLOCK
TT = SEQ // P

CH = SEQ // P
GH = 4
LEVELS = 7
META_LEVELS = 4
N_CONSTS = 20 + 6 * LEVELS
STEPS = 24
BODY_CHUNKS = N_GATES * 4 // CH
PIECE = 24 * BODY_CHUNKS // (2 * STEPS)

FREE = dict(a_copied=2, conv_done=2, qkv_ready=2, gate_freed=2, gates_stored=16, o_stored=1, p_copied=2,
            z_silu=2, z_y=2, z_lo=2, ya_gated=2, yb_gated=2, merged_sum=2, h1_ready=TT, h2_ready=TT,
            silu_ready=2, act_y=2, act_lo=2)

G_A = 0
G_GATES = G_A + N_A * 4
G_P = G_GATES + N_GATES * 4
G_Z = G_P + N_POOL * 4
G_MERGE = G_Z + N_Z * 4
G_OUT = G_MERGE + N_MERGE * 4
G_FFN = G_OUT + N_OUT * 8
G_END = G_FFN + N_FFN * 24

SEMAPHORES = """
rows_landed ab_landed small_landed poolw_landed scalew_landed
consts_built rows_turned vectors_ready vectors_more
x_squared x_rms_a x_rms x_diag x_turned x_weighted x_hi x_lo x_lo_v
h_squared h_summed
hi_ready lo_ready chunk_used
a_done a_copied conv_step conv_done qkv_ready
ab_hi ab_lo ab_product ab_copied ab_done logits_copied ab_vec ab_act
meta_staged meta_pe meta_vec meta_act meta_pool
staged qkv_turned gates_summed q_squared k_squared norms_a norms_summed norms_ready q_eps_ready
sums_copied g_differenced g_masked decay_exp decay_ready last_differenced decays_small nbeg_ready
beta_k_ready vb_ready kd_factor kd_ready
kk_done kq_done nt_ready pt_ready s_products rhs_ready qs_ready
n_turned z_masked z_ready z_kept z_product mask_ready x_ready v_copied v_ready vx_product
vn_product vn_ready o_product ds_product o_ready state_ready o_squared o_sum o_mean o_rms o_scaled
o_turned o_stored
gate_done gate_freed gates_stored
p_done p_copied window_step pooled_ready
z_done z_silu z_y z_hi z_lo
zb_done zb_y zb_hi zb_lo
ya_done yb_done ya_gated yb_gated merged_sum merged_hi merged_lo gate_a_landed gate_b_landed
out_done h1_ready xr_landed
fg_done fu_done silu_ready act_y act_hi act_lo down_done h2_ready
f_squared f_summed f_mean f_rms f_scaled out_stored
""".split()


def hybrid_block(nc, x, meta_tokens, norm_mix_w, w_in, conv_w, a_log, dt_bias, o_norm_w, w_proj_a, pool_w,
                 pool_scale, w_proj_b, w_out, norm_ffn_w, w_ffn_gate, w_ffn_up, w_ffn_down, norm_final_w, out):
    ctx = ExitStack()
    with ctx:
        S = {n: ctx.enter_context(nc.semaphore(n)) for n in SEMAPHORES}
        landed = [ctx.enter_context(nc.semaphore(f"weights_landed{i}")) for i in range(SLOTS)]
        x_landed = [ctx.enter_context(nc.semaphore(f"x_landed{i}")) for i in range(TT + 1)]
        gates_dram = nc.dram_tensor("gates_dram", [2 * D, SEQ], F32).ap()

        top = [(nc.sbuf_base + 63) // 64 * 64]

        def place(name, shape, dtype=F32, at=None):
            size = int(np.prod(shape[1:])) * 4
            offset = top[0] if at is None else at
            if at is None:
                top[0] += (size + 63) // 64 * 64
            return nc.alloc_sbuf_tensor_at(name, shape, dtype, offset=offset)

        raw = [place(f"w_raw{i}", [P, CHUNK]) for i in range(SLOTS)]
        whi = [place(f"w_hi{i}", [P, CHUNK], F32R) for i in range(SLOTS)]
        wlo = [place(f"w_lo{i}", [P, CHUNK], F32R) for i in range(SLOTS)]
        ident = place("ident", [P, P])
        upper = place("upper", [P, P])
        ones = place("ones", [P, P])
        cap = place("cap", [P, P])
        levels_at = top[0]
        levels = place("levels", [P, LEVELS, P])
        minus_half = place("minus_half", [P, 16])
        vec_a = place("vec_a", [P, CONV * 3 * HEADS])
        vec_b = place("vec_b", [P, 2 * KT + HEADS + 1])
        nmix, nffn = vec_b[:, 0:KT], vec_b[:, KT:2 * KT]
        pscale, onorm = vec_b[:, 2 * KT:2 * KT + HEADS], vec_b[:, 2 * KT + HEADS:2 * KT + HEADS + 1]
        g_all = place("g_all", [P, CH + 1, HEADS])
        b_all = place("b_all", [P, CH + 1, HEADS])
        ssq = place("ssq", [P, 16])
        rms_a = place("rms_a", [P, 16])
        rms = place("rms", [P, 16])
        small = place("small", [P, 160])
        state_at = top[0]
        state = place("state", [P, HEADS, P])
        hn_at = top[0]
        hn_hi = place("hn_hi", [P, KT, TOK], F32R)
        hn_lo = place("hn_lo", [P, KT, TOK], F32R)
        qkv_at = top[0]
        qkv = place("qkv", [P, 3 * HEADS, TOK])
        kv_at = qkv_at + HEADS * TOK * 4
        v_at = kv_at + HEADS * TOK * 4
        tmp_at = top[0]
        B = [place(f"gdn{i}", [P, GH, P]) for i in range(14)]
        top[0] = tmp_at + 16 * SEQ * 4
        ext_at = top[0]
        gate_out = place("gate_out", [P, 2, SEQ])
        top[0] += 2 * SEQ * 4
        poolw_at = top[0]
        top[0] += POOL_GROUPS * 2 * UNIT * 4
        XB, mask_buf = (B[3], B[13]), (B[2], B[9])
        kept = B[10]
        xt = [place(f"xt{i}", [P, D], at=qkv_at + i * D * 4) for i in range(TT + 1)]
        x_junk = place("x_junk", [P, D], at=qkv_at + (TT + 1) * D * 4)
        rows_a = place("rows_a", [CONV * 3 * HEADS, P], at=qkv_at + (TT + 2) * D * 4)
        rows_b = place("rows_b", [2 * KT + HEADS + 1, P], at=qkv_at + (TT + 2) * D * 4 + 512)
        xy = [place(f"xy{i}", [P, 4, P], at=tmp_at + i * 2048) for i in range(4)]
        diag = [place(f"diag{i}", [P, P], at=ext_at + 4608 + 512 * i) for i in range(TT + 1)]
        conv_in = [place(f"conv_in{i}", [P, TOK + CONV - 1], at=tmp_at + 20480 + i * 2176) for i in range(2)]
        conv_acc = [place(f"conv_acc{i}", [P, TOK], at=tmp_at + 20480 + (2 + i) * 2176) for i in range(2)]
        ab_raw = place("ab_raw", [P, KT, 2 * HEADS], at=ext_at)
        ab_hl = place("ab_hl", [P, KT, 2, 2 * HEADS], F32R, at=ext_at + 1024)
        ab_h, ab_l = ab_hl[:, :, 0, :], ab_hl[:, :, 1, :]
        lg = place("lg", [P, CH + 1, 2 * HEADS], at=ext_at + 3072)
        ab_t = [place(f"ab_t{i}", [P, CH + 1, HEADS], at=ext_at + 3392 + 192 * i) for i in range(4)]
        alog_b = place("alog_b", [P, HEADS], at=ext_at + 4224)
        dtb_b = place("dtb_b", [P, HEADS], at=ext_at + 4288)
        ab_cm = place("ab_cm", [4 * HEADS, SEQ], at=tmp_at)
        ab_cm_meta = place("ab_cm_meta", [4 * HEADS, HEADS, META], at=tmp_at + 2048)
        both = place("both", [4 * HEADS, 2 * HEADS], at=poolw_at + (LEVELS + 1) * P * 4)
        keep = place("keep", [P, LEVELS, P], at=poolw_at)
        strict = place("strict", [P, P], at=poolw_at + LEVELS * P * 4)
        meta_upper = place("meta_upper", [P, P], at=tmp_at + 29184)
        meta_block = place("meta_block", [P, P], at=tmp_at + 29184 + 512)
        meta_neg = place("meta_neg", [P, P], at=tmp_at + 29184 + 1024)
        meta_sel = place("meta_sel", [P, HEADS], at=tmp_at + 29184 + 1536)
        meta_u = place("meta_u", [P, HEADS, P], at=ext_at + 4096)
        (m_k, m_v, m_square, m_decay, m_kd, m_beta_v, m_x, m_t, m_nt, m_tt) = (B[i // 4][:, i % 4, :] for i in range(10))
        m_level, m_masks = B[3], B[4]
        o_hi = place("o_hi", [P, HEADS, SEQ], F32R, at=tmp_at)
        o_lo = place("o_lo", [P, HEADS, SEQ], F32R, at=tmp_at + HEADS * SEQ * 4)
        p_in = place("p_in", [P, HEADS, TOK], at=kv_at)
        pooled = place("pooled", [P, HEADS, SEQ], at=v_at)
        zt = place("zt", [P, 2, SEQ], at=ext_at)
        zy = place("zy", [P, 2, SEQ], at=ext_at + 4096)
        zb_hi = place("zb_hi", [P, HEADS, SEQ], F32R, at=kv_at)
        zb_lo = place("zb_lo", [P, HEADS, SEQ], F32R, at=v_at)
        poolw = place("poolw", [P, POOL_GROUPS, 2, UNIT], at=poolw_at)
        win = [place(f"win{i}", [P, TOK], at=at_) for i, at_ in enumerate((levels_at, state_at))]
        zb_y = [win[i][:, 0:SEQ] for i in range(2)]
        gate_a = place("gate_a", [P, 2, SEQ], at=qkv_at)
        gate_b = place("gate_b", [P, 2, SEQ], at=qkv_at + 4096)
        mg = place("mg", [P, 2, SEQ], at=qkv_at + 8192)
        mg_hi = place("mg_hi", [P, KT, SEQ], F32R, at=hn_at)
        mg_lo = place("mg_lo", [P, KT, SEQ], F32R, at=hn_at + KT * SEQ * 4)
        h = place("h", [P, TT, D], at=tmp_at)
        xr = place("xr", [P, TT, BLOCK], at=v_at)
        h_junk = place("h_junk", [P, D - BLOCK], at=qkv_at)
        hy = [place(f"hy{i}", [P, 4, P], at=kv_at + i * 2048) for i in range(4)]
        a_hi = place("a_hi", [P, 2, 4, SEQ], F32R, at=qkv_at)
        a_lo = place("a_lo", [P, 2, 4, SEQ], F32R, at=qkv_at + 16384)
        sg = place("sg", [P, 2, SEQ], at=qkv_at + 32768)
        ay = place("ay", [P, 2, SEQ], at=qkv_at + 32768 + 4096)
        ot = [place(f"ot{i}", [P, D], at=hn_at + i * 8192) for i in range(TT)]
        scalew = place("scalew", [P, D], at=hn_at + TT * 8192)
        f_junk = place("f_junk", [P, D // 2], at=hn_at + (TT + 1) * 8192)
        assert top[0] <= nc.sbuf_usable_end, (top[0], nc.sbuf_usable_end)

        PS = ctx.enter_context(nc.psum_tensor("psum", [P, 8, 512], F32))

        def bank(i, heads=GH):
            return PS[:, i, :].rearrange("p (h c) -> p h c", h=4)[:, 0:heads, :]

        def last_bank(t, b):
            return PS[:, (4 if b == 0 else 0) + t, :]

        def zb_bank(i):
            return PS[:, 2 + i % 6, :]

        def tile_of(b, i):
            return b[:, i, :] if isinstance(i, int) else b[:, bass.ds(i, 1), :].rearrange("p o t -> p (o t)")

        def first_tile(u, q):
            return 2 * u - 2 * N_KV if q else 2 * u + K_T

        def x_tokens(u):
            return slice(0, META) if u == 0 else slice(META + P * (u - 1), META + P * u)

        def slot(g_static):
            return g_static % SLOTS

        gcur, bcur = (small[:, 0:8], small[:, 130:138]), (small[:, 8:16], small[:, 138:146])
        norm_s, norm_e, norm_r = small[:, 16:24], small[:, 24:32], small[:, 32:40]
        sums = small[:, 40:56]
        egc, egl, ged, nbeg = small[:, 56:60], small[:, 60:64], small[:, 64:68], small[:, 68:72]
        gld, ged_k, beta_k = small[:, 72:76], small[:, 88:92], small[:, 92:96]
        q_eps = norm_r[:, 0:GH]
        osum, omean, orms = small[:, 76:80], small[:, 80:84], small[:, 84:88]
        m_g, m_b, m_bk, m_ss, m_se, m_r, m_edk = (small[:, 96 + i:97 + i] for i in range(7))
        m_sums, m_nd, m_ed, m_sel8 = small[:, 104:106], small[:, 107:108], small[:, 108:109], small[:, 112:120]
        m_sel8b = small[:, 120:128]
        rms_s = small[:, 108:108 + TT]
        ssf = small[:, 96:96 + 3 * TT]

        def heads_of(v, width=P):
            return v.unsqueeze(2).broadcast_to([P, GH, width])

        def blocks_of(b, l, odd):
            return b.rearrange("p h (n two s) -> p h n two s", two=2, s=1 << l)[:, :, :, odd, :]

        def over_heads(m):
            return m.unsqueeze(1).broadcast_to([P, GH, P])

        w_in_v = w_in[0].rearrange("(k p) n -> p k n", p=P)
        pa_v = w_proj_a[0].rearrange("(k p) n -> p k n", p=P)
        pb_v = w_proj_b[0].rearrange("(k p) n -> p k n", p=P)
        wo_v = w_out[0].rearrange("(k p) n -> p k n", p=P)
        fg_v = w_ffn_gate[0].rearrange("(k p) n -> p k n", p=P)
        fu_v = w_ffn_up[0].rearrange("(k p) n -> p k n", p=P)
        fd_v = w_ffn_down[0].rearrange("(k p) n -> p k n", p=P)
        gates_v = gates_dram.rearrange("(k p) n -> p k n", p=P)
        x_v = x[0].rearrange("(t p) d -> p t d", p=P)
        out_v = out[0].rearrange("(t p) d -> p t d", p=P)

        def unit_tile(m, name, unit, last_chunk):
            return (S[name], unit + 1) if m == 0 else (S["chunk_used"], last_chunk + 1)

        def block_tile(t, name, unit, last_chunk):
            return (S[name], (TT - 1) * unit + t + 1) if t < TT - 1 else (S["chunk_used"], last_chunk + 1)

        block = ctx.enter_context(nc.Block())

        @block.sync
        def _(sp):
            def load_x(u, src, rows):
                sp.dma_start(xt[u][0:rows, :], src).then_inc(x_landed[u], 16)

            def load(g, g_static, src, k):
                if not (isinstance(g, int) and g < SLOTS):
                    sp.wait_ge(S["lo_ready"], g - (SLOTS - 1))
                s = slot(g_static)
                sp.dma_start(raw[s][:].rearrange("p (k n) -> p k n", k=k), src).then_inc(landed[s], 16)

            for name, count in FREE.items():
                sp.sem_inc(S[name], count)
            load_x(0, meta_tokens, META)
            load_x(1, x_v[:, 0, :], P)
            sp.dma_start(rows_a[:, :], conv_w[0].rearrange("j (m p) -> (j m) p", p=P)).then_inc(S["rows_landed"], 16)
            at = 0
            for v, n in ((norm_mix_w[0], KT), (norm_ffn_w[0], KT), (pool_scale[0], HEADS), (o_norm_w[0], 1)):
                sp.dma_start(rows_b[at:at + n, :], v.rearrange("(m p) -> m p", p=P)).then_inc(S["rows_landed"], 16)
                at += n
            for t in range(1, TT):
                load_x(t + 1, x_v[:, t, :], P)
            for c in range(4):
                load(c, c, w_in_v[:, 4 * c:4 * c + 4, COL_K:COL_K + UNIT], 4)
            sp.dma_start(ab_raw[:, :, :], w_in_v[:, :, COL_AB:COL_AB + 2 * HEADS]).then_inc(S["ab_landed"], 16)
            sp.dma_start(alog_b[:, :], a_log[0].partition_broadcast(P)).then_inc(S["small_landed"], 16)
            sp.dma_start(dtb_b[:, :], dt_bias[0].partition_broadcast(P)).then_inc(S["small_landed"], 16)
            for first, end, col in ((1, N_KV, COL_K), (N_KV, N_A, -N_KV * UNIT)):
                with sp.Fori(first, end) as u:
                    for c in range(4):
                        load(G_A + 4 * u + c, c, w_in_v[:, 4 * c:4 * c + 4, bass.ds(UNIT * u + col, UNIT)], 4)
            with sp.Fori(0, N_GATES) as u:
                for c in range(4):
                    load(G_GATES + 4 * u + c, c, w_in_v[:, 4 * c:4 * c + 4, bass.ds(COL_GATES + UNIT * u, UNIT)], 4)
            with sp.Fori(0, N_POOL) as u:
                for c in range(4):
                    load(G_P + 4 * u + c, c, w_in_v[:, 4 * c:4 * c + 4, bass.ds(COL_P + UNIT * u, UNIT)], 4)
            sp.wait_ge(S["state_ready"], 2 * CH + 1)
            sp.dma_start(poolw[:, :, :, :], pool_w[0].rearrange("g (k p) d -> p g k d", p=P)).then_inc(S["poolw_landed"], 16)
            with sp.Fori(0, N_Z) as u:
                for c in range(4):
                    load(G_Z + 4 * u + c, c, w_in_v[:, 4 * c:4 * c + 4, bass.ds(COL_Z + UNIT * u, UNIT)], 4)
            sp.wait_ge(S["gates_stored"], FREE["gates_stored"] + 16 * N_GATES)

            def merge_unit(u, first):
                for c in range(2):
                    load(G_MERGE + 4 * u + c, c, pa_v[:, 4 * c:4 * c + 4, bass.ds(UNIT * u, UNIT)], 4)
                for c in range(2):
                    load(G_MERGE + 4 * u + 2 + c, 2 + c, pb_v[:, 4 * c:4 * c + 4, bass.ds(UNIT * u, UNIT)], 4)
                if first:
                    sp.wait_ge(S["z_y"], FREE["z_y"] + 2 * N_Z)
                else:
                    sp.wait_ge(S["merged_sum"], FREE["merged_sum"] + 2 * u)
                sp.dma_start(gate_a[:, :, :], gates_v[:, bass.ds(2 * u, 2), :]).then_inc(S["gate_a_landed"], 16)
                sp.dma_start(gate_b[:, :, :], gates_v[:, bass.ds(KT + 2 * u, 2), :]).then_inc(S["gate_b_landed"], 16)

            merge_unit(0, True)
            with sp.Fori(1, N_MERGE) as u:
                merge_unit(u, False)

            def out_unit(u, first):
                for c in range(8):
                    load(G_OUT + 8 * u + c, c, wo_v[:, 2 * c:2 * c + 2, bass.ds(BLOCK * u, BLOCK)], 2)
                if first:
                    sp.wait_ge(S["chunk_used"], G_OUT)
                else:
                    sp.wait_ge(S["h1_ready"], FREE["h1_ready"] + TT * u)
                sp.dma_start(xr[:, :, :], x_v[:, :, bass.ds(BLOCK * u, BLOCK)]).then_inc(S["xr_landed"], 16)

            out_unit(0, True)
            with sp.Fori(1, N_OUT) as u:
                out_unit(u, False)

            def gate_up(g, u):
                for sub in range(2):
                    for i, v in enumerate((fg_v, fu_v)):
                        for c in range(4):
                            n = 8 * sub + 4 * i + c
                            load(g + n, n, v[:, 4 * c:4 * c + 4, bass.ds(BLOCK * u + UNIT * sub, UNIT)], 4)

            def down(g, u):
                for blk in range(N_OUT):
                    for c in range(2):
                        n = 2 * blk + c
                        load(g + n, n, fd_v[:, bass.ds(4 * u + 2 * c, 2), BLOCK * blk:BLOCK * (blk + 1)], 2)

            gate_up(G_FFN, 0)
            with sp.Fori(0, N_FFN // 2) as i:
                g = G_FFN + 16 + 48 * i
                gate_up(g, 2 * i + 1)
                down(g + 16, 2 * i)
                gate_up(g + 24, 2 * i + 2)
                down(g + 40, 2 * i + 1)
            down(G_END - 8, N_FFN - 1)
            sp.wait_ge(S["chunk_used"], G_END - 16)
            sp.dma_start(scalew[:, :], norm_final_w.partition_broadcast(P)).then_inc(S["scalew_landed"], 16)
            for t in range(TT):
                for i in range(2):
                    cols = slice(D // 2 * i, D // 2 * (i + 1))
                    sp.wait_ge(S["f_scaled"], 2 * t + i + 1)
                    sp.dma_start(out_v[:, t, cols], ot[t][:, cols]).then_inc(S["out_stored"], 16)
            sp.wait_ge(S["out_stored"], 16 * 2 * TT)

        @block.gpsimd
        def _(pool):
            built = [0]

            def const(ins):
                built[0] += 1
                ins.then_inc(S["consts_built"], 1)
                pool.wait_ge(S["consts_built"], built[0])

            const(pool.memset(ident[:], 0.0))
            const(pool.affine_select(out=ident[:], in_=ident[:], compare_op=ALU.not_equal, fill=1.0, base=0,
                                     pattern=[[-1, P]], channel_multiplier=1))
            const(pool.memset(minus_half[:], -0.5))

            const(pool.tensor_tensor(both[:], ident[0:4 * HEADS, 0:2 * HEADS], ident[0:4 * HEADS, 2 * HEADS:4 * HEADS],
                                     ALU.add))

            def rms_of(u, rows, total, ready, count):
                pool.wait_ge(S[ready], count)
                pool.tensor_scalar(rms_a[0:rows, u:u + 1], total, 1.0 / D, RMS_EPS, ALU.mult, ALU.add) \
                    .then_inc(S["x_rms_a"], 1)
                pool.wait_ge(S["x_rms_a"], u + 1)
                pool.tensor_tensor(rms[0:rows, u:u + 1], rms_a[0:rows, u:u + 1], minus_half[0:rows, 0:1], ALU.pow) \
                    .then_inc(S["x_rms"], 1)

            def lo_quads(u, ybuf, cols, n):
                for q in range(2):
                    pool.wait_ge(S["x_hi"], 4 * u + q + 1)
                    pool.tensor_tensor(hn_lo[:, 4 * q:4 * q + 4, cols], ybuf[q][:, :, 0:n],
                                       hn_hi[:, 4 * q:4 * q + 4, cols].bitcast(F32), ALU.subtract) \
                        .then_inc(S["x_lo"], 1)

            def rms_of_x(u):
                rows = META if u == 0 else P
                rms_of(u, rows, ssq[0:rows, u:u + 1], "x_squared", u + 1)

            for u in range(3):
                rms_of_x(u)
            for u in range(TT + 1):
                if 3 <= u + 2 <= TT:
                    rms_of_x(u + 2)
                lo_quads(u, xy, x_tokens(u), META if u == 0 else P)

            const(pool.memset(ones[:], 1.0))
            const(pool.affine_select(out=upper[:], in_=ones[:], compare_op=ALU.is_ge, fill=0.0, base=0,
                                     pattern=[[1, P]], channel_multiplier=-1))
            const(pool.memset(cap[:], 0.0))
            const(pool.affine_select(out=cap[:], in_=cap[:], compare_op=ALU.is_ge, fill=NEG, base=0,
                                     pattern=[[1, P]], channel_multiplier=-1))
            for masks, first, row in ((levels, 0, 1), (keep, 1, 0)):
                const(pool.memset(masks[:], 0.0))
                for l in range(LEVELS):
                    s = 1 << l
                    n = P // (2 * s)
                    m = masks[:, l, :].rearrange("p (n w) -> p n w", w=2 * s)
                    const(pool.memset(m[:, :, s * first:s * (first + 1)], 1.0))
                    const(pool.affine_select(out=m, in_=m, compare_op=ALU.is_ge, fill=0.0, base=-s * row,
                                             pattern=[[-2 * s, n], [0, 2 * s]], channel_multiplier=1))
                    const(pool.affine_select(out=m, in_=m, compare_op=ALU.is_ge, fill=0.0, base=s * (row + 1) - 1,
                                             pattern=[[2 * s, n], [0, 2 * s]], channel_multiplier=-1))
            const(pool.tensor_copy(m_masks[:, 0:META_LEVELS, :], keep[:, 0:META_LEVELS, :]))
            const(pool.tensor_scalar(keep[:], keep[:], -1.0, 1.0, ALU.mult, ALU.add))
            const(pool.tensor_tensor(strict[:], upper[:], ident[:], ALU.subtract))
            for dst, src, w in ((meta_upper[:], upper[:], META), (meta_block[:], ones[:], META),
                                (meta_sel[:], ones[:, 0:HEADS], 1)):
                dv, sv = (a.rearrange("p (n w) -> p n w", w=w) for a in (dst, src))
                const(pool.affine_select(out=dv, in_=sv, compare_op=ALU.is_ge, fill=0.0, base=0,
                                         pattern=[[-META, HEADS], [0, w]], channel_multiplier=1))
                const(pool.affine_select(out=dv, in_=dv, compare_op=ALU.is_ge, fill=0.0, base=META - 1,
                                         pattern=[[META, HEADS], [0, w]], channel_multiplier=-1))
            const(pool.tensor_scalar(meta_neg[:], meta_upper[:], -1.0, -NEG, ALU.add, ALU.mult))

            assert built[0] == N_CONSTS

            pool.wait_ge(S["qkv_ready"], FREE["qkv_ready"] + 2 * N_KV)
            for dst, t0 in ((m_k, K_T), (m_v, VT)):
                pool.tensor_copy(dst.rearrange("p (h c) -> p h c", h=HEADS), qkv[:, t0:t0 + HEADS, 0:META]) \
                    .then_inc(S["meta_staged"], 1)
            pool.wait_ge(S["meta_vec"], 4)
            pool.tensor_tensor(m_r, m_se, minus_half[:, 0:1], ALU.pow).then_inc(S["meta_pool"], 1)
            pool.wait_ge(S["meta_vec"], 14)
            for l in range(META_LEVELS):
                pool.tensor_tensor(m_level[:, l, :], m_nt, m_masks[:, l, :], ALU.mult).then_inc(S["meta_pool"], 1)

            def stage(n, hf):
                h0 = GH * hf
                v = 2 * n + hf
                tok = bass.ds(META + P * n, P) if not isinstance(n, int) else slice(META + P * n, META + P * (n + 1))
                row = bass.ds(n + 1, 1) if not isinstance(n, int) else slice(n + 1, n + 2)
                if isinstance(n, int) and n == 0:
                    pool.wait_ge(S["qkv_ready"], FREE["qkv_ready"] + 2 * N_KV + GH)
                else:
                    pool.wait_ge(S["s_products"], 2 * v)
                    pool.wait_ge(S["rhs_ready"], GH * v)
                for b, t0 in ((7, QT), (8, K_T), (6, VT)):
                    pool.tensor_copy(B[b][:], qkv[:, t0 + h0:t0 + h0 + GH, tok]).then_inc(S["staged"], 1)
                pool.tensor_copy(gcur[hf], g_all[:, row, :].rearrange("p o h -> p (o h)")).then_inc(S["staged"], 1)
                pool.tensor_copy(bcur[hf], b_all[:, row, :].rearrange("p o h -> p (o h)")).then_inc(S["staged"], 1)

            def gdn_pool(n, hf, following):
                v = 2 * n + hf
                pool.wait_ge(S["norms_summed"], 2 * v + 2)
                pool.tensor_tensor(norm_r[:, GH:], norm_e[:, GH:], minus_half[:, 0:GH], ALU.pow) \
                    .then_inc(S["norms_ready"], 1)
                pool.wait_ge(S["g_differenced"], v + 1)
                pool.tensor_tensor(B[9][:], B[9][:], over_heads(cap[:]), ALU.add).then_inc(S["g_masked"], 1)
                pool.wait_ge(S["norms_ready"], v + 1)
                pool.wait_ge(S["decay_exp"], v + 1)
                pool.tensor_tensor(B[9][:], B[9][:], heads_of(norm_r[:, GH:]), ALU.mult).then_inc(S["decay_ready"], 1)
                pool.wait_ge(S["beta_k_ready"], v + 1)
                pool.wait_ge(S["nt_ready"], v + 1)

                def level_mask(l):
                    if l == 1:
                        pool.wait_ge(S["pt_ready"], v + 1)
                    elif l >= 2:
                        pool.wait_ge(S["x_ready"], LEVELS * v + l - 1)
                    pool.tensor_tensor(mask_buf[l % 2][:], over_heads(levels[:, l, :]), heads_of(beta_k), ALU.mult) \
                        .then_inc(S["mask_ready"], 1)

                pool.tensor_tensor(B[11][:], B[10][:], over_heads(strict[:]), ALU.mult).then_inc(S["z_masked"], 1)
                level_mask(0)
                level_mask(1)
                pool.wait_ge(S["n_turned"], v + 1)
                for l in range(LEVELS):
                    pool.wait_ge(S["z_ready"], (LEVELS + 1) * v + l + 1)
                    pool.tensor_tensor(kept[:], B[11][:], over_heads(keep[:, l, :]), ALU.mult).then_inc(S["z_kept"], 1)
                    if l + 2 < LEVELS:
                        level_mask(l + 2)
                    if l == 3 and following is not None:
                        stage(*following)
                pool.wait_ge(S["o_mean"], v + 1)
                pool.tensor_tensor(orms, omean, minus_half[:, 0:GH], ALU.pow).then_inc(S["o_rms"], 1)

            stage(0, 0)
            pool.wait_ge(S["qkv_ready"], FREE["qkv_ready"] + 2 * N_A)
            with pool.Fori(0, CH - 1) as n:
                gdn_pool(n, 0, (n, 1))
                gdn_pool(n, 1, (n + 1, 0))
            gdn_pool(CH - 1, 0, (CH - 1, 1))
            gdn_pool(CH - 1, 1, None)
            pool.wait_ge(S["state_ready"], 2 * CH + 1)

            step = [0]

            def chained(ins):
                step[0] += 1
                ins.then_inc(S["window_step"], 1)
                pool.wait_ge(S["window_step"], step[0])

            for i in range(HEADS):
                pool.wait_ge(S["p_copied"], FREE["p_copied"] + i + 1)
                g = i // 2
                src = p_in[:, i, :]
                for l in range(g + 1):
                    s = 1 << l
                    dst = win[l % 2]
                    chained(pool.tensor_tensor(dst[:, 2 * s - 1:TOK], src[:, 2 * s - 1:TOK], src[:, s - 1:TOK - s],
                                               ALU.add))
                    src = dst
                mean = win[(g + 1) % 2]
                chained(pool.tensor_scalar(mean[:, META:TOK], src[:, META:TOK], 1.0 / (2 << g), None, ALU.mult))
                chained(pool.tensor_tensor(pooled[:, i, :], mean[:, META:TOK], p_in[:, i, META:TOK], ALU.subtract))
            pool.memset(minus_half[:, 8:9], -0.5).then_inc(S["pooled_ready"], 1)

            with pool.Fori(0, N_MERGE) as u:
                for m in range(2):
                    pool.wait_ge(S["yb_gated"], FREE["yb_gated"] + 2 * u + m + 1)
                    pool.tensor_tensor(mg[:, m, :], gate_a[:, m, :], gate_b[:, m, :], ALU.add).then_inc(S["merged_sum"], 1)

            for t in range(TT):
                if t == 0:
                    rms_of(TT + 1, P, rms_a[:, TT + 1:TT + 2], "h_summed", 1)
                if t + 1 < TT:
                    rms_of(TT + 2 + t, P, rms_a[:, TT + 2 + t:TT + 3 + t], "h_summed", t + 2)
                lo_quads(TT + 1 + t, hy, slice(P * t, P * (t + 1)), P)

            for t in range(TT):
                pool.wait_ge(S["f_mean"], t + 1)
                pool.tensor_tensor(rms[:, 9 + t:10 + t], rms_a[:, 9 + t:10 + t], minus_half[:, 0:1], ALU.pow) \
                    .then_inc(S["f_rms"], 1)

        @block.scalar
        def _(act):
            def split(g, g_static):
                s = slot(g_static)
                if isinstance(g, int):
                    act.wait_ge(landed[s], 16 * (g // SLOTS + 1))
                    if g >= SLOTS:
                        act.wait_ge(S["chunk_used"], g - (SLOTS - 1))
                else:
                    act.wait_ge(landed[s], 4 * (g - g_static % SLOTS) + 16)
                    act.wait_ge(S["chunk_used"], g - (SLOTS - 1))
                act.activation(whi[s][:], raw[s][:], ACT.Copy).then_inc(S["hi_ready"], 1)

            def square_tile(u):
                rows = META if u == 0 else P
                act.wait_ge(x_landed[u], 16)
                if u > 0:
                    act.wait_ge(S["x_squared"], u)
                act.activation(x_junk[0:rows, :], xt[u][0:rows, :], ACT.Square, accum_out=ssq[0:rows, u:u + 1]) \
                    .then_inc(S["x_squared"], 1)

            def hi_quads(u, ybuf, cols, n):
                for q in range(4):
                    act.wait_ge(S["x_weighted"], 4 * u + q + 1)
                    act.activation(hn_hi[:, 4 * q:4 * q + 4, cols], ybuf[q][:, :, 0:n], ACT.Copy).then_inc(S["x_hi"], 1)

            for u in range(3):
                square_tile(u)
            act.wait_ge(S["rows_turned"], 1)
            act.activation(vec_a[:], PS[:, 0, 0:CONV * 3 * HEADS], ACT.Copy).then_inc(S["vectors_ready"], 1)
            act.activation(vec_b[:], PS[:, 1, 0:2 * KT + HEADS + 1], ACT.Copy).then_inc(S["vectors_ready"], 1)
            for u in range(TT + 1):
                if 3 <= u + 2 <= TT:
                    square_tile(u + 2)
                hi_quads(u, xy, x_tokens(u), META if u == 0 else P)
                if u >= 2:
                    split(u - 2, u - 2)
            split(SLOTS - 1, SLOTS - 1)
            act.wait_ge(S["ab_landed"], 16)
            act.activation(ab_h, ab_raw[:], ACT.Copy).then_inc(S["ab_hi"], 1)

            def a_unit(u, q, beside=lambda c: None):
                for c in range(4):
                    beside(c)
                    if c == 3:
                        for m in range(2):
                            act.wait_ge(*unit_tile(m, "a_done", u, G_A + 4 * u + 3))
                            act.wait_ge(S["conv_done"], FREE["conv_done"] + 2 * u + m - 1)
                            act.activation(conv_in[m][:, CONV - 1:CONV - 1 + TOK].rearrange("p (a b) -> p a b", a=2),
                                           PS[:, 2 * m:2 * m + 2, 0:HALF], ACT.Copy).then_inc(S["a_copied"], 1)
                    split(G_A + 4 * u + c + 4, c)
                for m in range(2):
                    act.wait_ge(S["conv_done"], FREE["conv_done"] + 2 * u + m + 1)
                    act.activation(tile_of(qkv, first_tile(u, q) + m), conv_acc[m][:], ACT.Silu).then_inc(S["qkv_ready"], 1)

            a_unit(0, False)
            act.wait_ge(S["logits_copied"], 1)
            act.activation(b_all[:], lg[:, :, 0:HEADS], ACT.Sigmoid).then_inc(S["ab_act"], 1)
            act.wait_ge(S["small_landed"], 32)
            act.activation(alog_b[:], alog_b[:], ACT.Exp).then_inc(S["ab_act"], 1)
            act.wait_ge(S["ab_vec"], 2)
            act.activation(ab_t[1][:], ab_t[1][:], ACT.Exp).then_inc(S["ab_act"], 1)
            act.wait_ge(S["ab_act"], 3)
            act.activation(ab_t[2][:], ab_t[1][:], ACT.Ln, bias=1.0).then_inc(S["ab_act"], 1)

            with act.Fori(1, N_KV) as u:
                a_unit(u, False)
            with act.Fori(N_KV, N_A - N_BESIDE) as u:
                a_unit(u, True)

            def meta_act():
                act.wait_ge(S["meta_pe"], 1)
                act.activation(m_square, PS[:, 7, 0:P], ACT.Square).then_inc(S["meta_act"], 1)
                act.wait_ge(S["meta_vec"], 8)
                act.activation(m_ed, m_nd, ACT.Exp).then_inc(S["meta_act"], 1)
                act.activation(m_decay, m_decay, ACT.Exp).then_inc(S["meta_act"], 1)
                for _ in range(5):
                    yield
                act.wait_ge(S["meta_pe"], 16)
                for i in range(2):
                    act.activation(state[:, 4 * i:4 * i + 4, :], bank(4 + i), ACT.Copy).then_inc(S["meta_act"], 1)
                yield

            meta_steps = meta_act()
            for u in range(N_A - N_BESIDE, N_A):
                a_unit(u, True, lambda c: next(meta_steps) if c > 0 else None)

            act.wait_ge(S["qkv_ready"], FREE["qkv_ready"] + 2 * N_A)
            def gdn_act(n, hf):
                v = 2 * n + hf
                h0 = GH * hf
                act.wait_ge(S["qkv_turned"], 3 * v + 1)
                act.activation(B[12][:], bank(0), ACT.Square).then_inc(S["q_squared"], 1)
                act.wait_ge(S["qkv_turned"], 3 * v + 2)
                act.activation(B[13][:], bank(1), ACT.Square).then_inc(S["k_squared"], 1)
                yield
                act.wait_ge(S["sums_copied"], v + 1)
                act.activation(egc, sums[:, h0:h0 + GH], ACT.Exp).then_inc(S["decays_small"], 1)
                act.activation(egl, sums[:, 8 + h0:8 + h0 + GH], ACT.Exp).then_inc(S["decays_small"], 1)
                act.wait_ge(S["last_differenced"], v + 1)
                act.activation(ged, gld, ACT.Exp).then_inc(S["decays_small"], 1)
                act.wait_ge(S["g_masked"], v + 1)
                act.activation(B[9][:], B[9][:], ACT.Exp).then_inc(S["decay_exp"], 1)
                yield
                yield
                act.wait_ge(S["norms_a"], 2 * v + 1)
                act.wait_ge(S["s_products"], 2 * v + 2)
                act.wait_ge(S["decays_small"], 3 * v + 3)
                for b in range(GH):
                    act.activation(B[12][:, b, :], PS[:, 5, P * b:P * (b + 1)], ACT.Copy, scale=egc[:, b:b + 1]) \
                        .then_inc(S["qs_ready"], 1)
                yield
                act.wait_ge(S["x_ready"], LEVELS * v + 1)
                act.activation(B[1][:], bank(0), ACT.Copy).then_inc(S["v_copied"], 1)
                for _ in range(14):
                    yield
                act.wait_ge(S["vn_product"], v + 1)
                act.activation(B[10][:], bank(3), ACT.Copy).then_inc(S["vn_ready"], 1)
                yield
                act.wait_ge(S["o_ready"], v + 1)
                act.activation(B[13][:], B[12][:], ACT.Square).then_inc(S["o_squared"], 1)
                yield
                yield
                yield
                yield
                act.wait_ge(S["o_turned"], v + 1)
                act.activation(qkv[:, h0:h0 + GH, bass.ds(META + P * n, P)], bank(2), ACT.Copy).then_inc(S["o_stored"], 1)
                yield

            def gate_unit(n, u):
                r = 4 * n + u
                act.wait_ge(S["gates_stored"], FREE["gates_stored"] + 16 * r)
                for m in range(2):
                    act.wait_ge(*unit_tile(m, "gate_done", r, G_GATES + 4 * r + 3))
                    act.activation(gate_out[:, m, :], PS[:, 6 + m, :], ACT.Tanh, scale=0.5).then_inc(S["gate_freed"], 1)
                act.wait_ge(S["gate_freed"], FREE["gate_freed"] + 2 * r + 2)
                act.dma_start(gates_v[:, bass.ds(2 * r, 2), :], gate_out[:, :, :]).then_inc(S["gates_stored"], 16)

            with act.Fori(0, CH) as n:
                k = 0
                for hf in range(2):
                    steps_of_half = gdn_act(n, hf)
                    for _ in range(STEPS):
                        if k % 12 == 11:
                            gate_unit(n, k // 12)
                        next(steps_of_half)
                        if k % 3 == 2:
                            c = (k + 10) // 3
                            split(G_GATES + BODY_CHUNKS * n + c, c)
                        k += 1

            with act.Fori(0, N_POOL) as u:
                for c in range(4):
                    if c == 3:
                        for m in range(2):
                            act.wait_ge(*unit_tile(m, "p_done", u, G_P + 4 * u + 3))
                            act.activation(p_in[:, bass.ds(2 * u + m, 1), :].rearrange("p o (a b) -> p (o a) b", a=2),
                                           PS[:, 4 + 2 * m:6 + 2 * m, 0:HALF], ACT.Copy).then_inc(S["p_copied"], 1)
                    split(G_P + 4 * u + c + 4, c)

            act.wait_ge(S["gates_stored"], FREE["gates_stored"] + 16 * N_GATES)
            def z_unit(u, beside):
                for c in range(4):
                    beside(c)
                    if c == 3:
                        for m in range(2):
                            act.wait_ge(*unit_tile(m, "z_done", u, G_Z + 4 * u + 3))
                            act.wait_ge(S["z_y"], FREE["z_y"] + 2 * u + m - 1)
                            act.activation(zt[:, m, :], PS[:, m, :], ACT.Silu).then_inc(S["z_silu"], 1)
                        for m in range(2):
                            act.wait_ge(S["z_y"], FREE["z_y"] + 2 * u + m + 1)
                            act.activation(tile_of(o_hi, 2 * u + m), zy[:, m, :], ACT.Copy).then_inc(S["z_hi"], 1)
                    split(G_Z + 4 * u + c + 4, c)

            def zb_tiles(c):
                for i in range(2 * c, 2 * c + 2):
                    act.wait_ge(S["zb_y"], i + 1)
                    act.activation(zb_hi[:, i, :], zb_y[i % 2], ACT.Copy).then_inc(S["zb_hi"], 1)

            with act.Fori(0, N_Z - 1) as u:
                z_unit(u, lambda c: None)
            z_unit(N_Z - 1, zb_tiles)

            with act.Fori(0, N_MERGE) as u:
                for c in range(4):
                    if c == 3:
                        for m in range(2):
                            act.wait_ge(S["merged_sum"], FREE["merged_sum"] + 2 * u + m + 1)
                            act.activation(mg_hi[:, bass.ds(2 * u + m, 1), :].rearrange("p o t -> p (o t)"),
                                           mg[:, m, :], ACT.Copy, scale=0.5).then_inc(S["merged_hi"], 1)
                    split(G_MERGE + 4 * u + c + 4, c)

            with act.Fori(0, N_OUT - 1) as u:
                for c in range(8):
                    split(G_OUT + 8 * u + c + 4, c)

            def square_h(n, t, cols):
                act.wait_ge(S["h1_ready"], FREE["h1_ready"] + TT * (cols.stop // BLOCK - 1) + t + 1)
                if n > 0:
                    act.wait_ge(S["h_squared"], n)
                i = 5 + 2 * t + (n >= TT)
                act.activation(h_junk[:, 0:cols.stop - cols.start], h[:, t, cols], ACT.Square,
                               accum_out=ssq[:, i:i + 1]).then_inc(S["h_squared"], 1)

            for c in range(8):
                if c < TT:
                    square_h(c, c, slice(0, D - BLOCK))
                if c == 7:
                    for t in range(TT):
                        square_h(TT + t, t, slice(D - BLOCK, D))
                split(G_OUT + 8 * (N_OUT - 1) + c + 4, c)

            for t in range(TT):
                hi_quads(TT + 1 + t, hy, slice(P * t, P * (t + 1)), P)

            def gate_up(g, u, slot_a, splits=16):
                for sub in range(2):
                    for c in range(8):
                        if c == 3:
                            for m in range(2):
                                r = 4 * u + 2 * sub + m
                                act.wait_ge(*unit_tile(m, "fg_done", 2 * u + sub, g + 8 * sub + 3))
                                act.wait_ge(S["act_y"], FREE["act_y"] + r - 1)
                                act.activation(sg[:, m, :], PS[:, m, :], ACT.Silu).then_inc(S["silu_ready"], 1)
                        if c == 7:
                            for m in range(2):
                                r = 4 * u + 2 * sub + m
                                act.wait_ge(S["act_y"], FREE["act_y"] + r + 1)
                                act.activation(a_hi[:, slot_a, 2 * sub + m, :], ay[:, m, :], ACT.Copy) \
                                    .then_inc(S["act_hi"], 1)
                        split(g + 8 * sub + c + 4, c)

            def down(g):
                for c in range(8):
                    split(g + c + 4, c)

            gate_up(G_FFN, 0, 0)
            with act.Fori(0, N_FFN // 2) as i:
                g = G_FFN + 16 + 48 * i
                gate_up(g, 2 * i + 1, 1)
                down(g + 16)
                gate_up(g + 24, 2 * i + 2, 0)
                down(g + 40)
            for c in range(4):
                split(G_END - 4 + c, c)
            done = TT * (N_OUT * N_FFN - 2)
            pieces = [(done - TT + t + 1, t, 0, D // 2) for t in range(TT)]
            for t in range(TT):
                pieces += [(done + 2 * t + b + 1, t, 1 + b, BLOCK) for b in range(2)]
            for n, (count, t, part, width) in enumerate(pieces):
                act.wait_ge(S["h2_ready"], FREE["h2_ready"] + count)
                if n > 0:
                    act.wait_ge(S["f_squared"], n)
                first = 0 if part == 0 else D // 2 + BLOCK * (part - 1)
                act.activation(f_junk[:, 0:width], h[:, t, first:first + width], ACT.Square,
                               accum_out=ssf[:, 3 * t + part:3 * t + part + 1]).then_inc(S["f_squared"], 1)

        @block.vector
        def _(dve):
            def split(g, g_static):
                s = slot(g_static)
                dve.wait_ge(S["hi_ready"], g + 1)
                dve.tensor_tensor(wlo[s][:], raw[s][:], whi[s][:].bitcast(F32), ALU.subtract).then_inc(S["lo_ready"], 1)

            def diagonal(u, rows=P):
                dve.wait_ge(S["x_rms"], u + 1)
                dve.tensor_scalar(diag[u % (TT + 1)][0:rows, 0:rows], ident[0:rows, 0:rows], rms[0:rows, u:u + 1], None,
                                  ALU.mult).then_inc(S["x_diag"], 1)

            def weight_quads(u, ybuf, w, cols, n):
                for q in range(4):
                    dve.wait_ge(S["x_turned"], 4 * u + q + 1)
                    if u not in (0, TT + 1):
                        dve.wait_ge(S["x_lo" if q < 2 else "x_lo_v"], 2 * (u - 1) + q % 2 + 1)
                    dve.tensor_tensor(ybuf[q][:, :, 0:n], bank(4 + q)[:, :, 0:n],
                                      w[:, 4 * q:4 * q + 4].unsqueeze(2).broadcast_to([P, 4, n]), ALU.mult) \
                        .then_inc(S["x_weighted"], 1)
                for q in range(2, 4):
                    dve.wait_ge(S["x_hi"], 4 * u + q + 1)
                    dve.tensor_tensor(hn_lo[:, 4 * q:4 * q + 4, cols], ybuf[q][:, :, 0:n],
                                      hn_hi[:, 4 * q:4 * q + 4, cols].bitcast(F32), ALU.subtract) \
                        .then_inc(S["x_lo_v"], 1)

            for m in range(2):
                dve.memset(conv_in[m][:, 0:CONV - 1], 0.0).then_inc(S["vectors_more"], 1)
            diagonal(0, META)
            diagonal(1)
            dve.wait_ge(S["vectors_ready"], 2)
            for u in range(TT + 1):
                if 2 <= u + 1 <= TT:
                    diagonal(u + 1)
                weight_quads(u, xy, nmix, x_tokens(u), META if u == 0 else P)
                if u >= 2:
                    split(u - 2, u - 2)
            split(SLOTS - 1, SLOTS - 1)
            dve.wait_ge(S["ab_hi"], 1)
            dve.tensor_tensor(ab_l, ab_raw[:], ab_h.bitcast(F32), ALU.subtract).then_inc(S["ab_lo"], 1)
            dve.wait_ge(S["ab_product"], 1)
            dve.tensor_copy(ab_cm_meta[:], PS[0:4 * HEADS, 4, 0:META].unsqueeze(1).broadcast_to([4 * HEADS, HEADS, META])) \
                .then_inc(S["ab_copied"], 1)
            dve.tensor_copy(ab_cm[:, 0:HALF - META], PS[0:4 * HEADS, 4, META:HALF]).then_inc(S["ab_copied"], 1)
            dve.tensor_copy(ab_cm[:, HALF - META:], PS[0:4 * HEADS, 5, 0:HALF]).then_inc(S["ab_copied"], 1)

            dve.wait_ge(S["vectors_more"], 2)

            def a_unit(u, q, beside=lambda c: None):
                for c in range(4):
                    beside(c)
                    if c == 3:
                        for m in range(2):
                            dve.wait_ge(S["a_copied"], FREE["a_copied"] + 2 * u + m + 1)
                            dve.wait_ge(S["qkv_ready"], FREE["qkv_ready"] + 2 * u + m - 1)
                            r = 2 * u + m
                            for j in range(CONV):
                                column = 3 * HEADS * j + first_tile(u, q) + m
                                tap = vec_a[:, column:column + 1] if isinstance(u, int) else vec_a[:, bass.ds(column, 1)]
                                src = conv_in[m][:, j:j + TOK]
                                if j == 0:
                                    ins = dve.tensor_scalar(conv_acc[m][:], src, tap, None, ALU.mult)
                                else:
                                    dve.wait_ge(S["conv_step"], 3 * r + j)
                                    ins = dve.scalar_tensor_tensor(conv_acc[m][:], src, tap, conv_acc[m][:],
                                                                   ALU.mult, ALU.add)
                                ins.then_inc(S["conv_done"] if j == CONV - 1 else S["conv_step"], 1)
                    split(G_A + 4 * u + c + 4, c)

            a_unit(0, False)
            dve.wait_ge(S["ab_done"], 1)
            dve.tensor_copy(lg[:], PS[:, 6, 0:(CH + 1) * 2 * HEADS].rearrange("p (t c) -> p t c", c=2 * HEADS)) \
                .then_inc(S["logits_copied"], 1)
            dve.wait_ge(S["logits_copied"], 1)
            dve.wait_ge(S["small_landed"], 32)
            bc5 = [P, CH + 1, HEADS]
            dve.tensor_tensor(ab_t[0][:], lg[:, :, HEADS:], dtb_b[:].unsqueeze(1).broadcast_to(bc5), ALU.add) \
                .then_inc(S["ab_vec"], 1)
            dve.wait_ge(S["ab_vec"], 1)
            dve.scalar_tensor_tensor(ab_t[1][:], ab_t[0][:], -1.0, ab_t[0][:], ALU.mult, ALU.min) \
                .then_inc(S["ab_vec"], 1)
            dve.wait_ge(S["ab_act"], 4)
            dve.scalar_tensor_tensor(ab_t[3][:], ab_t[0][:], 0.0, ab_t[2][:], ALU.max, ALU.add).then_inc(S["ab_vec"], 1)
            dve.wait_ge(S["ab_vec"], 3)
            dve.scalar_tensor_tensor(g_all[:], ab_t[3][:], -1.0, alog_b[:].unsqueeze(1).broadcast_to(bc5),
                                     ALU.mult, ALU.mult).then_inc(S["ab_vec"], 1)

            with dve.Fori(1, N_KV) as u:
                a_unit(u, False)
            with dve.Fori(N_KV, N_A - N_BESIDE) as u:
                a_unit(u, True)

            def meta_dve():
                count = [0]

                def meta(ins):
                    count[0] += 1
                    ins.then_inc(S["meta_vec"], 1)
                    dve.wait_ge(S["meta_vec"], count[0])

                dve.wait_ge(S["consts_built"], N_CONSTS)
                dve.wait_ge(S["ab_vec"], 4)
                meta(dve.tensor_tensor(m_sel8, g_all[:, 0, :], meta_sel[:], ALU.mult))
                meta(dve.tensor_reduce(m_g, m_sel8, AX.X, ALU.add))
                dve.wait_ge(S["meta_act"], 1)
                meta(dve.tensor_reduce(m_ss, m_square, AX.X, ALU.add))
                meta(dve.tensor_scalar(m_se, m_ss, L2_EPS, None, ALU.add))
                dve.wait_ge(S["meta_pe"], 3)
                meta(dve.tensor_copy(m_sums, PS[:, 5, P:P + 2]))
                meta(dve.scalar_tensor_tensor(m_decay, PS[:, 5, 0:P], m_sums[:, 0:1], meta_upper[:],
                                              ALU.subtract, ALU.mult))
                meta(dve.tensor_tensor(m_decay, m_decay, meta_neg[:], ALU.add))
                meta(dve.tensor_tensor(m_nd, m_sums[:, 1:2], m_sums[:, 0:1], ALU.subtract))
                meta(dve.tensor_tensor(m_sel8b, b_all[:, 0, :], meta_sel[:], ALU.mult))
                meta(dve.tensor_reduce(m_b, m_sel8b, AX.X, ALU.add))
                dve.wait_ge(S["meta_pool"], 1)
                meta(dve.tensor_tensor(m_bk, m_b, m_r, ALU.mult))
                dve.wait_ge(S["meta_act"], 3)
                meta(dve.tensor_tensor(m_edk, m_ed, m_r, ALU.mult))
                meta(dve.tensor_scalar(m_decay, m_decay, m_r, None, ALU.mult))
                meta(dve.tensor_tensor(m_nt, PS[:, 6, 0:P], m_decay, ALU.mult))
                meta(dve.tensor_scalar(m_kd, PS[:, 7, 0:P], m_edk, None, ALU.mult))
                meta(dve.tensor_scalar(m_beta_v, PS[:, 4, 0:P], m_b, None, ALU.mult))
                yield
                for l in range(META_LEVELS):
                    dve.wait_ge(S["meta_pe"], 3 * l + 3 + (l == 0))
                    meta(dve.tensor_scalar(m_x, PS[:, 6, 0:P], m_bk, None, ALU.mult))
                    if l == 0:
                        meta(dve.tensor_tensor(m_t, ident[:], m_x, ALU.subtract))
                    else:
                        dve.wait_ge(S["meta_pe"], 3 * l + 4)
                        meta(dve.tensor_tensor(m_t, m_t, PS[:, 4, 0:P], ALU.subtract))
                    dve.wait_ge(S["meta_pe"], 3 * l + 5)
                    meta(dve.tensor_tensor(m_tt, ident[:] if l == 0 else m_tt, PS[:, 7, 0:P], ALU.subtract))
                    yield
                dve.wait_ge(S["meta_pe"], 15)
                meta(dve.tensor_tensor(meta_u[:], PS[:, 6, 0:P].unsqueeze(1).broadcast_to([P, HEADS, P]),
                                       meta_sel[:].unsqueeze(2).broadcast_to([P, HEADS, P]), ALU.mult))
                dve.wait_ge(S["meta_act"], 5)
                dve.memset(m_sel8b, 0.0).then_inc(S["state_ready"], 1)
                yield

            meta_steps = meta_dve()
            for u in range(N_A - N_BESIDE, N_A):
                a_unit(u, True, lambda c: next(meta_steps) if c > 0 else None)

            def gdn_dve(n, hf):
                v = 2 * n + hf
                h0 = GH * hf
                bh = bcur[hf][:, h0:h0 + GH]
                dve.wait_ge(S["q_squared"], v + 1)
                dve.tensor_reduce(norm_s[:, 0:GH], B[12][:], AX.X, ALU.add).then_inc(S["norms_a"], 1)
                dve.wait_ge(S["k_squared"], v + 1)
                dve.tensor_reduce(norm_s[:, GH:], B[13][:], AX.X, ALU.add).then_inc(S["norms_a"], 1)
                dve.wait_ge(S["norms_a"], 2 * v + 2)
                dve.tensor_scalar(norm_e[:, 0:GH], norm_s[:, 0:GH], L2_EPS, float(P), ALU.add, ALU.mult) \
                    .then_inc(S["norms_summed"], 1)
                dve.tensor_scalar(norm_e[:, GH:], norm_s[:, GH:], L2_EPS, None, ALU.add).then_inc(S["norms_summed"], 1)
                dve.wait_ge(S["norms_summed"], 2 * v + 1)
                dve.tensor_scalar(q_eps, norm_e[:, 0:GH], RMS_EPS, None, ALU.mult).then_inc(S["q_eps_ready"], 1)
                yield
                dve.wait_ge(S["gates_summed"], v + 1)
                dve.tensor_copy(sums, PS[:, 4, 0:16]).then_inc(S["sums_copied"], 1)
                dve.wait_ge(S["sums_copied"], v + 1)
                dve.tensor_tensor(B[9][:], bank(3), heads_of(sums[:, h0:h0 + GH]), ALU.subtract) \
                    .then_inc(S["g_differenced"], 1)
                dve.tensor_tensor(gld, sums[:, 8 + h0:8 + h0 + GH], sums[:, h0:h0 + GH], ALU.subtract) \
                    .then_inc(S["last_differenced"], 1)
                dve.wait_ge(S["qkv_turned"], 3 * v + 3)
                dve.tensor_tensor(B[6][:], bank(2), heads_of(bh), ALU.mult).then_inc(S["vb_ready"], 1)
                dve.wait_ge(S["norms_ready"], v + 1)
                dve.tensor_tensor(beta_k, bh, norm_r[:, GH:], ALU.mult).then_inc(S["beta_k_ready"], 1)
                dve.wait_ge(S["decays_small"], 3 * v + 3)
                dve.tensor_tensor(ged_k, ged, norm_r[:, GH:], ALU.mult).then_inc(S["kd_factor"], 1)
                dve.wait_ge(S["beta_k_ready"], v + 1)
                dve.scalar_tensor_tensor(nbeg, beta_k, -1.0, egc, ALU.mult, ALU.mult).then_inc(S["nbeg_ready"], 1)
                dve.wait_ge(S["kd_factor"], v + 1)
                dve.tensor_tensor(B[5][:], bank(1), heads_of(ged_k), ALU.mult).then_inc(S["kd_ready"], 1)
                yield
                dve.wait_ge(S["kk_done"], v + 1)
                dve.wait_ge(S["decay_ready"], v + 1)
                dve.tensor_tensor(B[10][:], bank(2), B[9][:], ALU.mult).then_inc(S["nt_ready"], 1)
                dve.wait_ge(S["kq_done"], v + 1)
                dve.tensor_tensor(B[4][:], bank(3), B[9][:], ALU.mult).then_inc(S["pt_ready"], 1)
                yield
                dve.wait_ge(S["s_products"], 2 * v + 1)
                dve.wait_ge(S["nbeg_ready"], v + 1)
                for b in range(GH):
                    dve.scalar_tensor_tensor(B[0][:, b, :], PS[:, 4, P * b:P * (b + 1)], nbeg[:, b:b + 1],
                                             B[6][:, b, :], ALU.mult, ALU.add).then_inc(S["rhs_ready"], 1)
                yield
                dve.wait_ge(S["z_masked"], v + 1)
                dve.tensor_tensor(B[11][:], B[11][:], over_heads(ident[:]), ALU.add).then_inc(S["z_ready"], 1)
                dve.wait_ge(S["n_turned"], v + 1)
                dve.wait_ge(S["mask_ready"], LEVELS * v + 1)
                dve.tensor_tensor(XB[0][:], bank(0), mask_buf[0][:], ALU.mult).then_inc(S["x_ready"], 1)
                yield
                for l in range(LEVELS):
                    if l < LEVELS - 1:
                        dve.wait_ge(S["v_copied"], v + 1)
                        dve.wait_ge(S["vx_product"], (LEVELS - 1) * v + l + 1)
                        v_even = blocks_of(B[1][:], l, 0)
                        dve.tensor_tensor(v_even, v_even, blocks_of(bank(2), l, 0), ALU.subtract).then_inc(S["v_ready"], 1)
                        dve.wait_ge(S["v_ready"], (LEVELS - 1) * v + l + 1)
                        dve.wait_ge(S["mask_ready"], LEVELS * v + l + 2)
                        if l >= 1:
                            dve.wait_ge(S["z_product"], LEVELS * v + l)
                        dve.tensor_tensor(XB[(l + 1) % 2][:], B[1][:], mask_buf[(l + 1) % 2][:], ALU.mult) \
                            .then_inc(S["x_ready"], 1)
                        yield
                    dve.wait_ge(S["z_kept"], LEVELS * v + l + 1)
                    dve.wait_ge(S["z_product"], LEVELS * v + l + 1)
                    dve.tensor_tensor(B[11][:], kept[:], bank(1), ALU.subtract).then_inc(S["z_ready"], 1)
                    yield
                yield
                dve.wait_ge(S["o_product"], v + 1)
                dve.wait_ge(S["qs_ready"], GH * v + GH)
                dve.tensor_tensor(B[12][:], B[12][:], bank(0), ALU.add).then_inc(S["o_ready"], 1)
                yield
                dve.wait_ge(S["o_squared"], v + 1)
                dve.tensor_reduce(osum, B[13][:], AX.X, ALU.add).then_inc(S["o_sum"], 1)
                dve.wait_ge(S["o_sum"], v + 1)
                dve.wait_ge(S["q_eps_ready"], v + 1)
                dve.scalar_tensor_tensor(omean, osum, 1.0 / P, q_eps, ALU.mult, ALU.add).then_inc(S["o_mean"], 1)
                dve.wait_ge(S["ds_product"], v + 1)
                for b in range(GH):
                    ins = dve.scalar_tensor_tensor(state[:, h0 + b, :], state[:, h0 + b, :], egl[:, b:b + 1],
                                                   PS[:, 1, P * b:P * (b + 1)], ALU.mult, ALU.add)
                ins.then_inc(S["state_ready"], 1)
                yield
                dve.wait_ge(S["o_rms"], v + 1)
                dve.tensor_tensor(B[13][:], B[12][:], heads_of(orms), ALU.mult).then_inc(S["o_scaled"], 1)
                yield
                yield
                yield

            with dve.Fori(0, CH) as n:
                k = 0
                for hf in range(2):
                    for _ in gdn_dve(n, hf):
                        if k % 3 == 2:
                            c = (k + 10) // 3
                            split(G_GATES + BODY_CHUNKS * n + c, c)
                        k += 1

            with dve.Fori(0, N_POOL) as u:
                for c in range(4):
                    split(G_P + 4 * u + c + 4, c)

            def z_unit(u, beside):
                for c in range(4):
                    beside(c)
                    if c == 3:
                        for m in range(2):
                            dve.wait_ge(S["z_silu"], FREE["z_silu"] + 2 * u + m + 1)
                            dve.wait_ge(S["z_lo"], FREE["z_lo"] + 2 * u + m - 1)
                            o_tile = (qkv[:, 2 * u + m, META:] if isinstance(u, int) else
                                      qkv[:, bass.ds(2 * u + m, 1), META:].rearrange("p o t -> p (o t)"))
                            dve.scalar_tensor_tensor(zy[:, m, :], zt[:, m, :], onorm, o_tile, ALU.mult, ALU.mult) \
                                .then_inc(S["z_y"], 1)
                        for m in range(2):
                            dve.wait_ge(S["z_hi"], 2 * u + m + 1)
                            dve.tensor_tensor(tile_of(o_lo, 2 * u + m), zy[:, m, :],
                                              tile_of(o_hi, 2 * u + m).bitcast(F32), ALU.subtract).then_inc(S["z_lo"], 1)
                    split(G_Z + 4 * u + c + 4, c)

            def zb_tiles(c):
                for i in range(2 * c, 2 * c + 2):
                    dve.wait_ge(S["zb_done"], i + 1)
                    if i >= 2:
                        dve.wait_ge(S["zb_lo"], i - 1)
                    dve.tensor_scalar(zb_y[i % 2], zb_bank(i), pscale[:, i:i + 1], None, ALU.mult).then_inc(S["zb_y"], 1)
                    dve.wait_ge(S["zb_hi"], i + 1)
                    dve.wait_ge(S["zb_done"], i // 2 * 2 + 2)
                    dve.tensor_tensor(zb_lo[:, i, :], zb_y[i % 2], zb_hi[:, i, :].bitcast(F32), ALU.subtract) \
                        .then_inc(S["zb_lo"], 1)

            with dve.Fori(0, N_Z - 1) as u:
                z_unit(u, lambda c: None)
            z_unit(N_Z - 1, zb_tiles)

            with dve.Fori(0, N_MERGE) as u:
                for c in range(4):
                    if c == 1:
                        for m in range(2):
                            dve.wait_ge(S["gate_a_landed"], 16 * u + 16)
                            dve.wait_ge(*unit_tile(m, "ya_done", u, G_MERGE + 4 * u + 1))
                            dve.scalar_tensor_tensor(gate_a[:, m, :], gate_a[:, m, :], 1.0, PS[:, 4 + m, :],
                                                     ALU.add, ALU.mult).then_inc(S["ya_gated"], 1)
                    if c == 3:
                        for m in range(2):
                            dve.wait_ge(S["gate_b_landed"], 16 * u + 16)
                            dve.wait_ge(*unit_tile(m, "yb_done", u, G_MERGE + 4 * u + 3))
                            dve.wait_ge(S["ya_gated"], FREE["ya_gated"] + 2 * u + m + 1)
                            dve.scalar_tensor_tensor(gate_b[:, m, :], gate_b[:, m, :], 1.0, PS[:, 6 + m, :],
                                                     ALU.add, ALU.mult).then_inc(S["yb_gated"], 1)
                        for m in range(2):
                            dve.wait_ge(S["merged_hi"], 2 * u + m + 1)
                            one = bass.ds(2 * u + m, 1)
                            dve.scalar_tensor_tensor(mg_lo[:, one, :].rearrange("p o t -> p (o t)"), mg[:, m, :], 0.5,
                                                     mg_hi[:, one, :].rearrange("p o t -> p (o t)").bitcast(F32),
                                                     ALU.mult, ALU.subtract).then_inc(S["merged_lo"], 1)
                    split(G_MERGE + 4 * u + c + 4, c)

            def add_residual(u, t):
                dve.wait_ge(S["xr_landed"], 16 * u + 16)
                dve.wait_ge(*block_tile(t, "out_done", u, G_OUT + 8 * u + 7))
                cols = slice(BLOCK * u, BLOCK * (u + 1)) if isinstance(u, int) else bass.ds(BLOCK * u, BLOCK)
                dve.tensor_tensor(h[:, t, cols], xr[:, t, :], PS[:, t, :], ALU.add).then_inc(S["h1_ready"], 1)

            def sum_of_h(t):
                dve.wait_ge(S["h_squared"], TT + t + 1)
                dve.tensor_reduce(rms_a[:, TT + 1 + t:TT + 2 + t], ssq[:, 5 + 2 * t:7 + 2 * t], AX.X, ALU.add) \
                    .then_inc(S["h_summed"], 1)

            with dve.Fori(0, N_OUT - 1) as u:
                for c in range(8):
                    if c == 7:
                        for t in range(TT):
                            add_residual(u, t)
                    split(G_OUT + 8 * u + c + 4, c)
            for c in range(7):
                split(G_OUT + 8 * (N_OUT - 1) + c + 4, c)
            for t in range(TT):
                add_residual(N_OUT - 1, t)
                if t > 0:
                    sum_of_h(t - 1)

            diagonal(TT + 1)
            sum_of_h(TT - 1)
            split(G_FFN + 3, 3)
            for t in range(TT):
                if t + 1 < TT:
                    diagonal(TT + 2 + t)
                weight_quads(TT + 1 + t, hy, nffn, slice(P * t, P * (t + 1)), P)

            def gate_up(g, u, slot_a):
                for sub in range(2):
                    for c in range(8):
                        if c == 7:
                            for m in range(2):
                                r = 4 * u + 2 * sub + m
                                dve.wait_ge(*unit_tile(m, "fu_done", 2 * u + sub, g + 8 * sub + 7))
                                dve.wait_ge(S["silu_ready"], FREE["silu_ready"] + r + 1)
                                dve.wait_ge(S["act_lo"], FREE["act_lo"] + r - 1)
                                dve.tensor_tensor(ay[:, m, :], sg[:, m, :], PS[:, 2 + m, :], ALU.mult) \
                                    .then_inc(S["act_y"], 1)
                            for m in range(2):
                                r = 4 * u + 2 * sub + m
                                dve.wait_ge(S["act_hi"], r + 1)
                                dve.tensor_tensor(a_lo[:, slot_a, 2 * sub + m, :], ay[:, m, :],
                                                  a_hi[:, slot_a, 2 * sub + m, :].bitcast(F32), ALU.subtract) \
                                    .then_inc(S["act_lo"], 1)
                        split(g + 8 * sub + c + 4, c)

            def down(g, u, blocks=N_OUT):
                for blk in range(blocks):
                    for c in range(2):
                        if c == 1:
                            for t in range(TT):
                                r = TT * (N_OUT * u + blk) + t
                                dve.wait_ge(*block_tile(t, "down_done", N_OUT * u + blk, g + 2 * blk + 1))
                                dve.wait_ge(S["h2_ready"], FREE["h2_ready"] + r - TT + 1)
                                dst = h[:, t, BLOCK * blk:BLOCK * (blk + 1)]
                                dve.tensor_tensor(dst, dst, PS[:, 4 + t, :], ALU.add).then_inc(S["h2_ready"], 1)
                        split(g + 2 * blk + c + 4, 2 * blk + c)

            gate_up(G_FFN, 0, 0)
            with dve.Fori(0, N_FFN // 2) as i:
                g = G_FFN + 16 + 48 * i
                gate_up(g, 2 * i + 1, 1)
                down(g + 16, 2 * i)
                gate_up(g + 24, 2 * i + 2, 0)
                down(g + 40, 2 * i + 1)
            down(G_END - 8, N_FFN - 1, 2)
            dve.wait_ge(S["scalew_landed"], 16)
            for t in range(TT):
                for b in range(2):
                    dve.wait_ge(S["down_done"], (TT - 1) * (N_OUT * N_FFN - 2) + 2 * t + b + 1)
                    dve.wait_ge(S["h2_ready"], FREE["h2_ready"] + TT * (N_OUT * N_FFN - 2))
                    dst = h[:, t, BLOCK * (2 + b):BLOCK * (3 + b)]
                    dve.tensor_tensor(dst, dst, last_bank(t, b), ALU.add).then_inc(S["h2_ready"], 1)
                dve.wait_ge(S["f_squared"], TT + 2 * t + 2)
                dve.tensor_reduce(rms_s[:, t:t + 1], ssf[:, 3 * t:3 * t + 3], AX.X, ALU.add).then_inc(S["f_summed"], 1)
                dve.wait_ge(S["f_summed"], t + 1)
                dve.tensor_scalar(rms_a[:, 9 + t:10 + t], rms_s[:, t:t + 1], 1.0 / D, RMS_EPS, ALU.mult, ALU.add) \
                    .then_inc(S["f_mean"], 1)
                dve.wait_ge(S["f_rms"], t + 1)
                dve.wait_ge(S["h2_ready"], FREE["h2_ready"] + TT * (N_OUT * N_FFN - 2) + 2 * t + 2)
                for i in range(2):
                    cols = slice(D // 2 * i, D // 2 * (i + 1))
                    dve.scalar_tensor_tensor(ot[t][:, cols], h[:, t, cols], rms[:, 9 + t:10 + t], scalew[:, cols],
                                             ALU.mult, ALU.mult).then_inc(S["f_scaled"], 1)

        @block.tensor
        def _(pe):
            def turn_quads(u, src, rows):
                pe.wait_ge(S["x_diag"], u + 1)
                for q in range(4):
                    if u not in (0, TT + 1):
                        pe.wait_ge(S["x_weighted"], 4 * u + q - 3)
                    for i in range(4):
                        k = 4 * q + i
                        ins = pe.matmul(bank(4 + q)[:, i, 0:rows], src[0:rows, P * k:P * (k + 1)],
                                        diag[u % (TT + 1)][0:rows, 0:rows], start=True, stop=True)
                    ins.then_inc(S["x_turned"], 1)

            def tiles_split(u):
                pe.wait_ge(S["x_lo"], 2 * (u + 1))
                pe.wait_ge(S["x_lo_v"], 2 * (u + 1))

            def first_unit(g, halves, outs, done, last_tiles, beside=lambda c: None, between=lambda: None):
                for i in range(2):
                    tiles_split(last_tiles[i])
                    if i == 1:
                        between()
                    for c in range(4):
                        if i == 0:
                            pe.wait_ge(S["lo_ready"], g + c + 1)
                        for m in range(2):
                            for k in range(4):
                                kt = 4 * c + k
                                hi, lo = halves(kt)
                                w = [t[c][:].rearrange("p (k n) -> p k n", k=4)[:, k, P * m:P * (m + 1)]
                                     for t in (whi, wlo)]
                                for j, (lhs, mv) in enumerate(((w[0], hi[i]), (w[0], lo[i]), (w[1], hi[i]))):
                                    ins = pe.matmul(outs(m)[i], lhs, mv, start=kt == 0 and j == 0,
                                                    stop=kt == KT - 1 and j == 2)
                            if i == 1 and m == 0 and c == 3:
                                ins.then_inc(S[done], 1)
                        if i == 1:
                            ins.then_inc(S["chunk_used"], 1)
                        else:
                            beside(c)

            def chunk_products(g, g_static, j, n_chunks, moving, outs, done, freed, used=True):
                s = slot(g_static)
                pe.wait_ge(S["lo_ready"], g + 1)
                for m in range(2):
                    if j == 0:
                        freed(m)
                    for k in range(4):
                        kt = 4 * j + k
                        hi, lo = moving(kt)
                        w = [t[s][:].rearrange("p (k n) -> p k n", k=4)[:, k, P * m:P * (m + 1)] for t in (whi, wlo)]
                        for i, (lhs, mv) in enumerate(((w[0], hi), (w[0], lo), (w[1], hi))):
                            for o, r in zip(outs(m), mv):
                                ins = pe.matmul(o, lhs, r, start=kt == 0 and i == 0,
                                                stop=kt == 4 * n_chunks - 1 and i == 2)
                            end = k == 3 and i == 2
                            if end and m == 0 and j == n_chunks - 1:
                                ins.then_inc(S[done], 1)
                            if end and m == 1:
                                ins.then_inc(S["chunk_used"], 1)
                            yield

            def run(products):
                for _ in products:
                    pass

            def token_chunk(g, g_static, k0, n_k, lhs_of, banks, done, freed):
                s = slot(g_static)
                pe.wait_ge(S["lo_ready"], g + 1)
                for t in range(TT):
                    if k0 == 0:
                        freed(t)
                    for k in range(2):
                        hi, lo = lhs_of(k0 + k, t)
                        w = [b[s][:, BLOCK * k:BLOCK * (k + 1)] for b in (whi, wlo)]
                        first, last = k0 + k == 0, k0 + k == n_k - 1
                        pe.matmul(PS[:, banks + t, :], hi, w[0], start=first, stop=False)
                        pe.matmul(PS[:, banks + t, :], hi, w[1], start=False, stop=False)
                        ins = pe.matmul(PS[:, banks + t, :], lo, w[0], start=False, stop=last)
                    if k0 + 2 == n_k and t < TT - 1:
                        ins.then_inc(S[done], 1)
                ins.then_inc(S["chunk_used"], 1)

            pe.wait_ge(S["consts_built"], 2)
            pe.wait_ge(S["rows_landed"], 80)
            na, nb = CONV * 3 * HEADS, 2 * KT + HEADS + 1
            pe.transpose(PS[:, 0, 0:na], rows_a[:, :], ident[0:na, 0:na])
            pe.transpose(PS[:, 1, 0:nb], rows_b[:, :], ident[0:nb, 0:nb]).then_inc(S["rows_turned"], 1)
            turn_quads(0, xt[0], META)
            for t in range(TT - 1):
                turn_quads(t + 1, xt[t + 1], P)

            pe.wait_ge(S["vectors_ready"], 2)

            def hn_halves(kt):
                return tuple([b[:, kt, HALF * i:HALF * (i + 1)] for i in range(2)] for b in (hn_hi, hn_lo))

            def hn_real(kt):
                return [hn_hi[:, kt, META:]], [hn_lo[:, kt, META:]]

            def half_banks(m):
                return [PS[:, 2 * m + i, 0:HALF] for i in range(2)]

            def ab_products():
                pe.wait_ge(S["ab_lo"], 1)
                for k in range(KT):
                    hi, lo = hn_halves(k)
                    w = ab_hl[:, k, :, :].rearrange("p a c -> p (a c)")
                    for j, mv in enumerate((hi, lo)):
                        for i in range(2):
                            ins = pe.matmul(PS[0:4 * HEADS, 4 + i, 0:HALF], w, mv[i], start=k == 0 and j == 0,
                                            stop=k == KT - 1 and j == 1)
                ins.then_inc(S["ab_product"], 1)

            first_unit(G_A, hn_halves, half_banks, "a_done", (2, TT),
                       lambda c: turn_quads(TT, xt[TT], P) if c == 0 else None, ab_products)
            pe.wait_ge(S["ab_copied"], 3)
            pe.wait_ge(S["consts_built"], 4)
            for t in range(CH + 1):
                src = ab_cm_meta[:].rearrange("p h t -> p (h t)") if t == 0 else ab_cm[:, P * (t - 1):P * t]
                ins = pe.matmul(PS[:, 6, 2 * HEADS * t:2 * HEADS * (t + 1)], src, both[:], start=True, stop=True)
            ins.then_inc(S["ab_done"], 1)

            def a_chunk(u, c):
                return chunk_products(G_A + 4 * u + c, c, c, 4, hn_halves, half_banks, "a_done",
                                      lambda m: pe.wait_ge(S["a_copied"], FREE["a_copied"] + 2 * u + m - 1))

            with pe.Fori(1, N_A - N_BESIDE) as u:
                for c in range(4):
                    run(a_chunk(u, c))

            def meta_pe():
                pe.wait_ge(S["meta_staged"], 2)
                pe.transpose(PS[:, 7, 0:P], m_k, ident[:]).then_inc(S["meta_pe"], 1)
                pe.transpose(PS[:, 4, 0:P], m_v, ident[:])
                pe.matmul(PS[:, 6, 0:P], m_k, m_k, start=True, stop=True).then_inc(S["meta_pe"], 1)
                yield
                pe.wait_ge(S["meta_vec"], 2)
                pe.matmul(PS[:, 5, 0:P], m_g.broadcast_to([P, P]), meta_upper[:], start=True, stop=True)
                pe.matmul(PS[:, 5, P:P + 1], meta_upper[:], m_g, start=True, stop=True)
                pe.matmul(PS[:, 5, P + 1:P + 2], meta_block[:], m_g, start=True, stop=True).then_inc(S["meta_pe"], 1)
                yield
                pe.wait_ge(S["meta_pool"], 2)
                pe.transpose(PS[:, 6, 0:P], m_level[:, 0, :], ident[:]).then_inc(S["meta_pe"], 1)
                yield
                pe.wait_ge(S["meta_vec"], 17)
                pe.transpose(PS[:, 7, 0:P], m_x, ident[:]).then_inc(S["meta_pe"], 1)
                yield
                for l in range(1, META_LEVELS):
                    pe.wait_ge(S["meta_pool"], l + 2)
                    pe.wait_ge(S["meta_vec"], 15 + 3 * l)
                    pe.matmul(PS[:, 6, 0:P], m_level[:, l, :], m_t, start=True, stop=True).then_inc(S["meta_pe"], 1)
                    yield
                    pe.wait_ge(S["meta_vec"], 17 + 3 * l)
                    pe.matmul(PS[:, 4, 0:P], m_tt, m_x, start=True, stop=True).then_inc(S["meta_pe"], 1)
                    pe.matmul(PS[:, 7, 0:P], m_x, m_tt, start=True, stop=True).then_inc(S["meta_pe"], 1)
                    yield
                pe.wait_ge(S["meta_vec"], 16 + 3 * META_LEVELS)
                pe.matmul(PS[:, 6, 0:P], m_tt, m_beta_v, start=True, stop=True).then_inc(S["meta_pe"], 1)
                yield
                pe.wait_ge(S["meta_vec"], 17 + 3 * META_LEVELS)
                for i in range(2):
                    ins = pe.matmul(bank(4 + i), m_kd, meta_u[:, 4 * i:4 * i + 4, :], start=True, stop=True)
                ins.then_inc(S["meta_pe"], 1)
                yield

            meta_steps = meta_pe()
            for u in range(N_A - N_BESIDE, N_A):
                for c in range(4):
                    for i, _ in enumerate(a_chunk(u, c)):
                        if c > 0 and i in (7, 15):
                            next(meta_steps)
            pe.wait_ge(S["state_ready"], 1)

            def gdn_pe(n, hf):
                v = 2 * n + hf
                h0 = GH * hf
                pe.wait_ge(S["staged"], 5 * v + 5)
                pe.wait_ge(S["a_copied"], FREE["a_copied"] + 2 * N_A)
                pe.wait_ge(S["state_ready"], v + 1)
                for j, b in enumerate((7, 8, 6)):
                    if j == 2:
                        pe.wait_ge(S["o_stored"], FREE["o_stored"] + v)
                    for i in range(GH):
                        ins = pe.transpose(bank(j)[:, i, :], B[b][:, i, :], ident[:])
                    ins.then_inc(S["qkv_turned"], 1)
                yield
                for i in range(GH):
                    pe.matmul(bank(3)[:, i, :], gcur[hf][:, h0 + i:h0 + i + 1].broadcast_to([P, P]), upper[:],
                              start=True, stop=True)
                pe.matmul(PS[:, 4, 0:8], upper[:], gcur[hf], start=True, stop=True)
                pe.matmul(PS[:, 4, 8:16], ones[:], gcur[hf], start=True, stop=True).then_inc(S["gates_summed"], 1)
                yield
                pe.wait_ge(S["g_differenced"], v + 1)
                pe.wait_ge(S["vb_ready"], v + 1)
                for i in range(GH):
                    ins = pe.matmul(bank(2)[:, i, :], B[8][:, i, :], B[8][:, i, :], start=True, stop=True)
                ins.then_inc(S["kk_done"], 1)
                for i in range(GH):
                    ins = pe.matmul(bank(3)[:, i, :], B[8][:, i, :], B[7][:, i, :], start=True, stop=True)
                ins.then_inc(S["kq_done"], 1)
                yield
                pe.wait_ge(S["sums_copied"], v + 1)
                for j in (8, 7):
                    for i in range(GH):
                        ins = pe.matmul(bank(4 if j == 8 else 5)[:, i, :], B[j][:, i, :], state[:, h0 + i, :],
                                        start=True, stop=True)
                    ins.then_inc(S["s_products"], 1)
                yield
                pe.wait_ge(S["nt_ready"], v + 1)
                for i in range(GH):
                    ins = pe.transpose(bank(0)[:, i, :], B[10][:, i, :], ident[:])
                ins.then_inc(S["n_turned"], 1)
                yield
                pe.wait_ge(S["kd_ready"], v + 1)
                for l in range(LEVELS):
                    x = XB[l % 2]
                    pe.wait_ge(S["x_ready"], LEVELS * v + l + 1)
                    pe.wait_ge(S["z_ready"], (LEVELS + 1) * v + l + 1)
                    if l < LEVELS - 1:
                        for i in range(GH):
                            ins = pe.matmul(blocks_of(bank(2), l, 0)[:, i, :, :], B[11][:, i, :],
                                            blocks_of(x[:], l, 0)[:, i, :, :], start=True, stop=True)
                        ins.then_inc(S["vx_product"], 1)
                        yield
                    for i in range(GH):
                        ins = pe.matmul(bank(1)[:, i, :], x[:, i, :], B[11][:, i, :], start=True, stop=True)
                    ins.then_inc(S["z_product"], 1)
                    yield
                pe.wait_ge(S["z_ready"], (LEVELS + 1) * (v + 1))
                pe.wait_ge(S["rhs_ready"], GH * v + GH)
                pe.wait_ge(S["pt_ready"], v + 1)
                for i in range(GH):
                    ins = pe.matmul(bank(3)[:, i, :], B[11][:, i, :], B[0][:, i, :], start=True, stop=True)
                ins.then_inc(S["vn_product"], 1)
                yield
                pe.wait_ge(S["vn_ready"], v + 1)
                for i in range(GH):
                    ins = pe.matmul(bank(0)[:, i, :], B[4][:, i, :], B[10][:, i, :], start=True, stop=True)
                ins.then_inc(S["o_product"], 1)
                yield
                for i in range(GH):
                    ins = pe.matmul(bank(1)[:, i, :], B[5][:, i, :], B[10][:, i, :], start=True, stop=True)
                ins.then_inc(S["ds_product"], 1)
                yield
                yield
                yield
                pe.wait_ge(S["o_scaled"], v + 1)
                for i in range(GH):
                    ins = pe.transpose(bank(2)[:, i, :], B[13][:, i, :], ident[:])
                ins.then_inc(S["o_turned"], 1)
                yield

            def gate_products(n):
                for u in range(BODY_CHUNKS // 4):
                    for c in range(4):
                        yield from chunk_products(G_GATES + BODY_CHUNKS * n + 4 * u + c, c, c, 4, hn_real,
                                                  lambda m: [PS[:, 6 + m, :]], "gate_done",
                                                  lambda m: pe.wait_ge(S["gate_freed"], FREE["gate_freed"] + 8 * n + 2 * u + m - 1))

            with pe.Fori(0, CH) as n:
                gates = gate_products(n)
                for hf in range(2):
                    steps_of_half = gdn_pe(n, hf)
                    for _ in range(STEPS):
                        for _ in range(PIECE):
                            next(gates, None)
                        next(steps_of_half)

            def p_banks_free(u, m):
                if m == 1:
                    pe.wait_ge(S["gate_freed"], FREE["gate_freed"] + 2 * N_GATES)
                pe.wait_ge(S["p_copied"], FREE["p_copied"] + 2 * u + m - 1)

            with pe.Fori(0, N_POOL) as u:
                for c in range(4):
                    run(chunk_products(G_P + 4 * u + c, c, c, 4, hn_halves,
                                       lambda m: [PS[:, 4 + 2 * m + i, 0:HALF] for i in range(2)], "p_done",
                                       lambda m: p_banks_free(u, m)))
            def z_unit(u):
                for c in range(4):
                    run(chunk_products(G_Z + 4 * u + c, c, c, 4, hn_real, lambda m: [PS[:, m, :]],
                                       "z_done", lambda m: pe.wait_ge(S["z_silu"], FREE["z_silu"] + 2 * u + m - 1)))

            pe.wait_ge(S["o_stored"], FREE["o_stored"] + 2 * CH)
            pe.wait_ge(S["state_ready"], 2 * CH + 1)
            with pe.Fori(0, N_Z - 1) as u:
                z_unit(u)
            pe.wait_ge(S["poolw_landed"], 16)
            pe.wait_ge(S["pooled_ready"], 1)
            for i in range(HEADS):
                g, m = i // 2, i % 2
                if i >= 6:
                    pe.wait_ge(S["zb_y"], i - 5)
                for k in range(2):
                    ins = pe.matmul(zb_bank(i), poolw[:, g, k, P * m:P * (m + 1)], pooled[:, 2 * g + k, :],
                                    start=k == 0, stop=k == 1)
                ins.then_inc(S["zb_done"], 1)
            z_unit(N_Z - 1)
            pe.wait_ge(S["zb_y"], HEADS)

            with pe.Fori(0, N_MERGE) as u:
                for c in range(2):
                    pe.wait_ge(S["z_lo"], FREE["z_lo"] + 2 * (N_Z - 1 + c))
                    run(chunk_products(G_MERGE + 4 * u + c, c, c, 2, lambda kt: ([o_hi[:, kt, :]], [o_lo[:, kt, :]]),
                                       lambda m: [PS[:, 4 + m, :]], "ya_done",
                                       lambda m: pe.wait_ge(S["ya_gated"], FREE["ya_gated"] + 2 * u + m - 1)))
                pe.wait_ge(S["zb_lo"], HEADS)
                for c in range(2):
                    run(chunk_products(G_MERGE + 4 * u + 2 + c, 2 + c, c, 2,
                                       lambda kt: ([zb_hi[:, kt, :]], [zb_lo[:, kt, :]]),
                                       lambda m: [PS[:, 6 + m, :]], "yb_done",
                                       lambda m: pe.wait_ge(S["yb_gated"], FREE["yb_gated"] + 2 * u + m - 1)))

            def merged_tile(kt, t):
                return mg_hi[:, kt, P * t:P * (t + 1)], mg_lo[:, kt, P * t:P * (t + 1)]

            with pe.Fori(0, N_OUT) as u:
                for c in range(8):
                    pe.wait_ge(S["merged_lo"], 2 * (N_MERGE - 1 + c // 7))
                    token_chunk(G_OUT + 8 * u + c, c, 2 * c, KT, merged_tile, 0, "out_done",
                                lambda t: pe.wait_ge(S["h1_ready"], FREE["h1_ready"] + TT * (u - 1) + t + 1))
            for t in range(TT):
                turn_quads(TT + 1 + t, h[:, t, :], P)

            def hn_ffn(kt):
                return [hn_hi[:, kt, 0:SEQ]], [hn_lo[:, kt, 0:SEQ]]

            def ffn_halves(kt):
                return tuple([b[:, kt, SEQ // 2 * i:SEQ // 2 * (i + 1)] for i in range(2)] for b in (hn_hi, hn_lo))

            def gate_up(g, u, first=False):
                for sub in range(2):
                    r = 4 * u + 2 * sub

                    if first and sub == 0:
                        first_unit(g, ffn_halves, lambda m: [PS[:, m, SEQ // 2 * i:SEQ // 2 * (i + 1)] for i in range(2)],
                                   "fg_done", (TT + 2, 2 * TT))
                    for c in range(4) if not (first and sub == 0) else ():
                        run(chunk_products(g + 8 * sub + c, c, c, 4, hn_ffn, lambda m: [PS[:, m, :]], "fg_done",
                                           lambda m: pe.wait_ge(S["silu_ready"], FREE["silu_ready"] + r + m - 1)))
                    for c in range(4):
                        run(chunk_products(g + 8 * sub + 4 + c, c, c, 4, hn_ffn, lambda m: [PS[:, 2 + m, :]],
                                           "fu_done", lambda m: pe.wait_ge(S["act_y"], FREE["act_y"] + r + m - 1)))

            def down(g, u, slot_a, blocks=N_OUT):
                pe.wait_ge(S["act_lo"], FREE["act_lo"] + 4 * u + 4)
                for blk in range(blocks):
                    for c in range(2):
                        token_chunk(g + 2 * blk + c, 2 * blk + c, 2 * c, 4,
                                    lambda k, t: (a_hi[:, slot_a, k, P * t:P * (t + 1)],
                                                  a_lo[:, slot_a, k, P * t:P * (t + 1)]),
                                    4, "down_done",
                                    lambda t: pe.wait_ge(S["h2_ready"], FREE["h2_ready"] + TT * (N_OUT * u + blk - 1) + t + 1))

            gate_up(G_FFN, 0, first=True)
            with pe.Fori(0, N_FFN // 2) as i:
                g = G_FFN + 16 + 48 * i
                gate_up(g, 2 * i + 1)
                down(g + 16, 2 * i, 0)
                gate_up(g + 24, 2 * i + 2)
                down(g + 40, 2 * i + 1, 1)
            down(G_END - 8, N_FFN - 1, 0, 2)
            for t in range(TT):
                for b in range(2):
                    if b == 0:
                        pe.wait_ge(S["h2_ready"], FREE["h2_ready"] + TT * (N_OUT * N_FFN - 3) + t + 1)
                    for k in range(4):
                        s = slot(2 * b + k // 2)
                        if t == 0 and k % 2 == 0:
                            pe.wait_ge(S["lo_ready"], G_END - 3 + s)
                        w_hi, w_lo = (x[s][:, BLOCK * (k % 2):BLOCK * (k % 2 + 1)] for x in (whi, wlo))
                        hi, lo = (x[:, 0, k, P * t:P * (t + 1)] for x in (a_hi, a_lo))
                        pe.matmul(last_bank(t, b), hi, w_hi, start=k == 0, stop=False)
                        pe.matmul(last_bank(t, b), hi, w_lo, start=False, stop=False)
                        ins = pe.matmul(last_bank(t, b), lo, w_hi, start=False, stop=k == 3)
                    ins.then_inc(S["down_done"], 1)


_INS = ["x", "meta_tokens", "norm_mix_w", "w_in", "conv_w", "a_log", "dt_bias", "o_norm_w", "w_proj_a", "pool_w",
        "pool_scale", "w_proj_b", "w_out", "norm_ffn_w", "w_ffn_gate", "w_ffn_up", "w_ffn_down", "norm_final_w"]


def kernel(**inputs):
    import concourse.bacc as bacc
    from concourse.bass_utils import run_bass_kernel_spmd

    nc = bacc.Bacc("TRN2", target_bir_lowering=False, num_devices=1, dynamic_dma_scratch_size=1024)
    arrays, args = {}, []
    for name in _INS:
        a = np.ascontiguousarray(inputs[name])
        arrays[f"in_{name}"] = a
        args.append(nc.dram_tensor(f"in_{name}", a.shape, mybir.dt.from_np(a.dtype), kind="ExternalInput").ap())
    res = nc.dram_tensor("result", (1, SEQ, D), F32, kind="ExternalOutput").ap()
    hybrid_block(nc, *args, res)
    return run_bass_kernel_spmd(nc, [arrays], core_ids=[0]).results[0]["result"]
```
